# Optimizing a Trainium2 kernel written in Bass

```python
import math
import jax, jax.numpy as jnp
from jax import lax
import numpy as np

D_MODEL = 1024
BATCH = 1
SEQ = 512
DEPTH = 2

N_A_LAYERS = DEPTH // 2
N_B_LAYERS = DEPTH - N_A_LAYERS

DEEPNORM_ALPHA = (2 * DEPTH) ** 0.25
DEEPNORM_BETA = (8 * DEPTH) ** -0.25
LN_EPS = 1e-5
RMS_EPS = 1e-6

GDN_HEADS = 8
GDN_DK = 128
GDN_DV = 128
GDN_CONV = 4
GDN_CHUNK = 64
GDN_QK = GDN_HEADS * GDN_DK
GDN_V = GDN_HEADS * GDN_DV
GDN_IN = 2 * GDN_QK + 2 * GDN_V + 2 * GDN_HEADS

MLA_HEADS = 16
MLA_NOPE = 64
MLA_ROPE = 32
MLA_V = 64
MLA_KV_RANK = 256
MLA_Q_RANK = 384
MLA_QBLOCK = 128
ROPE_THETA = 10000.0

PEER_HEADS = 8
PEER_NKEYS = 128
PEER_N = PEER_NKEYS * PEER_NKEYS
PEER_DQ = 256
PEER_DHALF = PEER_DQ // 2
PEER_TOPK = 16
PEER_TOKEN_BLOCK = 512

kernel_name = 'yoco_gdn_mla_peer_deepnorm'

def layer_norm(x, g, b):
    xf = x.astype(jnp.float32)
    mu = xf.mean(-1, keepdims=True)
    var = jnp.square(xf - mu).mean(-1, keepdims=True)
    return ((xf - mu) * lax.rsqrt(var + LN_EPS) * g.astype(jnp.float32) + b.astype(jnp.float32)).astype(x.dtype)

def rms_norm(x, g):
    xf = x.astype(jnp.float32)
    return (xf * lax.rsqrt(jnp.mean(xf * xf, -1, keepdims=True) + RMS_EPS) * g.astype(jnp.float32)).astype(x.dtype)

def l2_normalize(x):
    xf = x.astype(jnp.float32)
    return xf * lax.rsqrt(jnp.sum(xf * xf, -1, keepdims=True) + RMS_EPS)

def rope(x, positions):
    half = MLA_ROPE // 2
    inv_freq = ROPE_THETA ** (-jnp.arange(half, dtype=jnp.float32) / half)
    ang = positions.astype(jnp.float32)[..., None] * inv_freq
    ang = ang.reshape(ang.shape[:2] + (1,) * (x.ndim - 3) + (half,))
    cos, sin = jnp.cos(ang), jnp.sin(ang)
    xf = x.astype(jnp.float32)
    x1, x2 = xf[..., :half], xf[..., half:]
    return jnp.concatenate([x1 * cos - x2 * sin, x2 * cos + x1 * sin], -1).astype(x.dtype)

def causal_depthwise_conv(x, w):
    c = x.shape[-1]
    return lax.conv_general_dilated(x, w[:, None, :].astype(x.dtype), window_strides=(1,),
                                    padding=[(GDN_CONV - 1, 0)],
                                    dimension_numbers=('NWC', 'WIO', 'NWC'),
                                    feature_group_count=c)

def chunk_gated_delta_rule(q, k, v, g, beta):
    b, s, h, dk = q.shape
    dv = v.shape[-1]
    c = GDN_CHUNK
    n = s // c

    def to_chunks(t):
        t = t.reshape((b, n, c, h) + t.shape[3:])
        return jnp.moveaxis(t, (1, 3), (0, 2))

    q = to_chunks(q * dk ** -0.5)
    k = to_chunks(k)
    v = to_chunks(v)
    beta = to_chunks(beta)
    g = jnp.cumsum(to_chunks(g), axis=-1)
    tril = jnp.tril(jnp.ones((c, c), bool))
    strict = jnp.tril(jnp.ones((c, c), bool), -1)
    gdiff = jnp.where(tril, g[..., :, None] - g[..., None, :], 0.0)
    decay = jnp.where(tril, jnp.exp(gdiff), 0.0)
    k_beta = k * beta[..., None]
    lower = jnp.where(strict, jnp.einsum('nbhcd,nbhed->nbhce', k_beta, k) * decay, 0.0)
    rhs = jnp.concatenate([v * beta[..., None], k_beta * jnp.exp(g)[..., None]], -1)
    sol = lax.linalg.triangular_solve(lower, rhs, left_side=True, lower=True, unit_diagonal=True)
    u, w = sol[..., :dv], sol[..., dv:]

    def step(state, inp):
        q_i, k_i, u_i, w_i, g_i, decay_i = inp
        v_new = u_i - jnp.einsum('bhcd,bhde->bhce', w_i, state)
        attn = jnp.einsum('bhcd,bhed->bhce', q_i, k_i) * decay_i
        o = (jnp.einsum('bhcd,bhde->bhce', q_i * jnp.exp(g_i)[..., None], state)
             + jnp.einsum('bhce,bhef->bhcf', attn, v_new))
        g_last = g_i[..., -1:]
        state = (state * jnp.exp(g_last)[..., None]
                 + jnp.einsum('bhcd,bhce->bhde', k_i * jnp.exp(g_last - g_i)[..., None], v_new))
        return state, o

    state0 = jnp.zeros((b, h, dk, dv), jnp.float32)
    _, o = lax.scan(step, state0, (q, k, u, w, g, decay))
    return jnp.moveaxis(o, (0, 2), (1, 3)).reshape(b, s, h, dv)

def gated_deltanet(h, w_in, conv_w, a_log, dt_bias, norm_g, w_out):
    b, s, _ = h.shape
    proj = h @ w_in
    qkv, z, b_logit, a_logit = jnp.split(
        proj, [2 * GDN_QK + GDN_V, 2 * GDN_QK + 2 * GDN_V, 2 * GDN_QK + 2 * GDN_V + GDN_HEADS], -1)
    qkv = jax.nn.silu(causal_depthwise_conv(qkv, conv_w))
    q, k, v = jnp.split(qkv, [GDN_QK, 2 * GDN_QK], -1)
    q = l2_normalize(q.reshape(b, s, GDN_HEADS, GDN_DK))
    k = l2_normalize(k.reshape(b, s, GDN_HEADS, GDN_DK))
    v = v.reshape(b, s, GDN_HEADS, GDN_DV).astype(jnp.float32)
    beta = jax.nn.sigmoid(b_logit.astype(jnp.float32))
    g = -jnp.exp(a_log.astype(jnp.float32)) * jax.nn.softplus(a_logit.astype(jnp.float32) + dt_bias.astype(jnp.float32))
    o = chunk_gated_delta_rule(q, k, v, g, beta)
    o = rms_norm(o, norm_g) * jax.nn.silu(z.reshape(b, s, GDN_HEADS, GDN_DV).astype(jnp.float32))
    return o.reshape(b, s, GDN_V).astype(h.dtype) @ w_out

def mla_shared_kv(h, positions, w_kv_a, kv_norm_g, w_uk, w_uv):
    b, s, _ = h.shape
    kv = h @ w_kv_a
    c_kv = rms_norm(kv[..., :MLA_KV_RANK], kv_norm_g)
    k_rope = rope(kv[..., MLA_KV_RANK:], positions)
    k_nope = (c_kv @ w_uk).reshape(b, s, MLA_HEADS, MLA_NOPE)
    v = (c_kv @ w_uv).reshape(b, s, MLA_HEADS, MLA_V)
    return k_nope, k_rope, v

def mla_attention(h, positions, k_nope, k_rope, v, w_qa, q_norm_g, w_qb, w_out):
    b, s, _ = h.shape
    q = (rms_norm(h @ w_qa, q_norm_g) @ w_qb).reshape(b, s, MLA_HEADS, MLA_NOPE + MLA_ROPE)
    q_nope = q[..., :MLA_NOPE]
    q_rope = rope(q[..., MLA_NOPE:], positions)
    nb = s // MLA_QBLOCK
    scale = (MLA_NOPE + MLA_ROPE) ** -0.5
    key_pos = jnp.arange(s)

    def blocks(t):
        return jnp.moveaxis(t.reshape((b, nb, MLA_QBLOCK) + t.shape[2:]), 1, 0)

    def attend(inp):
        qn, qr, blk = inp
        sc = (jnp.einsum('bqhd,bkhd->bhqk', qn, k_nope, preferred_element_type=jnp.float32)
              + jnp.einsum('bqhr,bkr->bhqk', qr, k_rope, preferred_element_type=jnp.float32))
        qpos = blk * MLA_QBLOCK + jnp.arange(MLA_QBLOCK)
        sc = jnp.where(key_pos[None, :] <= qpos[:, None], sc * scale, -jnp.inf)
        p = jax.nn.softmax(sc, -1).astype(v.dtype)
        return jnp.einsum('bhqk,bkhd->bqhd', p, v)

    o = lax.map(attend, (blocks(q_nope), blocks(q_rope), jnp.arange(nb)))
    o = jnp.moveaxis(o, 0, 1).reshape(b, s, MLA_HEADS * MLA_V)
    return o @ w_out

def peer(h, w_q, sub_keys, u_tab, v_tab):
    b, s, d = h.shape
    t = b * s
    tb = math.gcd(t, PEER_TOKEN_BLOCK)
    xs = h.reshape(t // tb, tb, d)

    def block(xb):
        q = (xb @ w_q).reshape(tb, PEER_HEADS, 2, PEER_DHALF)
        sc = jnp.einsum('thpd,hpnd->thpn', q, sub_keys, preferred_element_type=jnp.float32)
        top_s, top_i = lax.top_k(sc, PEER_TOPK)
        cand_s = top_s[:, :, 0, :, None] + top_s[:, :, 1, None, :]
        cand_id = top_i[:, :, 0, :, None] * PEER_NKEYS + top_i[:, :, 1, None, :]
        best_s, best_j = lax.top_k(cand_s.reshape(tb, PEER_HEADS, PEER_TOPK * PEER_TOPK), PEER_TOPK)
        ids = jnp.take_along_axis(cand_id.reshape(tb, PEER_HEADS, PEER_TOPK * PEER_TOPK), best_j, -1)
        gate = jax.nn.softmax(best_s, -1).reshape(tb, PEER_HEADS * PEER_TOPK)
        ids = ids.reshape(tb, PEER_HEADS * PEER_TOPK)
        hid = jnp.einsum('td,ted->te', xb, u_tab[ids], preferred_element_type=jnp.float32)
        act = (gate * jax.nn.gelu(hid, approximate=False)).astype(xb.dtype)
        return jnp.einsum('te,ted->td', act, v_tab[ids])

    return lax.map(block, xs).reshape(b, s, d)

def setup_inputs(seed: int = 0) -> dict:
    key = jax.random.key(seed)
    ks = jax.random.split(key, 32)
    f32 = jnp.float32

    def dense(k, shape, fan_in, scale=1.0):
        return jax.random.normal(k, shape, f32) * (scale * fan_in ** -0.5)

    def gain(k, shape):
        return 1.0 + 0.02 * jax.random.normal(k, shape, f32)

    x = jax.random.normal(ks[0], (BATCH, SEQ, D_MODEL), f32)
    offset = jax.random.randint(ks[1], (BATCH, 1), 0, 4096, dtype=jnp.int32)
    positions = offset + jnp.arange(SEQ, dtype=jnp.int32)[None, :]

    a_w_in = jnp.concatenate([
        dense(ks[2], (N_A_LAYERS, D_MODEL, 2 * GDN_QK), D_MODEL),
        dense(ks[3], (N_A_LAYERS, D_MODEL, GDN_V), D_MODEL, DEEPNORM_BETA),
        dense(ks[4], (N_A_LAYERS, D_MODEL, GDN_V + 2 * GDN_HEADS), D_MODEL),
    ], -1)
    a_conv_w = dense(ks[5], (N_A_LAYERS, GDN_CONV, 2 * GDN_QK + GDN_V), GDN_CONV)
    a_a_log = jnp.log(jax.random.uniform(ks[6], (N_A_LAYERS, GDN_HEADS), f32, 1.0, 16.0))
    dt = jnp.exp(jax.random.uniform(ks[7], (N_A_LAYERS, GDN_HEADS), f32, math.log(1e-3), math.log(1e-1)))
    a_dt_bias = jnp.log(jnp.expm1(dt))
    a_norm_g = gain(ks[8], (N_A_LAYERS, GDN_DV))
    a_w_out = dense(ks[9], (N_A_LAYERS, GDN_V, D_MODEL), GDN_V, DEEPNORM_BETA)

    kv_w_a = dense(ks[10], (D_MODEL, MLA_KV_RANK + MLA_ROPE), D_MODEL)
    kv_norm_g = gain(ks[11], (MLA_KV_RANK,))
    kv_w_uk = dense(ks[12], (MLA_KV_RANK, MLA_HEADS * MLA_NOPE), MLA_KV_RANK)
    kv_w_uv = dense(ks[13], (MLA_KV_RANK, MLA_HEADS * MLA_V), MLA_KV_RANK, DEEPNORM_BETA)

    b_w_qa = dense(ks[14], (N_B_LAYERS, D_MODEL, MLA_Q_RANK), D_MODEL)
    b_q_norm_g = gain(ks[15], (N_B_LAYERS, MLA_Q_RANK))
    b_w_qb = dense(ks[16], (N_B_LAYERS, MLA_Q_RANK, MLA_HEADS * (MLA_NOPE + MLA_ROPE)), MLA_Q_RANK)
    b_w_out = dense(ks[17], (N_B_LAYERS, MLA_HEADS * MLA_V, D_MODEL), MLA_HEADS * MLA_V, DEEPNORM_BETA)

    peer_w_q = dense(ks[18], (DEPTH, D_MODEL, PEER_HEADS * PEER_DQ), D_MODEL)
    peer_sub_keys = dense(ks[19], (DEPTH, PEER_HEADS, 2, PEER_NKEYS, PEER_DHALF), PEER_DHALF)
    peer_u = dense(ks[20], (DEPTH, PEER_N, D_MODEL), D_MODEL)
    peer_v = jax.random.normal(ks[21], (DEPTH, PEER_N, D_MODEL), f32) * DEEPNORM_BETA

    ln_g = gain(ks[22], (DEPTH, 2, D_MODEL))
    ln_b = 0.02 * jax.random.normal(ks[23], (DEPTH, 2, D_MODEL), f32)

    return {'x': x, 'positions': positions,
            'a_w_in': a_w_in, 'a_conv_w': a_conv_w, 'a_a_log': a_a_log, 'a_dt_bias': a_dt_bias,
            'a_norm_g': a_norm_g, 'a_w_out': a_w_out,
            'kv_w_a': kv_w_a, 'kv_norm_g': kv_norm_g, 'kv_w_uk': kv_w_uk, 'kv_w_uv': kv_w_uv,
            'b_w_qa': b_w_qa, 'b_q_norm_g': b_q_norm_g, 'b_w_qb': b_w_qb, 'b_w_out': b_w_out,
            'peer_w_q': peer_w_q, 'peer_sub_keys': peer_sub_keys, 'peer_u': peer_u, 'peer_v': peer_v,
            'ln_g': ln_g, 'ln_b': ln_b}

def reference(x, positions, a_w_in, a_conv_w, a_a_log, a_dt_bias, a_norm_g, a_w_out,
              kv_w_a, kv_norm_g, kv_w_uk, kv_w_uv, b_w_qa, b_q_norm_g, b_w_qb, b_w_out,
              peer_w_q, peer_sub_keys, peer_u, peer_v, ln_g, ln_b):
    h = x
    k_nope = k_rope = v_shared = None
    for layer in range(DEPTH):
        if layer < N_A_LAYERS:
            i = layer
            mix = gated_deltanet(h, a_w_in[i], a_conv_w[i], a_a_log[i], a_dt_bias[i], a_norm_g[i], a_w_out[i])
        else:
            if layer == N_A_LAYERS:
                k_nope, k_rope, v_shared = mla_shared_kv(h, positions, kv_w_a, kv_norm_g, kv_w_uk, kv_w_uv)
            j = layer - N_A_LAYERS
            mix = mla_attention(h, positions, k_nope, k_rope, v_shared, b_w_qa[j], b_q_norm_g[j], b_w_qb[j], b_w_out[j])
        h = layer_norm(DEEPNORM_ALPHA * h + mix, ln_g[layer, 0], ln_b[layer, 0])
        h = layer_norm(DEEPNORM_ALPHA * h + peer(h, peer_w_q[layer], peer_sub_keys[layer], peer_u[layer], peer_v[layer]),
                       ln_g[layer, 1], ln_b[layer, 1])
    return h


_drawn_inputs = setup_inputs


def setup_inputs(seed=0):
    import zlib

    import numpy as np

    out = dict(_drawn_inputs(seed))
    spreads = {}
    factors = {'kv_norm_g': 8.0, 'b_q_norm_g': 8.0}
    for name, (base, spread) in spreads.items():
        noise = np.random.default_rng([zlib.crc32(name.encode()), seed]).standard_normal(out[name].shape)
        drawn = base * np.exp(spread * noise) if base else spread * noise
        out[name] = __import__('jax').numpy.asarray(drawn.astype(out[name].dtype))
    for name, factor in factors.items():
        out[name] = (out[name] * factor).astype(out[name].dtype)
    return out
```

```python
import math
from contextlib import ExitStack

import concourse.bass as bass
import concourse.mybir as mybir

F32 = mybir.dt.float32
U32 = mybir.dt.uint32
I32 = mybir.dt.int32
ALU = mybir.AluOpType
ACT = mybir.ActivationFunctionType
AX = mybir.AxisListType

P = 128
SEQ = 512
TT = SEQ // P
D = 1024
KC = D // P
BANK = 512
HALVES = D // BANK
DEPTH = 2
ALPHA = (2 * DEPTH) ** 0.25
LN_EPS = 1e-5
RMS_EPS = 1e-6

HEADS = 8
NKEYS = 128
TOPK = 16
SETS = 2 * HEADS
NEG = -3.0e38


class Chain:

    def __init__(self, eng, sem, before=0, alone=None):
        self.eng, self.sem, self.before, self.count, self.alone = eng, sem, before, 0, alone

    def link(self, ins):
        self.count += 1
        ins.then_inc(self.sem, 1)
        self.eng.wait_ge(self.sem, self.before + self.count)
        if self.alone is not None:
            self.eng.sem_inc(self.alone, 1)

    def end(self, count):
        assert self.count == count, self.count


def starts_at_one(eng, *sems):
    for sem in sems:
        eng.sem_inc(sem, 1)


class Stage:

    def __init__(self, nc, name):
        self.nc, self.name, self.ctx, self.sems = nc, name, ExitStack(), []

    def __enter__(self):
        self.ctx.__enter__()
        return self

    def __exit__(self, *e):
        if self.sems:
            self.nc.clear_and_free_semaphores(self.sems)
            self.nc.all_engine_barrier()
        return self.ctx.__exit__(*e)

    def sb(self, name, shape, dt=F32):
        return self.ctx.enter_context(self.nc.sbuf_tensor(f"{self.name}_{name}", shape, dt))

    def ps(self, name, shape, dt=F32):
        return self.ctx.enter_context(self.nc.psum_tensor(f"{self.name}_{name}", shape, dt))

    def sem(self, name):
        self.sems.append(self.nc.alloc_semaphore(name=f"{self.name}_{name}"))
        return self.sems[-1]

    def block(self):
        return self.nc.Block()


def make_constants(nc, c):
    with Stage(nc, "const") as s:
        zeroed, made, itoa, copied = s.sem("zeroed"), s.sem("made"), s.sem("iota"), s.sem("copied")
        iota_i = s.sb("iota_i", [P, P], I32)
        with s.block() as block:
            @block.gpsimd
            def _(pool):
                nc.gpsimd.memset(c["ident"][:], 0.0).then_inc(zeroed, 1)
                nc.gpsimd.memset(c["ones"][:], 1.0).then_inc(zeroed, 1)
                nc.gpsimd.iota(iota_i[:], pattern=[[1, P]], base=0, channel_multiplier=0).then_inc(itoa, 1)
                pool.wait_ge(zeroed, 2)
                nc.gpsimd.affine_select(out=c["ident"][:], in_=c["ident"][:], compare_op=ALU.not_equal, fill=1.0,
                                        base=0, pattern=[[-1, P]], channel_multiplier=1).then_inc(made, 1)
                nc.gpsimd.affine_select(out=c["upper"][:], in_=c["ones"][:], compare_op=ALU.is_ge, fill=0.0,
                                        base=0, pattern=[[1, P]], channel_multiplier=-1).then_inc(made, 1)
                nc.gpsimd.affine_select(out=c["lower"][:], in_=c["ones"][:], compare_op=ALU.is_ge, fill=0.0,
                                        base=0, pattern=[[-1, P]], channel_multiplier=1).then_inc(made, 1)
                nc.gpsimd.affine_select(out=c["strict"][:], in_=c["ones"][:], compare_op=ALU.is_gt, fill=0.0,
                                        base=0, pattern=[[-1, P]], channel_multiplier=1).then_inc(made, 1)
                nc.gpsimd.affine_select(out=c["block16"][:].rearrange("p (b j) -> p b j", j=16),
                                        in_=c["ones"][:].rearrange("p (b j) -> p b j", j=16),
                                        compare_op=ALU.is_ge, fill=0.0,
                                        base=0, pattern=[[-16, P // 16], [0, 16]], channel_multiplier=1).then_inc(made, 1)
                pool.wait_ge(made, 5)
                nc.gpsimd.affine_select(out=c["block16"][:].rearrange("p (b j) -> p b j", j=16),
                                        in_=c["block16"][:].rearrange("p (b j) -> p b j", j=16),
                                        compare_op=ALU.is_ge, fill=0.0,
                                        base=15, pattern=[[16, P // 16], [0, 16]], channel_multiplier=-1).then_inc(made, 1)

            @block.vector
            def _(dve):
                dve.wait_ge(itoa, 1)
                nc.vector.tensor_copy(c["iota"][:], iota_i[:]).then_inc(copied, 1)
                dve.wait_ge(made, 6)
                dve.wait_ge(copied, 1)


def transpose_tokens(nc, c, h, hT):
    with Stage(nc, f"t{nc.next_id()}") as s:
        flipped, taken = s.sem("flipped"), s.sem("taken")
        bank = [s.ps(f"bank{i}", [P, BANK]) for i in range(2)]
        with s.block() as block:
            @block.tensor
            def _(pe):
                for k in range(KC):
                    if k >= 2:
                        pe.wait_ge(taken, k - 1)
                    for t in range(TT):
                        last = nc.tensor.transpose(bank[k % 2][:, t * P:(t + 1) * P], h[:, t, k * P:(k + 1) * P],
                                                   c["ident"][:])
                    last.then_inc(flipped, 1)

            @block.vector
            def _(dve):
                for k in range(KC):
                    dve.wait_ge(flipped, k + 1)
                    nc.vector.tensor_copy(hT[:, k, :], bank[k % 2][:]).then_inc(taken, 1)
                dve.wait_ge(taken, KC)


def peer_select(nc, c, name, hT, w_q, sub_keys, giT):
    SLABS = SETS * P // BANK
    PER = BANK // P
    with Stage(nc, name) as s:
        wslab = [s.sb(f"wslab{i}", [P, KC, BANK]) for i in range(2)]
        keys = s.sb("keys", [P, SETS, P])
        keysT = s.sb("keysT", [P, SETS, P])
        qT = [s.sb(f"qT{i}", [P, SEQ]) for i in range(2)]
        masked = s.sb("masked", [P, TT, NKEYS])
        best = s.sb("best", [P, TT, TOPK])
        besti = s.sb("besti", [P, TT, TOPK], U32)
        val = s.sb("val", [P, SETS, TT, TOPK])
        num = s.sb("num", [P, SETS, TT, TOPK])
        cand = s.sb("cand", [P, HEADS, TOPK * TOPK])
        candm = s.sb("candm", [P, HEADS, TOPK * TOPK])
        top = s.sb("top", [P, HEADS, TOPK])
        topi = s.sb("topi", [P, HEADS, TOPK], U32)
        digit = s.sb("digit", [P, HEADS * TOPK], U32)
        digitf = s.sb("digitf", [P, HEADS * TOPK])
        valt = s.sb("valt", [P, SETS, TOPK])
        numt = s.sb("numt", [P, SETS, TOPK])
        hot = s.sb("hot", [P, HEADS, TOPK * TOPK])
        mass = s.sb("mass", [P, HEADS])
        picks = s.sb("picks", [P, 3, HEADS * TOPK])
        load_w = [s.sem("load_w0"), s.sem("load_w1")]
        load_k, kflip, ktaken = s.sem("load_k"), s.sem("kflip"), s.sem("ktaken")
        projected, qready, scored, ranked = s.sem("projected"), s.sem("qready"), s.sem("scored"), s.sem("ranked")
        chain, passed = s.sem("chain"), s.sem("passed")
        logits, expd, picked, turned, done = s.sem("logits"), s.sem("expd"), s.sem("picked"), s.sem("turned"), s.sem("done")
        qps = [s.ps(f"qps{i}", [P, SEQ]) for i in range(2)]
        sps = [s.ps(f"sps{i}", [P, TT, NKEYS]) for i in range(2)]
        tps = s.ps("tps", [P, 4, P])
        gps = s.ps("gps", [P, 3, P])
        wq_v = w_q.rearrange("(k p) (s n) -> s p k n", p=P, n=BANK)
        ROUND1 = 2 * PER
        with s.block() as block:
            @block.sync
            def _(sp):
                sp.dma_start(keys[:], sub_keys.rearrange("h p n d -> n (h p) d")).then_inc(load_k, 16)
                with sp.Fori(0, SLABS // 2) as i:
                    for b in range(2):
                        sp.wait_ge(projected, i * ROUND1 + 1)
                        sp.dma_start(wslab[b][:], wq_v[bass.ds(2 * i + b, 1)]).then_inc(load_w[b], 16)

            @block.tensor
            def _(pe):
                starts_at_one(pe, projected)
                pe.wait_ge(load_k, 16)
                for q in range(SETS // 4):
                    if q:
                        pe.wait_ge(ktaken, q)
                    for j in range(4):
                        last = nc.tensor.transpose(tps[:, j, :], keys[:, 4 * q + j, :], c["ident"][:])
                    last.then_inc(kflip, 1)
                pe.wait_ge(ktaken, SETS // 4)
                with pe.Fori(0, SLABS // 2) as i:
                    def score(n):
                        pe.wait_ge(qready, i * ROUND1 + n + 1)
                        pe.wait_ge(ranked, i * ROUND1 + n + 1)
                        for t in range(TT):
                            last = nc.tensor.matmul(sps[n % 2][:, t, :], qT[n % 2][:, t * P:(t + 1) * P],
                                                    keysT[:, bass.ds(i * ROUND1 + n, 1), :], start=True, stop=True)
                        last.then_inc(scored, 1)

                    for b in range(2):
                        pe.wait_ge(load_w[b], 16 * (i + 1))
                        for j in range(PER):
                            n = b * PER + j
                            for k in range(KC):
                                last = nc.tensor.matmul(qps[n % 2][:], wslab[b][:, k, j * P:(j + 1) * P], hT[:, k, :],
                                                        start=(k == 0), stop=(k == KC - 1))
                            last.then_inc(projected, 1)
                            if n >= 1:
                                score(n - 1)
                    score(ROUND1 - 1)
                with pe.Fori(0, TT) as i:
                    pe.wait_ge(picked, i + 1)
                    for j in range(3):
                        last = nc.tensor.transpose(gps[:, j, :], picks[:, j, :], c["ident"][:])
                    last.then_inc(turned, 1)

            @block.scalar
            def _(act):
                for q in range(SETS // 4):
                    act.wait_ge(kflip, q + 1)
                    nc.scalar.copy(keysT[:, 4 * q:4 * q + 4, :], tps[:]).then_inc(ktaken, 1)
                with act.Fori(0, SLABS // 2) as i:
                    for n in range(ROUND1):
                        act.wait_ge(projected, i * ROUND1 + n + 2)
                        if n >= 2:
                            act.wait_ge(scored, i * ROUND1 + n - 1)
                        nc.scalar.copy(qT[n % 2][:], qps[n % 2][:]).then_inc(qready, 1)
                with act.Fori(0, TT) as i:
                    act.wait_ge(logits, i + 1)
                    nc.scalar.activation(picks[:, 0, :], picks[:, 0, :], ACT.Exp).then_inc(expd, 1)

            @block.vector
            def _(dve):
                nc.vector.memset(mass[:], 0.0).then_inc(ranked, 2)
                PER_SET = 5
                with dve.Fori(0, SLABS // 2) as i:
                    ch = Chain(dve, chain, i * (ROUND1 * PER_SET), passed)
                    for n in range(ROUND1):
                        sc, e = sps[n % 2], i * ROUND1 + n
                        dve.wait_ge(scored, e + 1)
                        dve.sem_inc(passed, 1)
                        for t in range(TT):
                            last = nc.vector.max(best[:, t, 0:8], sc[:, t, :])
                        ch.link(last)
                        for t in range(TT):
                            nc.vector.max_index(besti[:, t, 0:8], best[:, t, 0:8], sc[:, t, :])
                            last = nc.vector.match_replace(masked[:, t, :], best[:, t, 0:8], sc[:, t, :], NEG)
                        ch.link(last)
                        for t in range(TT):
                            last = nc.vector.max(best[:, t, 8:16], masked[:, t, :])
                        ch.link(last)
                        for t in range(TT):
                            last = nc.vector.max_index(besti[:, t, 8:16], best[:, t, 8:16], masked[:, t, :])
                        ch.link(last)
                        ch.link(nc.vector.tensor_copy(val[:, bass.ds(e, 1), :, :], best[:].unsqueeze(1)))
                        nc.vector.tensor_copy(num[:, bass.ds(e, 1), :, :], besti[:].unsqueeze(1)).then_inc(ranked, 1)
                        dve.wait_ge(ranked, e + 3)
                    ch.end(ROUND1 * PER_SET)
                PER_TILE = 18
                with dve.Fori(0, TT) as i:
                    ch = Chain(dve, chain, SETS * PER_SET + i * PER_TILE, passed)
                    nc.vector.tensor_copy(valt[:].unsqueeze(2), val[:, :, bass.ds(i, 1), :])
                    ch.link(nc.vector.tensor_copy(numt[:].unsqueeze(2), num[:, :, bass.ds(i, 1), :]))
                    v4 = valt[:].rearrange("p (h s) k -> p h s k", s=2)
                    n4 = numt[:].rearrange("p (h s) k -> p h s k", s=2)
                    cand4 = cand[:].rearrange("p h (a b) -> p h a b", a=TOPK)
                    hot4 = hot[:].rearrange("p h (a b) -> p h a b", a=TOPK)
                    for hh in range(HEADS):
                        last = nc.vector.tensor_tensor(cand4[:, hh],
                                                       v4[:, hh, 0].unsqueeze(2).broadcast_to([P, TOPK, TOPK]),
                                                       v4[:, hh, 1].unsqueeze(1).broadcast_to([P, TOPK, TOPK]), ALU.add)
                    ch.link(last)
                    for hh in range(HEADS):
                        last = nc.vector.max(top[:, hh, 0:8], cand[:, hh, :])
                    ch.link(last)
                    for hh in range(HEADS):
                        nc.vector.max_index(topi[:, hh, 0:8], top[:, hh, 0:8], cand[:, hh, :])
                        last = nc.vector.match_replace(candm[:, hh, :], top[:, hh, 0:8], cand[:, hh, :], NEG)
                    ch.link(last)
                    for hh in range(HEADS):
                        last = nc.vector.max(top[:, hh, 8:16], candm[:, hh, :])
                    ch.link(last)
                    for hh in range(HEADS):
                        last = nc.vector.max_index(topi[:, hh, 8:16], top[:, hh, 8:16], candm[:, hh, :])
                    ch.link(last)
                    g3 = picks[:, 0, :].rearrange("p (h k) -> p h k", k=TOPK)
                    last = nc.vector.tensor_tensor(g3, top[:], top[:, :, 0:1].broadcast_to([P, HEADS, TOPK]), ALU.subtract)
                    last.then_inc(logits, 1)
                    for side, (op, k) in enumerate(((ALU.logical_shift_right, 4), (ALU.bitwise_and, 15))):
                        ch.link(nc.vector.tensor_scalar(digit[:], topi[:].rearrange("p h k -> p (h k)"), k, None, op))
                        ch.link(nc.vector.tensor_copy(digitf[:], digit[:]))
                        ch.link(nc.vector.tensor_tensor(hot[:].rearrange("p h (k a) -> p (h k) a", a=TOPK),
                                                        digitf[:].unsqueeze(2).broadcast_to([P, HEADS * TOPK, TOPK]),
                                                        c["iota"][:, 0:TOPK].unsqueeze(1).broadcast_to([P, HEADS * TOPK, TOPK]),
                                                        ALU.is_equal))
                        for hh in range(HEADS):
                            last = nc.vector.tensor_tensor(hot4[:, hh], hot4[:, hh],
                                                           n4[:, hh, side].unsqueeze(1).broadcast_to([P, TOPK, TOPK]), ALU.mult)
                        ch.link(last)
                        ch.link(nc.vector.tensor_reduce(picks[:, 1 + side, :], hot[:].rearrange("p h (k a) -> p (h k) a", a=TOPK),
                                                        axis=AX.X, op=ALU.add))
                    dve.wait_ge(expd, i + 1)
                    ch.link(nc.vector.tensor_reduce(mass[:], g3, axis=AX.X, op=ALU.add))
                    ch.link(nc.vector.reciprocal(mass[:], mass[:]))
                    last = nc.vector.tensor_tensor(g3, g3, mass[:].unsqueeze(2).broadcast_to([P, HEADS, TOPK]), ALU.mult)
                    last.then_inc(picked, 1)
                    dve.wait_ge(turned, i + 1)
                    nc.vector.tensor_copy(giT[:, :, bass.ds(i * P, P)], gps[:]).then_inc(done, 1)
                    dve.wait_ge(done, i + 1)
                    ch.end(PER_TILE)


def peer_gates(nc, c, name, giT, gates):
    RING = 8
    ROUNDS = P // RING
    with Stage(nc, name) as s:
        first = [s.sb(f"first{i}", [P, NKEYS]) for i in range(RING)]
        second = [s.sb(f"second{i}", [P, NKEYS]) for i in range(RING)]
        grid = [s.sb(f"grid{i}", [P, NKEYS, P]) for i in range(2)]
        raised = s.sb("raised", [P, 1])
        bank = [s.ps(f"bank{i}", [P, 4, P]) for i in range(4)]
        zero, zeroed = s.sb("zero", [P, 1]), s.sem("zeroed")
        hot, spread, filled, stored = s.sem("hot"), s.sem("spread"), s.sem("filled"), s.sem("stored")
        with s.block() as block:
            @block.vector
            def _(dve):
                with dve.Fori(0, TT * ROUNDS) as i:
                    for r in range(RING):
                        if r % 4 == 0:
                            dve.wait_ge(spread, 2 * i + 1)
                        at = i * RING + r
                        nc.vector.tensor_scalar(first[r][:], c["iota"][:], giT[:, 1, bass.ds(at, 1)],
                                                giT[:, 0, bass.ds(at, 1)], ALU.is_equal, ALU.mult)
                        last = nc.vector.tensor_scalar(second[r][:], c["iota"][:], giT[:, 2, bass.ds(at, 1)],
                                                       None, ALU.is_equal)
                        if r % 4 == 3:
                            last.then_inc(hot, 1)

            @block.tensor
            def _(pe):
                starts_at_one(pe, spread)
                with pe.Fori(0, TT * ROUNDS // 2) as i:
                    for q in range(4):
                        pe.wait_ge(hot, 4 * i + q + 1)
                        pe.wait_ge(filled, 4 * i + q + 1)
                        for j in range(4):
                            r = (4 * q + j) % RING
                            last = nc.tensor.matmul(bank[q][:, j, :], second[r][:], first[r][:], start=True, stop=True)
                        last.then_inc(spread, 1)

            @block.scalar
            def _(act):
                act.wait_ge(zeroed, 1)
                nc.scalar.copy(raised[:, 0:1], zero[:, 0:1]).then_inc(filled, 4)
                with act.Fori(0, TT // 2) as pair:
                    for half in range(2):
                        act.wait_ge(stored, 32 * pair + 16)
                        with act.Fori(0, ROUNDS // 2) as i:
                            for q in range(4):
                                act.wait_ge(spread, (2 * pair + half) * (2 * ROUNDS) + 4 * i + q + 2)
                                nc.scalar.copy(grid[half][:, :, bass.ds(16 * i + 4 * q, 4)],
                                               bank[q][:].rearrange("p t n -> p n t")).then_inc(filled, 1)

            @block.gpsimd
            def _(pool):
                nc.gpsimd.memset(zero[:], 0.0).then_inc(zeroed, 1)

            @block.sync
            def _(sp):
                sp.sem_inc(stored, 16)
                for t in range(TT):
                    sp.wait_ge(filled, 4 + (t + 1) * P // 4)
                    sp.dma_start(gates[:, :, t * P:(t + 1) * P], grid[t % 2][:]).then_inc(stored, 16)
                sp.wait_ge(stored, 16 * (TT + 1))


def peer_experts(nc, c, name, hT, acc, u_tab, v_tab, gates):
    BLOCKS = NKEYS
    GROUP = 4
    OUTS = TT * HALVES
    with Stage(nc, name) as s:
        u = [s.sb(f"u{i}", [P, D]) for i in range(GROUP)]
        v = [s.sb(f"v{i}", [P, D]) for i in range(2 * GROUP)]
        g = [s.sb(f"g{i}", [P, SEQ]) for i in range(GROUP)]
        uT = [s.sb(f"uT{i}", [P, KC, P]) for i in range(2)]
        act_t = [s.sb(f"act{i}", [P, SEQ]) for i in range(2 * GROUP)]
        gel = [s.sb(f"gel{i}", [P, SEQ]) for i in range(2)]
        eased = s.sb("eased", [P, 1])
        tps = [s.ps(f"tps{i}", [P, BANK]) for i in range(2)]
        hps = [s.ps(f"hps{i}", [P, SEQ]) for i in range(2)]
        ops = [s.ps(f"ops{i}", [P, BANK]) for i in range(4)]
        load_u = [s.sem(f"load_u{i}") for i in range(GROUP)]
        load_v = [s.sem(f"load_v{i}") for i in range(2 * GROUP)]
        load_g = [s.sem(f"load_g{i}") for i in range(GROUP)]
        flip, flipped0, flipped1 = s.sem("flip"), s.sem("copied0"), s.sem("copied1")
        hid, gelued, gated, added = s.sem("hid"), s.sem("gelued"), s.sem("gated"), s.sem("added")
        summed = [s.sem(f"summed{i}") for i in range(2)]
        u_v = u_tab.rearrange("(b p) d -> b p d", p=P)
        v_v = v_tab.rearrange("(b p) d -> b p d", p=P)
        ROUND = 2 * GROUP
        with s.block() as block:
            @block.sync
            def _(sp):
                with sp.Fori(0, BLOCKS // ROUND) as i:
                    for b in range(ROUND):
                        at = i * ROUND + b
                        if b >= GROUP:
                            sp.wait_ge(gated, i * ROUND + b - GROUP + 2)
                        else:
                            sp.wait_ge(gated, i * ROUND + 1)
                        sp.dma_start(u[b % GROUP][:], u_v[bass.ds(at, 1)]).then_inc(load_u[b % GROUP], 16)
                        sp.dma_start(g[b % GROUP][:], gates[:, bass.ds(at, 1), :]).then_inc(load_g[b % GROUP], 16)
                        if b % GROUP == 0:
                            sp.wait_ge(summed[b // GROUP], OUTS * i + 1)
                        sp.dma_start(v[b][:], v_v[bass.ds(at, 1)]).then_inc(load_v[b], 16)

            @block.tensor
            def _(pe):
                starts_at_one(pe, flip, *summed)
                with pe.Fori(0, BLOCKS // ROUND) as i:
                    def flip_block(b):
                        pe.wait_ge(load_u[b % GROUP], 16 * (2 * i + b // GROUP + 1))
                        pe.wait_ge(flipped0, i * ROUND + b + 1)
                        pe.wait_ge(flipped1, i * ROUND + b + 1)
                        for half in range(2):
                            for j in range(4):
                                k = 4 * half + j
                                last = nc.tensor.transpose(tps[half][:, j * P:(j + 1) * P], u[b % GROUP][:, k * P:(k + 1) * P],
                                                           c["ident"][:])
                            last.then_inc(flip, 1)

                    for grp in range(2):
                        if grp == 0:
                            flip_block(0)
                        for x in range(GROUP):
                            b = GROUP * grp + x
                            if b + 1 < ROUND:
                                flip_block(b + 1)
                            pe.wait_ge(flipped0, i * ROUND + b + 2)
                            pe.wait_ge(flipped1, i * ROUND + b + 2)
                            if b >= 2:
                                pe.wait_ge(gelued, i * ROUND + b - 1)
                            for k in range(KC):
                                last = nc.tensor.matmul(hps[b % 2][:], uT[b % 2][:, k, :], hT[:, k, :],
                                                        start=(k == 0), stop=(k == KC - 1))
                            last.then_inc(hid, 1)
                        for part in range(OUTS // 4):
                            for x in range(GROUP):
                                b = GROUP * grp + x
                                if part == 0:
                                    pe.wait_ge(load_v[b], 16 * (i + 1))
                                    pe.wait_ge(gated, i * ROUND + b + 2)
                                for o in range(4):
                                    t, half = (4 * part + o) // HALVES, (4 * part + o) % HALVES
                                    if x == 0:
                                        pe.wait_ge(added, i * 2 * OUTS + grp * OUTS + 4 * part + o + OUTS - 3)
                                    last = nc.tensor.matmul(ops[o][:], act_t[b][:, t * P:(t + 1) * P],
                                                            v[b][:, half * BANK:(half + 1) * BANK],
                                                            start=(x == 0), stop=(x == GROUP - 1))
                                    if x == GROUP - 1:
                                        last.then_inc(summed[grp], 1)

            @block.scalar
            def _(act):
                starts_at_one(act, flipped1)
                with act.Fori(0, BLOCKS // ROUND) as i:
                    def copy_half(b):
                        act.wait_ge(flip, 2 * (i * ROUND + b) + 3)
                        if b >= 2:
                            act.wait_ge(hid, i * ROUND + b - 1)
                        nc.scalar.copy(uT[b % 2][:, 4:8, :], tps[1][:].rearrange("p (k n) -> p k n", n=P)).then_inc(flipped1, 1)

                    for grp in range(2):
                        if grp == 0:
                            copy_half(0)
                        for x in range(GROUP):
                            b = GROUP * grp + x
                            if b + 1 < ROUND:
                                copy_half(b + 1)
                            act.wait_ge(hid, i * ROUND + b + 1)
                            if b >= 2:
                                act.wait_ge(gated, i * ROUND + b)
                            nc.scalar.activation(gel[b % 2][:], hps[b % 2][:], ACT.Gelu).then_inc(gelued, 1)

            @block.vector
            def _(dve):
                nc.vector.memset(eased[:], 0.0).then_inc(added, OUTS)
                starts_at_one(dve, flipped0, gated)
                with dve.Fori(0, BLOCKS // ROUND) as i:
                    def copy_half(b):
                        dve.wait_ge(flip, 2 * (i * ROUND + b) + 2)
                        if b >= 2:
                            dve.wait_ge(hid, i * ROUND + b - 1)
                        nc.vector.tensor_copy(uT[b % 2][:, 0:4, :], tps[0][:].rearrange("p (k n) -> p k n", n=P)).then_inc(flipped0, 1)

                    for grp in range(2):
                        if grp == 0:
                            copy_half(0)
                        for x in range(GROUP):
                            b = GROUP * grp + x
                            if b + 1 < ROUND:
                                copy_half(b + 1)
                            dve.wait_ge(gelued, i * ROUND + b + 1)
                            dve.wait_ge(load_g[b % GROUP], 16 * (2 * i + b // GROUP + 1))
                            dve.wait_ge(summed[grp], i * OUTS + 1)
                            nc.vector.tensor_tensor(act_t[b][:], gel[b % 2][:], g[b % GROUP][:], ALU.mult).then_inc(gated, 1)
                        for o in range(OUTS):
                            dve.wait_ge(summed[grp], i * OUTS + o + 2)
                            dve.wait_ge(added, i * 2 * OUTS + grp * OUTS + o + 1)
                            t, half = o // HALVES, o % HALVES
                            nc.vector.tensor_tensor(acc[:, t, half * BANK:(half + 1) * BANK],
                                                    acc[:, t, half * BANK:(half + 1) * BANK], ops[o % 4][:],
                                                    ALU.add).then_inc(added, 1)


GDN_HEADS = 8
GDN_QKV = 3 * GDN_HEADS
CONV = 4


def gdn_project(nc, c, name, xT, w_in, conv_w, qkvT, z, logits):
    SLABS = GDN_QKV * P // BANK
    PER = BANK // P
    ROUND = 2 * PER
    with Stage(nc, name) as s:
        wslab = [s.sb(f"wslab{i}", [P, KC, BANK]) for i in range(2)]
        wtail = s.sb("wtail", [P, KC, 2 * GDN_HEADS])
        taps = s.sb("taps", [P, P])
        tapsT = s.sb("tapsT", [P, CONV * GDN_QKV])
        conv = [s.sb(f"conv{i}", [P, SEQ]) for i in range(2)]
        pp = [s.ps(f"pp{i}", [P, BANK]) for i in range(4)]
        taps_ps = s.ps("taps_ps", [P, CONV * GDN_QKV])
        load_w, load_z = [s.sem("load_w0"), s.sem("load_w1")], [s.sem("load_z0"), s.sem("load_z1")]
        load_taps, taps_turned, taps_ready = s.sem("load_taps"), s.sem("taps_turned"), s.sem("taps_ready")
        projected, mixed, convolved, silued = s.sem("projected"), s.sem("mixed"), s.sem("convolved"), s.sem("silued")
        zmade, ztaken = s.sem("zmade"), s.sem("ztaken")
        w_v = w_in[:, 0:(SLABS + 2) * BANK].rearrange("(k p) (s n) -> s p k n", p=P, n=BANK)
        with s.block() as block:
            @block.sync
            def _(sp):
                sp.dma_start(taps[0:CONV * GDN_QKV, :], conv_w.rearrange("j (t c) -> (j t) c", c=P)).then_inc(load_taps, 16)
                with nc.allow_non_contiguous_dma(reason="sixteen columns"):
                    sp.dma_start(wtail[:], w_in[:, (SLABS + 2) * BANK:].rearrange("(k p) n -> p k n", p=P)).then_inc(load_taps, 16)
                with sp.Fori(0, SLABS // 2) as i:
                    for b in range(2):
                        sp.wait_ge(projected, i * ROUND + 1)
                        sp.dma_start(wslab[b][:], w_v[bass.ds(2 * i + b, 1)]).then_inc(load_w[b], 16)
                for b in range(2):
                    sp.wait_ge(projected, SLABS * PER + 1)
                    sp.dma_start(wslab[b][:], w_v[SLABS + b]).then_inc(load_z[b], 16)

            @block.tensor
            def _(pe):
                starts_at_one(pe, projected)
                pe.wait_ge(load_taps, 32)
                n = CONV * GDN_QKV
                nc.tensor.transpose(taps_ps[:], taps[0:n, :], c["ident"][0:n, 0:n]).then_inc(taps_turned, 1)
                with pe.Fori(0, SLABS // 2) as i:
                    for b in range(2):
                        pe.wait_ge(load_w[b], 16 * (i + 1))
                        for j in range(PER):
                            n = b * PER + j
                            pe.wait_ge(convolved, i * ROUND + n + 1)
                            for k in range(KC):
                                last = nc.tensor.matmul(pp[n % 4][:], wslab[b][:, k, j * P:(j + 1) * P], xT[:, k, :],
                                                        start=(k == 0), stop=(k == KC - 1))
                            last.then_inc(projected, 1)
                pe.wait_ge(convolved, SLABS * PER + 4)
                for b in range(2):
                    pe.wait_ge(load_z[b], 16)
                    for t in range(TT):
                        n = b * TT + t
                        if n >= 4:
                            pe.wait_ge(ztaken, n - 3)
                        for k in range(KC):
                            last = nc.tensor.matmul(pp[n % 4][:], xT[:, k, t * P:(t + 1) * P], wslab[b][:, k, :],
                                                    start=(k == 0), stop=(k == KC - 1))
                        last.then_inc(zmade, 1)
                pe.wait_ge(ztaken, 5)
                for t in range(TT):
                    for k in range(KC):
                        last = nc.tensor.matmul(pp[0][:, t * 16:(t + 1) * 16], xT[:, k, t * P:(t + 1) * P], wtail[:, k, :],
                                                start=(k == 0), stop=(k == KC - 1))
                last.then_inc(zmade, 1)

            @block.vector
            def _(dve):
                dve.wait_ge(taps_turned, 1)
                nc.vector.tensor_copy(tapsT[:], taps_ps[:]).then_inc(taps_ready, 1)
                dve.wait_ge(taps_ready, 1)
                nc.vector.memset(conv[0][:, 0:1], 0.0).then_inc(convolved, 4)
                with dve.Fori(0, SLABS // 2) as i:
                    ch = Chain(dve, mixed, i * (ROUND * (CONV - 1)))
                    for n in range(ROUND):
                        at = i * ROUND + n
                        src, dst = pp[n % 4], conv[n % 2]
                        dve.wait_ge(projected, at + 2)
                        dve.wait_ge(silued, at + 1)

                        def tap(j):
                            return tapsT[:, bass.ds(at + j * GDN_QKV, 1)]

                        ch.link(nc.vector.tensor_scalar(dst[:], src[:], tap(CONV - 1), None, ALU.mult))
                        for back in range(1, CONV):
                            last = nc.vector.scalar_tensor_tensor(dst[:, back:], src[:, 0:SEQ - back], tap(CONV - 1 - back),
                                                                  dst[:, back:], ALU.mult, ALU.add)
                            if back < CONV - 1:
                                ch.link(last)
                        last.then_inc(convolved, 1)
                    ch.end(ROUND * (CONV - 1))

            @block.scalar
            def _(act):
                act.wait_ge(taps_ready, 1)
                nc.scalar.copy(conv[1][:, 0:1], tapsT[:, 0:1]).then_inc(silued, 2)
                with act.Fori(0, SLABS // 2) as i:
                    for n in range(ROUND):
                        at = i * ROUND + n
                        act.wait_ge(convolved, at + 5)
                        nc.scalar.activation(qkvT[:, bass.ds(at, 1), :], conv[n % 2][:].unsqueeze(1), ACT.Silu).then_inc(silued, 1)
                for n in range(2 * TT):
                    act.wait_ge(zmade, n + 1)
                    nc.scalar.activation(z[:, n % TT, (n // TT) * BANK:(n // TT + 1) * BANK], pp[n % 4][:],
                                         ACT.Silu).then_inc(ztaken, 1)
                act.wait_ge(zmade, 2 * TT + 1)
                nc.scalar.copy(logits[:], pp[0][:, 0:TT * 16].rearrange("p (t n) -> p t n", t=TT)).then_inc(ztaken, 1)
                act.wait_ge(ztaken, 2 * TT + 1)


def gdn_normalize(nc, c, name, qkvT):
    GROUP = 4
    with Stage(nc, name) as s:
        sq = [s.sb(f"sq{i}", [P, SEQ]) for i in range(GROUP)]
        rt = [s.sb(f"rt{i}", [P, SEQ]) for i in range(GROUP)]
        eps = [s.sb(f"eps{i}", [P, 1]) for i in range(2)]
        total = [s.ps(f"total{i}", [P, SEQ]) for i in range(GROUP)]
        squared, summed, rooted, halved, scaled = s.sem("squared"), s.sem("summed"), s.sem("rooted"), s.sem("halved"), s.sem("scaled")
        ready = s.sem("ready")
        rounds = 2 * GDN_HEADS // GROUP
        with s.block() as block:
            @block.scalar
            def _(act):
                starts_at_one(act, rooted)
                act.wait_ge(ready, 2)
                for part, mul in ((0, float(P)), (1, 1.0)):
                    with act.Fori(0, rounds // 2) as i:
                        base = (i + part * (rounds // 2)) * GROUP
                        for n in range(GROUP):
                            act.wait_ge(summed, base + 1)
                            nc.scalar.activation(sq[n][:].unsqueeze(1), qkvT[:, bass.ds(base + n, 1), :], ACT.Square).then_inc(squared, 1)
                        for n in range(GROUP):
                            act.wait_ge(summed, base + n + 2)
                            act.wait_ge(scaled, base + 1)
                            nc.scalar.activation(rt[n][:], total[n][:], ACT.Sqrt, bias=eps[part][:], scale=mul).then_inc(rooted, 1)

            @block.tensor
            def _(pe):
                starts_at_one(pe, summed)
                with pe.Fori(0, rounds) as i:
                    for n in range(GROUP):
                        pe.wait_ge(squared, i * GROUP + n + 1)
                        pe.wait_ge(rooted, i * GROUP + 1)
                        nc.tensor.matmul(total[n][:], c["ones"][:], sq[n][:], start=True, stop=True).then_inc(summed, 1)

            @block.vector
            def _(dve):
                starts_at_one(dve, scaled)
                nc.vector.memset(eps[0][:], P * RMS_EPS).then_inc(ready, 1)
                nc.vector.memset(eps[1][:], RMS_EPS).then_inc(ready, 1)
                with dve.Fori(0, rounds) as i:
                    for n in range(GROUP):
                        dve.wait_ge(rooted, i * GROUP + n + 2)
                        nc.vector.reciprocal(rt[n][:], rt[n][:]).then_inc(halved, 1)
                    for n in range(GROUP):
                        dve.wait_ge(halved, i * GROUP + n + 1)
                        at = qkvT[:, bass.ds(i * GROUP + n, 1), :]
                        nc.vector.tensor_tensor(at, at, rt[n][:].unsqueeze(1), ALU.mult).then_inc(scaled, 1)
                dve.wait_ge(scaled, rounds * GROUP + 1)


def gdn_gates(nc, c, name, logits, a_log, dt_bias, gate):
    H = GDN_HEADS
    with Stage(nc, name) as s:
        arow, brow = s.sb("arow", [P, H]), s.sb("brow", [P, H])
        x, e, t = s.sb("x", [P, TT, H]), s.sb("e", [P, TT, H]), s.sb("t", [P, TT, H])
        sums = s.ps("sums", [P, 2, TT * H])
        load, chain, acted, summed = s.sem("load"), s.sem("chain"), s.sem("acted"), s.sem("summed")
        wide = lambda ap: ap.unsqueeze(1).broadcast_to([P, TT, H])
        flat = lambda ap: ap.rearrange("p t h -> p (t h)")
        with s.block() as block:
            @block.sync
            def _(sp):
                sp.dma_start(arow[:], a_log.broadcast_to([P, H])).then_inc(load, 16)
                sp.dma_start(brow[:], dt_bias.broadcast_to([P, H])).then_inc(load, 16)

            @block.vector
            def _(dve):
                ch = Chain(dve, chain)
                dve.wait_ge(load, 32)
                ch.link(nc.vector.tensor_tensor(x[:], logits[:, :, H:2 * H], wide(brow[:]), ALU.add))
                ch.link(nc.vector.tensor_scalar(t[:], x[:], -1.0, None, ALU.mult))
                ch.link(nc.vector.tensor_tensor(t[:], t[:], x[:], ALU.min))
                dve.wait_ge(acted, 4)
                ch.link(nc.vector.tensor_scalar(gate["beta"][:], gate["beta"][:], 1.0, None, ALU.add))
                ch.link(nc.vector.reciprocal(gate["beta"][:], gate["beta"][:]))
                ch.link(nc.vector.tensor_scalar(x[:], x[:], 0.0, None, ALU.max))
                ch.link(nc.vector.tensor_tensor(x[:], x[:], e[:], ALU.add))
                ch.link(nc.vector.tensor_tensor(x[:], x[:], wide(arow[:]), ALU.mult))
                ch.link(nc.vector.tensor_scalar(gate["g"][:], x[:], -1.0, None, ALU.mult))
                dve.wait_ge(summed, 1)
                ch.link(nc.vector.tensor_copy(flat(gate["sum"][:]), sums[:, 0, :]))
                ch.link(nc.vector.tensor_copy(flat(gate["last"][:]), sums[:, 1, :]))
                ch.link(nc.vector.tensor_tensor(gate["rest"][:], gate["last"][:], gate["sum"][:], ALU.subtract))
                dve.wait_ge(acted, 7)
                ch.link(nc.vector.tensor_tensor(gate["beta_exp"][:], gate["beta"][:], gate["exp"][:], ALU.mult))

            @block.scalar
            def _(act):
                act.wait_ge(load, 32)
                nc.scalar.activation(arow[:], arow[:], ACT.Exp).then_inc(acted, 1)
                nc.scalar.activation(gate["beta"][:], logits[:, :, 0:H], ACT.Exp, scale=-1.0).then_inc(acted, 1)
                act.wait_ge(chain, 3)
                nc.scalar.activation(e[:], t[:], ACT.Exp).then_inc(acted, 1)
                act.wait_ge(acted, 3)
                nc.scalar.activation(e[:], e[:], ACT.Ln, bias=c["ones"][:, 0:1]).then_inc(acted, 1)
                act.wait_ge(chain, 12)
                nc.scalar.activation(gate["exp"][:], gate["sum"][:], ACT.Exp).then_inc(acted, 1)
                nc.scalar.activation(gate["last"][:], gate["last"][:], ACT.Exp).then_inc(acted, 1)
                nc.scalar.activation(gate["rest"][:], gate["rest"][:], ACT.Exp).then_inc(acted, 1)

            @block.tensor
            def _(pe):
                pe.wait_ge(chain, 9)
                nc.tensor.matmul(sums[:, 0, :], c["upper"][:], flat(gate["g"][:]), start=True, stop=True)
                nc.tensor.matmul(sums[:, 1, :], c["ones"][:], flat(gate["g"][:]), start=True, stop=True).then_inc(summed, 1)


class Steps:

    def __init__(self, names, heads):
        self.names, self.heads = names.split(), heads
        assert len(set(self.names)) == len(self.names)

    def after(self, i, name, j):
        return i * (len(self.names) * self.heads) + self.names.index(name) * self.heads + j + 2

    def rounds(self, i):
        return i * (len(self.names) * self.heads) + 1


def gdn_recur(nc, c, name, qkvT, gate, o):
    G = 2
    H, C = GDN_HEADS, TT
    PE_STEPS = Steps("row kk knat vnat qk decT LT L2 U2 Y1 L4 U4 Y2 L8 Y3 YT N NT W0 N2 N2T W1 N4T W2 wT "
                     + " ".join(f"v{n} s{n} o{n}" for n in range(C)), G)
    ACT_STEPS = Steps("gB kS vS dec expRow decMT U L2 L4 L8 YT N N2 N4T wT " + " ".join(f"v{n} o{n}" for n in range(C)), G)
    DVE_STEPS = Steps("gap decM qg kbg kdec vb L0 L attnT LD UD UO Y0 U2 Y1 U4 Y2 Y3 NT W0 N2T W1 W2 "
                      + " ".join(f"s{n}" for n in range(C)), G)
    with Stage(nc, name) as s:
        names = ("gB kS vS gap decM qg kbg kdec vb L attnT decMT LD U UO Y0 Y1 Y2 Y3 L2 U2 expRow vnew").split()
        b = {n: [s.sb(f"{n}{j}", [P, C, P]) for j in range(G)] for n in names}
        for new, old in (("L4", "LD"), ("U4", "expRow"), ("L8", "gap"), ("YT", "gB"), ("N", "L"), ("NT", "decM"),
                         ("W0", "Y0"), ("N2", "L2"), ("N2T", "U2"), ("W1", "Y1"), ("N4T", "Y2"), ("W2", "kS"), ("wT", "decMT")):
            b[new] = b[old]
        UD = [s.sb(f"UD{j}", [P, C, P]) for j in range(G)]
        b["UD"] = UD
        state = [s.sb(f"state{j}", [P, P]) for j in range(G)]
        bank = [[s.ps(f"bank{j}_{k}", [P, C, P]) for k in range(8 // G)] for j in range(G)]
        pe_done, act_done, dve_done = s.sem("pe_done"), s.sem("act_done"), s.sem("dve_done")
        ident4 = c["ident"][:].unsqueeze(1).broadcast_to([P, C, P])
        block4 = c["block16"][:].unsqueeze(1).broadcast_to([P, C, P])
        lower4 = c["lower"][:].unsqueeze(1).broadcast_to([P, C, P])
        strict4 = c["strict"][:].unsqueeze(1).broadcast_to([P, C, P])

        def ps(step, j):
            return bank[j][PE_STEPS.names.index(step) % len(bank[j])]

        with s.block() as block:
            @block.tensor
            def _(pe):
                starts_at_one(pe, pe_done)
                with pe.Fori(0, H // G) as i:

                    def from_act(step, j):
                        pe.wait_ge(act_done, ACT_STEPS.after(i, step, j))

                    def from_dve(step, j):
                        pe.wait_ge(dve_done, DVE_STEPS.after(i, step, j))

                    def each(step, lhsT, rhs, acts=(), dves=()):
                        for j in range(G):
                            for a in acts:
                                from_act(a, j)
                            for d in dves:
                                from_dve(d, j)
                            for n in range(C):
                                last = nc.tensor.matmul(ps(step, j)[:, n, :], lhsT(j, n), rhs(j, n), start=True, stop=True)
                            last.then_inc(pe_done, 1)

                    def turn(step, src, acts=(), dves=()):
                        for j in range(G):
                            for a in acts:
                                from_act(a, j)
                            for d in dves:
                                from_dve(d, j)
                            for n in range(C):
                                last = nc.tensor.transpose(ps(step, j)[:, n, :], src(j, n), c["ident"][:])
                            last.then_inc(pe_done, 1)

                    def of(m):
                        return lambda j, n: b[m][j][:, n, :]

                    each("row", of("gB"), lambda j, n: c["upper"][:], acts=["gB"])
                    each("kk", of("kS"), of("kS"), acts=["kS"])
                    turn("knat", of("kS"))
                    turn("vnat", of("vS"), acts=["vS"])
                    each("qk", of("kS"), lambda j, n: qkvT[:, bass.ds(i * G + j, 1), n * P:(n + 1) * P],
                         acts=["expRow"], dves=["gap"])
                    turn("decT", of("decM"), dves=["L0"])
                    turn("LT", of("L"), dves=["L", "kdec"])
                    each("L2", of("UD"), of("LD"), dves=["UD", "vb"])
                    each("U2", of("LD"), of("UD"), dves=["attnT"])
                    each("Y1", of("L2"), of("Y0"), acts=["L2", "decMT"], dves=["Y0"])
                    each("L4", of("U2"), of("L2"), acts=["U"], dves=["U2"])
                    each("U4", of("L2"), of("U2"))
                    each("Y2", of("L4"), of("Y1"), acts=["L4"], dves=["Y1"])
                    each("L8", of("U4"), of("L4"), dves=["U4"])
                    each("Y3", of("L8"), of("Y2"), acts=["L8"], dves=["Y2"])
                    turn("YT", of("Y3"), dves=["Y3"])
                    each("N", of("YT"), of("UO"), acts=["YT"], dves=["UO"])
                    each("NT", of("UO"), of("YT"))
                    each("W0", of("NT"), of("Y3"), dves=["NT"])
                    each("N2", of("NT"), of("N"), acts=["N"])
                    each("N2T", of("N"), of("NT"))
                    each("W1", of("N2T"), of("W0"), dves=["N2T", "W0"])
                    each("N4T", of("N2"), of("N2T"), acts=["N2"])
                    each("W2", of("N4T"), of("W1"), acts=["N4T"], dves=["W1"])
                    each("wT", of("kbg"), of("W2"), dves=["W2"])
                    for n in range(C):
                        for j in range(G):
                            new = ps(f"v{n}", j)[:, 0, :]
                            last = nc.tensor.matmul(new, b["W2"][j][:, n, :], b["vb"][j][:, n, :], start=True, stop=(n == 0))
                            if n:
                                from_act("wT", j)
                                from_dve(f"s{n - 1}", j)
                                last = nc.tensor.matmul(new, b["wT"][j][:, n, :], state[j][:], start=False, stop=True)
                            last.then_inc(pe_done, 1)
                        for j in range(G):
                            from_act(f"v{n}", j)
                            nc.tensor.matmul(ps(f"s{n}", j)[:, 0, :], b["kdec"][j][:, n, :], b["vnew"][j][:, n, :],
                                             start=True, stop=True).then_inc(pe_done, 1)
                        for j in range(G):
                            if n:
                                nc.tensor.matmul(ps(f"o{n}", j)[:, 0, :], b["qg"][j][:, n, :], state[j][:],
                                                 start=True, stop=False)
                            nc.tensor.matmul(ps(f"o{n}", j)[:, 0, :], b["attnT"][j][:, n, :], b["vnew"][j][:, n, :],
                                             start=(n == 0), stop=True).then_inc(pe_done, 1)

            @block.scalar
            def _(act):
                starts_at_one(act, act_done)
                with act.Fori(0, H // G) as i:
                    def do(step, make, pes=(), dves=(), acts=()):
                        for j in range(G):
                            for p in pes:
                                act.wait_ge(pe_done, PE_STEPS.after(i, p, j))
                            for d in dves:
                                act.wait_ge(dve_done, DVE_STEPS.after(i, d, j))
                            for a in acts:
                                act.wait_ge(act_done, ACT_STEPS.after(i, a, j))
                            make(j).then_inc(act_done, 1)

                    def copy(step):
                        do(step, lambda j: nc.scalar.copy(b[step][j][:], ps(step, j)[:]), pes=[step])

                    act.wait_ge(pe_done, PE_STEPS.rounds(i))
                    act.wait_ge(dve_done, DVE_STEPS.rounds(i))
                    do("gB", lambda j: nc.scalar.copy(b["gB"][j][:], gate["g"][:, :, bass.ds(i * G + j, 1)].broadcast_to([P, C, P])))
                    for part, step in ((1, "kS"), (2, "vS")):
                        do(step, lambda j: nc.scalar.copy(b[step][j][:].rearrange("p n t -> p (n t)").unsqueeze(1),
                                                          qkvT[:, bass.ds(i * G + j + part * H, 1), :]))
                    do("dec", lambda j: nc.scalar.activation(b["gap"][j][:], b["gap"][j][:], ACT.Exp, scale=-1.0), dves=["gap"])
                    do("expRow", lambda j: nc.scalar.activation(b["expRow"][j][:], ps("row", j)[:], ACT.Exp), pes=["row"])
                    do("decMT", lambda j: nc.scalar.copy(b["decMT"][j][:], ps("decT", j)[:]), pes=["decT"])
                    do("U", lambda j: nc.scalar.copy(b["U"][j][:], ps("LT", j)[:]), pes=["LT"])
                    copy("L2")
                    do("L4", lambda j: nc.scalar.copy(b["L4"][j][:], ps("L4", j)[:]), pes=["L4"])
                    copy("L8")
                    copy("YT")
                    copy("N")
                    copy("N2")
                    copy("N4T")
                    do("wT", lambda j: nc.scalar.mul(b["wT"][j][:], ps("wT", j)[:], -1.0), pes=["wT"])
                    for n in range(C):
                        do(f"v{n}", lambda j: nc.scalar.copy(b["vnew"][j][:, n, :], ps(f"v{n}", j)[:, 0, :]), pes=[f"v{n}"])
                        do(f"o{n}", lambda j: nc.scalar.copy(o[:, n, bass.ds((i * G + j) * P, P)], ps(f"o{n}", j)[:, 0, :]), pes=[f"o{n}"])
                act.wait_ge(act_done, ACT_STEPS.rounds(H // G))

            @block.vector
            def _(dve):
                starts_at_one(dve, dve_done)
                with dve.Fori(0, H // G) as i:
                    def do(step, make, pes=(), acts=(), dves=()):
                        for j in range(G):
                            for p in pes:
                                dve.wait_ge(pe_done, PE_STEPS.after(i, p, j))
                            for a in acts:
                                dve.wait_ge(act_done, ACT_STEPS.after(i, a, j))
                            for d in dves:
                                dve.wait_ge(dve_done, DVE_STEPS.after(i, d, j))
                            make(j).then_inc(dve_done, 1)

                    def col(m, j):
                        return gate[m][:, :, bass.ds(i * G + j, 1)].broadcast_to([P, C, P])

                    tt = nc.vector.tensor_tensor

                    def gaps(j):
                        for n in range(C):
                            last = nc.vector.tensor_scalar(b["gap"][j][:, n, :], ps("row", j)[:, n, :],
                                                           gate["sum"][:, n, bass.ds(i * G + j, 1)], 0.0, ALU.subtract, ALU.max)
                        return last

                    def lows(j):
                        for n in range(C):
                            last = nc.vector.scalar_tensor_tensor(b["L"][j][:, n, :], ps("kk", j)[:, n, :],
                                                                  gate["beta"][:, n, bass.ds(i * G + j, 1)],
                                                                  b["decM"][j][:, n, :], ALU.mult, ALU.mult)
                        return last

                    do("gap", gaps, pes=["row"])
                    do("decM", lambda j: tt(b["decM"][j][:], b["gap"][j][:], lower4, ALU.mult), acts=["dec"])
                    do("qg", lambda j: tt(b["qg"][j][:].rearrange("p n t -> p (n t)").unsqueeze(1),
                                          qkvT[:, bass.ds(i * G + j, 1), :],
                                          b["expRow"][j][:].rearrange("p n t -> p (n t)").unsqueeze(1), ALU.mult), acts=["expRow"])
                    do("kbg", lambda j: tt(b["kbg"][j][:], ps("knat", j)[:], col("beta_exp", j), ALU.mult), pes=["knat"])
                    do("kdec", lambda j: tt(b["kdec"][j][:], ps("knat", j)[:], col("rest", j), ALU.mult))
                    do("vb", lambda j: tt(b["vb"][j][:], ps("vnat", j)[:], col("beta", j), ALU.mult), pes=["vnat"])
                    do("L0", lows, pes=["kk"], dves=["decM"])
                    do("L", lambda j: tt(b["L"][j][:], b["L"][j][:], strict4, ALU.mult), dves=["L0"])
                    do("attnT", lambda j: tt(b["attnT"][j][:], ps("qk", j)[:], b["decMT"][j][:], ALU.mult), pes=["qk"], acts=["decMT"])
                    do("LD", lambda j: tt(b["LD"][j][:], b["L"][j][:], block4, ALU.mult), dves=["L"])
                    do("UD", lambda j: tt(b["UD"][j][:], b["U"][j][:], block4, ALU.mult), acts=["U"])
                    do("UO", lambda j: tt(b["UO"][j][:], b["U"][j][:], b["UD"][j][:], ALU.subtract), dves=["UD"])
                    do("Y0", lambda j: tt(b["Y0"][j][:], ident4, b["UD"][j][:], ALU.subtract))
                    do("U2", lambda j: nc.vector.tensor_copy(b["U2"][j][:], ps("U2", j)[:]), pes=["U2"])
                    do("Y1", lambda j: tt(b["Y1"][j][:], b["Y0"][j][:], ps("Y1", j)[:], ALU.add), pes=["Y1"])
                    do("U4", lambda j: nc.vector.tensor_copy(b["U4"][j][:], ps("U4", j)[:]), pes=["U4"])
                    do("Y2", lambda j: tt(b["Y2"][j][:], b["Y1"][j][:], ps("Y2", j)[:], ALU.add), pes=["Y2"], dves=["Y1"])
                    do("Y3", lambda j: tt(b["Y3"][j][:], b["Y2"][j][:], ps("Y3", j)[:], ALU.add), pes=["Y3"], dves=["Y2"])
                    do("NT", lambda j: nc.vector.tensor_copy(b["NT"][j][:], ps("NT", j)[:]), pes=["NT"])
                    do("W0", lambda j: tt(b["W0"][j][:], b["Y3"][j][:], ps("W0", j)[:], ALU.subtract), pes=["W0"])
                    do("N2T", lambda j: nc.vector.tensor_copy(b["N2T"][j][:], ps("N2T", j)[:]), pes=["N2T"])
                    do("W1", lambda j: tt(b["W1"][j][:], b["W0"][j][:], ps("W1", j)[:], ALU.add), pes=["W1"], dves=["W0"])
                    do("W2", lambda j: tt(b["W2"][j][:], b["W1"][j][:], ps("W2", j)[:], ALU.add), pes=["W2"], dves=["W1"])
                    do("s0", lambda j: nc.vector.tensor_copy(state[j][:], ps("s0", j)[:, 0, :]), pes=["s0"])
                    for n in range(1, C):
                        do(f"s{n}", lambda j: nc.vector.scalar_tensor_tensor(
                            state[j][:], state[j][:], gate["last"][:, n, bass.ds(i * G + j, 1)], ps(f"s{n}", j)[:, 0, :],
                            ALU.mult, ALU.add), pes=[f"s{n}", f"o{n}"], dves=[f"s{n - 1}"])
                dve.wait_ge(dve_done, DVE_STEPS.rounds(H // G))


def gdn_gate_out(nc, c, name, o, z, norm_g):
    H, L = GDN_HEADS, TT * GDN_HEADS
    with Stage(nc, name) as s:
        sq = s.sb("sq", [P, L, P])
        ss = s.sb("ss", [P, L])
        grow = s.sb("grow", [P, P])
        eps = s.sb("eps", [P, 1])
        load, chain, rooted = s.sem("load"), s.sem("chain"), s.sem("rooted")
        o3 = o[:].rearrange("p t (h d) -> p (t h) d", d=P)
        z3 = z[:].rearrange("p t (h d) -> p (t h) d", d=P)
        with s.block() as block:
            @block.sync
            def _(sp):
                sp.dma_start(grow[:], norm_g.broadcast_to([P, P])).then_inc(load, 16)

            @block.vector
            def _(dve):
                ch = Chain(dve, chain)
                ch.link(nc.vector.memset(eps[:], RMS_EPS))
                ch.link(nc.vector.tensor_tensor(sq[:], o3, o3, ALU.mult))
                ch.link(nc.vector.tensor_reduce(ss[:], sq[:], axis=AX.X, op=ALU.add))
                dve.wait_ge(rooted, 1)
                ch.link(nc.vector.reciprocal(ss[:], ss[:]))
                ch.link(nc.vector.tensor_tensor(o3, o3, ss[:].unsqueeze(2).broadcast_to([P, L, P]), ALU.mult))
                dve.wait_ge(load, 16)
                ch.link(nc.vector.tensor_tensor(o3, o3, grow[:].unsqueeze(1).broadcast_to([P, L, P]), ALU.mult))
                ch.link(nc.vector.tensor_tensor(o3, o3, z3, ALU.mult))

            @block.scalar
            def _(act):
                act.wait_ge(chain, 3)
                nc.scalar.activation(ss[:], ss[:], ACT.Sqrt, bias=eps[:], scale=1.0 / P).then_inc(rooted, 1)


def project_out(nc, c, name, oT, w_out, h):
    with Stage(nc, name) as s:
        w = s.sb("w", [P, KC, D])
        bank = [s.ps(f"bank{i}", [P, BANK]) for i in range(4)]
        load, made, added = s.sem("load"), s.sem("made"), s.sem("added")
        with s.block() as block:
            @block.sync
            def _(sp):
                sp.dma_start(w[:], w_out.rearrange("(k p) n -> p k n", p=P)).then_inc(load, 16)

            @block.tensor
            def _(pe):
                pe.wait_ge(load, 16)
                for n in range(TT * HALVES):
                    t, half = n // HALVES, n % HALVES
                    if n >= 4:
                        pe.wait_ge(added, n - 3)
                    for k in range(KC):
                        last = nc.tensor.matmul(bank[n % 4][:], oT[:, k, t * P:(t + 1) * P], w[:, k, half * BANK:(half + 1) * BANK],
                                                start=(k == 0), stop=(k == KC - 1))
                    last.then_inc(made, 1)

            @block.vector
            def _(dve):
                for n in range(TT * HALVES):
                    t, half = n // HALVES, n % HALVES
                    dve.wait_ge(made, n + 1)
                    piece = h[:, t, half * BANK:(half + 1) * BANK]
                    nc.vector.scalar_tensor_tensor(piece, piece, ALPHA, bank[n % 4][:], ALU.mult, ALU.add).then_inc(added, 1)
                dve.wait_ge(added, TT * HALVES)


def normalize(nc, c, name, h, ln_g, ln_b):
    with Stage(nc, name) as s:
        grow, brow = s.sb("grow", [P, D]), s.sb("brow", [P, D])
        stats = s.sb("stats", [P, TT, 2, 6])
        mv = s.sb("mv", [P, TT, 2])
        std, eps = s.sb("std", [P, TT]), s.sb("eps", [P, 1])
        load, chain, rooted = s.sem("load"), s.sem("chain"), s.sem("rooted")
        with s.block() as block:
            @block.sync
            def _(sp):
                sp.dma_start(grow[:], ln_g.broadcast_to([P, D])).then_inc(load, 16)
                sp.dma_start(brow[:], ln_b.broadcast_to([P, D])).then_inc(load, 16)

            @block.vector
            def _(dve):
                ch = Chain(dve, chain)
                for t in range(TT):
                    for half in range(2):
                        last = nc.vector.bn_stats(stats[:, t, half, :], h[:, t, half * BANK:(half + 1) * BANK])
                nc.vector.memset(eps[:], LN_EPS)
                ch.link(last)
                for t in range(TT):
                    last = nc.vector.bn_aggr(mv[:, t, :], stats[:, t, :, :])
                ch.link(last)
                dve.wait_ge(rooted, 1)
                ch.link(nc.vector.reciprocal(std[:], std[:]))
                for t in range(TT):
                    last = nc.vector.tensor_scalar(h[:, t, :], h[:, t, :], mv[:, t, 0:1], std[:, t:t + 1], ALU.subtract, ALU.mult)
                ch.link(last)
                dve.wait_ge(load, 32)
                wide = lambda ap: ap.unsqueeze(1).broadcast_to([P, TT, D])
                ch.link(nc.vector.tensor_tensor(h[:], h[:], wide(grow[:]), ALU.mult))
                ch.link(nc.vector.tensor_tensor(h[:], h[:], wide(brow[:]), ALU.add))

            @block.scalar
            def _(act):
                act.wait_ge(chain, 2)
                nc.scalar.activation(std[:], mv[:, :, 1], ACT.Sqrt, bias=eps[:]).then_inc(rooted, 1)


def gdn_layer(nc, c, h, w_in, conv_w, a_log, dt_bias, norm_g, w_out, debug=None):
    with Stage(nc, "gdn") as s:
        o, z = s.sb("o", [P, TT, D]), s.sb("z", [P, TT, D])
        gate = {n: s.sb(n, [P, TT, GDN_HEADS]) for n in ("g", "sum", "last", "rest", "exp", "beta", "beta_exp")}
        with Stage(nc, "gdn_in") as s1:
            qkvT = s1.sb("qkvT", [P, GDN_QKV, SEQ])
            logits = s1.sb("logits", [P, TT, 2 * GDN_HEADS])
            with Stage(nc, "gdn_x") as s2:
                xT = s2.sb("xT", [P, KC, SEQ])
                transpose_tokens(nc, c, h, xT)
                gdn_project(nc, c, "gdnp", xT, w_in, conv_w, qkvT, z, logits)
            gdn_normalize(nc, c, "gdnn", qkvT)
            gdn_gates(nc, c, "gdng", logits, a_log, dt_bias, gate)
            gdn_recur(nc, c, "gdnr", qkvT, gate, o)
        gdn_gate_out(nc, c, "gdno", o, z, norm_g)
        with Stage(nc, "gdn_out") as s1:
            oT = s1.sb("oT", [P, KC, SEQ])
            transpose_tokens(nc, c, o, oT)
            project_out(nc, c, "gdnq", oT, w_out, h)
        if debug is not None:
            st = s.sem("dbg")
            with nc.Block() as b:
                @b.sync
                def _(sp):
                    sp.dma_start(debug.rearrange("(t p) d -> p t d", p=P), h[:]).then_inc(st, 16)
                    sp.wait_ge(st, 16)


MLA_HEADS, NOPE, ROPE, VDIM = 16, 64, 32, 64
QK = NOPE + ROPE
HALF = ROPE // 2
KV_RANK, Q_RANK = 256, 384
THETA = 10000.0
TWO_PI = 2.0 * math.pi


def parts_of(x, bits, n):
    parts = []
    for _ in range(n - 1):
        unit = 2.0 ** (math.floor(math.log2(abs(x))) + 1 - bits)
        parts.append(math.floor(x / unit) * unit)
        x -= parts[-1]
    return parts + [x]


def rope_tables(nc, c, name, positions, cos, sin):
    MAGIC = 1.5 * 2.0 ** 23
    EDGE = 3.1415925
    with Stage(nc, name) as s:
        posi, pos = s.sb("posi", [P, TT], I32), s.sb("pos", [P, TT])
        freq = s.sb("freq", [P, HALF])
        ang, turns, low = s.sb("ang", [P, TT, HALF]), s.sb("turns", [P, TT, HALF]), s.sb("low", [P, TT, HALF])
        load, chain, acted = s.sem("load"), s.sem("chain"), s.sem("acted")
        with s.block() as block:
            @block.sync
            def _(sp):
                with nc.allow_non_contiguous_dma(reason="one position per partition"):
                    sp.dma_start(posi[:], positions.rearrange("a (t p) -> p (a t)", p=P)).then_inc(load, 16)

            @block.vector
            def _(dve):
                ch = Chain(dve, chain)
                for i in range(HALF):
                    last = nc.vector.memset(freq[:, i:i + 1], THETA ** (-i / HALF))
                dve.wait_ge(load, 16)
                ch.link(nc.vector.tensor_copy(pos[:], posi[:]))
                ch.link(nc.vector.tensor_tensor(ang[:], pos[:].unsqueeze(2).broadcast_to([P, TT, HALF]),
                                                freq[:].unsqueeze(1).broadcast_to([P, TT, HALF]), ALU.mult))
                for out, quarter in ((sin, 0.0), (cos, 0.25)):
                    ch.link(nc.vector.tensor_scalar(turns[:], ang[:], 1.0 / TWO_PI, quarter, ALU.mult, ALU.add))
                    ch.link(nc.vector.tensor_scalar(turns[:], turns[:], MAGIC, None, ALU.add))
                    ch.link(nc.vector.tensor_scalar(turns[:], turns[:], MAGIC, None, ALU.subtract))
                    src = ang
                    for part in parts_of(TWO_PI, 9, 3):
                        ch.link(nc.vector.scalar_tensor_tensor(low[:], turns[:], -part, src[:], ALU.mult, ALU.add))
                        src = low
                    ch.link(nc.vector.tensor_scalar(low[:], low[:], quarter * TWO_PI, EDGE, ALU.add, ALU.min))
                    ch.link(nc.vector.tensor_scalar(out[:], low[:], -EDGE, None, ALU.max))

            @block.scalar
            def _(act):
                act.wait_ge(chain, 2 + 8)
                nc.scalar.activation(sin[:], sin[:], ACT.Sin).then_inc(acted, 1)
                act.wait_ge(chain, 2 + 16)
                nc.scalar.activation(cos[:], cos[:], ACT.Sin).then_inc(acted, 1)
                act.wait_ge(acted, 2)


def mla_project(nc, c, name, hT, w_kv_a, kv_norm_g, w_uk, w_uv, w_qa, q_norm_g, w_qb, cos, sin, q, k, v):
    KV = KV_RANK + ROPE
    with Stage(nc, name) as s:
        wkv, wqa = s.sb("wkv", [P, KC, KV]), s.sb("wqa", [P, KC, Q_RANK])
        wuk, wuv = s.sb("wuk", [P, KV_RANK // P, D]), s.sb("wuv", [P, KV_RANK // P, D])
        wqb = s.sb("wqb", [P, Q_RANK // P, MLA_HEADS * QK])
        gkv, gq = s.sb("gkv", [P, KV_RANK]), s.sb("gq", [P, Q_RANK])
        kv, qa = s.sb("kv", [P, TT, KV]), s.sb("qa", [P, TT, Q_RANK])
        sq = s.sb("sq", [P, TT, Q_RANK])
        ss, sr, eps = s.sb("ss", [P, TT]), s.sb("sr", [P, TT]), s.sb("eps", [P, 1])
        kvT, qaT = s.sb("kvT", [P, KV_RANK // P, SEQ]), s.sb("qaT", [P, Q_RANK // P, SEQ])
        kr = s.sb("kr", [P, TT, ROPE])
        tmp = [sq[:, :, 0:MLA_HEADS * HALF].rearrange("p t (h d) -> p t h d", d=HALF), s.sb("tmp", [P, TT, MLA_HEADS, HALF])[:]]
        bank = [s.ps(f"bank{i}", [P, BANK]) for i in range(4)]
        load = [s.sem(f"load{i}") for i in range(4)]
        made, taken, chain, rooted = s.sem("made"), s.sem("taken"), s.sem("chain"), s.sem("rooted")
        kvready, qaready = s.sem("kvready"), s.sem("qaready")
        rows = lambda w: w.rearrange("(k p) n -> p k n", p=P)
        with s.block() as block:
            @block.sync
            def _(sp):
                sp.dma_start(wkv[:], rows(w_kv_a)).then_inc(load[0], 16)
                sp.dma_start(wqa[:], rows(w_qa)).then_inc(load[1], 16)
                sp.dma_start(gkv[:], kv_norm_g.unsqueeze(0).broadcast_to([P, KV_RANK])).then_inc(load[2], 16)
                sp.dma_start(gq[:], q_norm_g.broadcast_to([P, Q_RANK])).then_inc(load[2], 16)
                sp.dma_start(wuk[:], rows(w_uk)).then_inc(load[3], 16)
                sp.dma_start(wuv[:], rows(w_uv)).then_inc(load[3], 16)
                sp.dma_start(wqb[:], rows(w_qb)).then_inc(load[3], 16)

            NT = (KV_RANK + Q_RANK) // P
            up = [("k", b) for b in range(2)] + [("v", b) for b in range(2)] + [("q", b) for b in range(3)]

            @block.tensor
            def _(pe):
                n = 0

                def slot():
                    if n >= 4:
                        pe.wait_ge(taken, n - 3)
                    return bank[n % 4]

                for w, width, sem in ((wkv, KV, load[0]), (wqa, Q_RANK, load[1])):
                    pe.wait_ge(sem, 16)
                    for t in range(TT):
                        out = slot()
                        for kc in range(KC):
                            last = nc.tensor.matmul(out[:, 0:width], hT[:, kc, t * P:(t + 1) * P], w[:, kc, :],
                                                    start=(kc == 0), stop=(kc == KC - 1))
                        last.then_inc(made, 1)
                        n += 1
                for src, chunks, ready in ((kv, KV_RANK // P, kvready), (qa, Q_RANK // P, qaready)):
                    pe.wait_ge(ready, 1)
                    for kc in range(chunks):
                        out = slot()
                        for t in range(TT):
                            last = nc.tensor.transpose(out[:, t * P:(t + 1) * P], src[:, t, kc * P:(kc + 1) * P], c["ident"][:])
                        last.then_inc(made, 1)
                        n += 1
                pe.wait_ge(load[3], 48)
                pe.wait_ge(taken, n)
                for t in range(TT):
                    for what, b in up:
                        srcT, w = {"k": (kvT, wuk), "v": (kvT, wuv), "q": (qaT, wqb)}[what]
                        chunks = srcT.shape[1]
                        out = slot()
                        for kc in range(chunks):
                            last = nc.tensor.matmul(out[:], srcT[:, kc, t * P:(t + 1) * P], w[:, kc, b * BANK:(b + 1) * BANK],
                                                    start=(kc == 0), stop=(kc == chunks - 1))
                        last.then_inc(made, 1)
                        n += 1

            @block.scalar
            def _(act):
                n = 0
                for dst, width in ((kv, KV), (qa, Q_RANK)):
                    for t in range(TT):
                        act.wait_ge(made, n + 1)
                        nc.scalar.copy(dst[:, t, :], bank[n % 4][:, 0:width]).then_inc(taken, 1)
                        n += 1
                for done in (3, 8):
                    act.wait_ge(chain, done)
                    width = KV_RANK if done == 3 else Q_RANK
                    nc.scalar.activation(sr[:], ss[:], ACT.Sqrt, bias=eps[:], scale=1.0 / width).then_inc(rooted, 1)
                for dstT in (kvT, qaT):
                    for kc in range(dstT.shape[1]):
                        act.wait_ge(made, n + 1)
                        nc.scalar.copy(dstT[:, kc, :], bank[n % 4][:]).then_inc(taken, 1)
                        n += 1
                for t in range(TT):
                    for what, b in up:
                        act.wait_ge(made, n + 1)
                        if what == "k":
                            dst = k[:, t, 8 * b:8 * b + 8, 0:NOPE]
                            src = bank[n % 4][:].rearrange("p (h d) -> p h d", d=NOPE)
                        else:
                            flat = v[:, t, :] if what == "v" else q[:, t].rearrange("p h d -> p (h d)")
                            dst, src = flat[:, b * BANK:(b + 1) * BANK], bank[n % 4][:]
                        nc.scalar.copy(dst, src).then_inc(taken, 1)
                        n += 1

            @block.vector
            def _(dve):
                ch = Chain(dve, chain)
                ch.link(nc.vector.memset(eps[:], RMS_EPS))
                n = 0
                for at, (m, width, g, ready) in enumerate(((kv, KV_RANK, gkv, kvready), (qa, Q_RANK, gq, qaready))):
                    x = m[:, :, 0:width]
                    dve.wait_ge(taken, TT * (at + 1))
                    ch.link(nc.vector.tensor_tensor(sq[:, :, 0:width], x, x, ALU.mult))
                    ch.link(nc.vector.tensor_reduce(ss[:], sq[:, :, 0:width], axis=AX.X, op=ALU.add))
                    dve.wait_ge(rooted, at + 1)
                    ch.link(nc.vector.reciprocal(sr[:], sr[:]))
                    ch.link(nc.vector.tensor_tensor(x, x, sr[:].unsqueeze(2).broadcast_to([P, TT, width]), ALU.mult))
                    dve.wait_ge(load[2], 32)
                    last = nc.vector.tensor_tensor(x, x, g[:].unsqueeze(1).broadcast_to([P, TT, width]), ALU.mult)
                    last.then_inc(ready, 1)
                    if at == 0:
                        ch.link(nc.vector.memset(ss[:, 0:1], 0.0))

                def rotate(out, x, heads):
                    cs = cos[:].unsqueeze(2).broadcast_to([P, TT, heads, HALF])
                    sn = sin[:].unsqueeze(2).broadcast_to([P, TT, heads, HALF])
                    x1, x2 = x[:, :, :, 0:HALF], x[:, :, :, HALF:ROPE]
                    a, b = tmp[0][:, :, 0:heads, :], tmp[1][:, :, 0:heads, :]
                    nc.vector.tensor_tensor(a, x2, sn, ALU.mult)
                    ch.link(nc.vector.tensor_tensor(b, x1, sn, ALU.mult))
                    nc.vector.tensor_tensor(out[:, :, :, 0:HALF], x1, cs, ALU.mult)
                    ch.link(nc.vector.tensor_tensor(out[:, :, :, HALF:ROPE], x2, cs, ALU.mult))
                    nc.vector.tensor_tensor(out[:, :, :, 0:HALF], out[:, :, :, 0:HALF], a, ALU.subtract)
                    ch.link(nc.vector.tensor_tensor(out[:, :, :, HALF:ROPE], out[:, :, :, HALF:ROPE], b, ALU.add))

                rotate(kr[:].unsqueeze(2), kv[:, :, KV_RANK:].unsqueeze(2), 1)
                ch.link(nc.vector.tensor_copy(k[:, :, :, NOPE:], kr[:].unsqueeze(2).broadcast_to([P, TT, MLA_HEADS, ROPE])))
                dve.wait_ge(taken, 2 * TT + NT + TT * len(up))
                rotate(q[:, :, :, NOPE:], q[:, :, :, NOPE:], MLA_HEADS)


def mla_attend(nc, c, name, q, k, v, o):
    G = 2
    SCALE = QK ** -0.5
    PE_STEPS = Steps("qT kT s3 s0 s2 s1 p3 p02 p1 o", G)
    ACT_STEPS = Steps("qs ks qT e3 e0 e2 e1 p3", G)
    DVE_STEPS = Steps("kT x3 x0 x2 x1 nb p02 p1 rr o", G)
    with Stage(nc, name) as s:
        far = s.sb("far", [P, P])
        qs, ks = ([s.sb(f"{n}{j}", [P, TT, QK]) for j in range(G)] for n in ("qs", "ks"))
        qT, kT = ([s.sb(f"{n}{j}", [P, SEQ]) for j in range(G)] for n in ("qT", "kT"))
        prob = [[s.sb(f"prob{j}_{i}", [P, (i + 1) * P]) for i in range(TT)] for j in range(G)]
        probT = [[s.sb(f"probT{j}_{i}", [P, i + 1, P]) for i in range(TT)] for j in range(G)]
        mx, nb, rs = ([s.sb(f"{n}{j}", [P, TT]) for j in range(G)] for n in ("mx", "nb", "rs"))
        A, B, Cb, E = ([s.ps(f"{n}{j}", [P, BANK]) for j in range(G)] for n in ("A", "B", "C", "E"))
        pe_done, act_done, dve_done, masked = s.sem("pe_done"), s.sem("act_done"), s.sem("dve_done"), s.sem("masked")
        spot = {3: (A, 0), 0: (B, 0), 2: (B, P), 1: (Cb, 0)}

        def score(i, j):
            m, at = spot[i]
            return m[j][:, at:at + (i + 1) * P]

        with s.block() as block:
            @block.tensor
            def _(pe):
                pe.wait_ge(masked, 1)
                starts_at_one(pe, pe_done)
                with pe.Fori(0, MLA_HEADS // G) as r:
                    def act_at(step, j):
                        pe.wait_ge(act_done, ACT_STEPS.after(r, step, j))

                    def dve_at(step, j):
                        pe.wait_ge(dve_done, DVE_STEPS.after(r, step, j))

                    for src, dst, step in ((qs, E, "qs"), (ks, A, "ks")):
                        for j in range(G):
                            act_at(step, j)
                            for t in range(TT):
                                last = nc.tensor.transpose(dst[j][0:QK, t * P:(t + 1) * P], src[j][:, t, :], c["ident"][:])
                            last.then_inc(pe_done, 1)
                    for i in (3, 0, 2, 1):
                        for j in range(G):
                            if i == 3:
                                act_at("qT", j)
                                dve_at("kT", j)
                            sc = score(i, j)
                            nc.tensor.matmul(sc, qT[j][0:QK, i * P:(i + 1) * P], kT[j][0:QK, 0:(i + 1) * P], start=True, stop=False)
                            nc.tensor.matmul(sc[:, i * P:], c["ident"][:], far[:], start=False, stop=True).then_inc(pe_done, 1)
                    for step, dst, tiles, ready in (("p3", A, (3,), "e3"), ("p02", B, (0, 2), "e2"), ("p1", E, (1,), "e1")):
                        for j in range(G):
                            act_at(ready, j)
                            col = 0
                            for i in tiles:
                                for kt in range(i + 1):
                                    last = nc.tensor.transpose(dst[j][:, col:col + P], prob[j][i][:, kt * P:(kt + 1) * P], c["ident"][:])
                                    col += P
                            last.then_inc(pe_done, 1)
                    for j in range(G):
                        act_at("p3", j)
                        dve_at("p1", j)
                        for i in range(TT):
                            for kt in range(i + 1):
                                last = nc.tensor.matmul(Cb[j][:, 256 + i * VDIM:256 + (i + 1) * VDIM], probT[j][i][:, kt, :],
                                                        v[:, kt, bass.ds((r * G + j) * VDIM, VDIM)], start=(kt == 0), stop=(kt == i))
                        last.then_inc(pe_done, 1)

            @block.scalar
            def _(act):
                starts_at_one(act, act_done)
                with act.Fori(0, MLA_HEADS // G) as r:
                    def pe_at(step, j):
                        act.wait_ge(pe_done, PE_STEPS.after(r, step, j))

                    for dst, src in ((qs, q), (ks, k)):
                        for j in range(G):
                            act.wait_ge(pe_done, PE_STEPS.rounds(r))
                            nc.scalar.copy(dst[j][:].unsqueeze(2), src[:, :, bass.ds(r * G + j, 1), :]).then_inc(act_done, 1)
                    for j in range(G):
                        pe_at("qT", j)
                        nc.scalar.copy(qT[j][0:QK, :], E[j][0:QK, :]).then_inc(act_done, 1)
                    for i in (3, 0, 2, 1):
                        for j in range(G):
                            if i == 3:
                                act.wait_ge(dve_done, DVE_STEPS.after(r, "nb", j))
                            nc.scalar.activation(prob[j][i][:], score(i, j), ACT.Exp, bias=nb[j][:, i:i + 1], scale=SCALE,
                                                 accum_out=rs[j][:, i:i + 1]).then_inc(act_done, 1)
                    for j in range(G):
                        pe_at("p3", j)
                        nc.scalar.copy(probT[j][3][:].rearrange("p k q -> p (k q)"), A[j][:]).then_inc(act_done, 1)

            @block.vector
            def _(dve):
                nc.vector.tensor_scalar(far[:], c["lower"][:], -1.0, 1.0e30, ALU.add, ALU.mult).then_inc(masked, 1)
                starts_at_one(dve, dve_done)
                with dve.Fori(0, MLA_HEADS // G) as r:
                    def pe_at(step, j):
                        dve.wait_ge(pe_done, PE_STEPS.after(r, step, j))

                    for j in range(G):
                        pe_at("kT", j)
                        nc.vector.tensor_copy(kT[j][0:QK, :], A[j][0:QK, :]).then_inc(dve_done, 1)
                    for i in (3, 0, 2, 1):
                        for j in range(G):
                            pe_at("s2" if i == 0 else f"s{i}", j)
                            nc.vector.tensor_reduce(mx[j][:, i:i + 1], score(i, j), axis=AX.X, op=ALU.max).then_inc(dve_done, 1)
                    for j in range(G):
                        dve.wait_ge(dve_done, DVE_STEPS.after(r, "x1", j))
                        nc.vector.tensor_scalar(nb[j][:], mx[j][:], -SCALE, None, ALU.mult).then_inc(dve_done, 1)
                    for j in range(G):
                        pe_at("p02", j)
                        nc.vector.tensor_copy(probT[j][0][:, 0, :], B[j][:, 0:P])
                        nc.vector.tensor_copy(probT[j][2][:].rearrange("p k q -> p (k q)"), B[j][:, P:]).then_inc(dve_done, 1)
                    for j in range(G):
                        pe_at("p1", j)
                        nc.vector.tensor_copy(probT[j][1][:].rearrange("p k q -> p (k q)"), E[j][:, 0:2 * P]).then_inc(dve_done, 1)
                    for j in range(G):
                        dve.wait_ge(act_done, ACT_STEPS.after(r, "e1", j))
                        nc.vector.reciprocal(rs[j][:], rs[j][:]).then_inc(dve_done, 1)
                    for j in range(G):
                        pe_at("o", j)
                        dve.wait_ge(dve_done, DVE_STEPS.after(r, "rr", j))
                        nc.vector.tensor_tensor(o[:, :, bass.ds((r * G + j) * VDIM, VDIM)],
                                                Cb[j][:, 256:].rearrange("p (t d) -> p t d", d=VDIM),
                                                rs[j][:].unsqueeze(2).broadcast_to([P, TT, VDIM]), ALU.mult).then_inc(dve_done, 1)
                dve.wait_ge(dve_done, DVE_STEPS.rounds(MLA_HEADS // G))


def mla_layer(nc, c, h, hT, positions, w_kv_a, kv_norm_g, w_uk, w_uv, w_qa, q_norm_g, w_qb, w_out):
    with Stage(nc, "mla") as s:
        v = s.sb("v", [P, TT, MLA_HEADS * VDIM])
        o = s.sb("o", [P, TT, MLA_HEADS * VDIM])
        with Stage(nc, "mla_in") as s1:
            q, k = (s1.sb(n, [P, TT, MLA_HEADS, QK]) for n in ("q", "k"))
            cos, sin = (s1.sb(n, [P, TT, HALF]) for n in ("cos", "sin"))
            rope_tables(nc, c, "mlar", positions, cos, sin)
            mla_project(nc, c, "mlap", hT, w_kv_a, kv_norm_g, w_uk, w_uv, w_qa, q_norm_g, w_qb, cos, sin, q, k, v)
            mla_attend(nc, c, "mlaa", q, k, v, o)
        with Stage(nc, "mla_out") as s1:
            oT = s1.sb("oT", [P, KC, SEQ])
            transpose_tokens(nc, c, o, oT)
            project_out(nc, c, "mlaq", oT, w_out, h)


def peer_layer(nc, c, name, h, hT, w_q, sub_keys, u_tab, v_tab, gates):
    with Stage(nc, f"{name}k") as s:
        giT = s.sb("giT", [P, 3, SEQ])
        peer_select(nc, c, f"{name}s", hT, w_q, sub_keys, giT)
        peer_gates(nc, c, f"{name}g", giT, gates)
    with Stage(nc, f"{name}a") as s:
        scaled = s.sem("scaled")
        with s.block() as block:
            @block.vector
            def _(dve):
                nc.vector.tensor_scalar(h[:], h[:], ALPHA, None, ALU.mult).then_inc(scaled, 1)
                dve.wait_ge(scaled, 1)
    peer_experts(nc, c, f"{name}e", hT, h, u_tab, v_tab, gates)


def yoco_trunk(nc, x, positions, a_w_in, a_conv_w, a_a_log, a_dt_bias, a_norm_g, a_w_out, kv_w_a, kv_norm_g, kv_w_uk,
               kv_w_uv, b_w_qa, b_q_norm_g, b_w_qb, b_w_out, peer_w_q, peer_sub_keys, peer_u, peer_v, ln_g, ln_b, out):
    gates = nc.dram_tensor("gates", [P, NKEYS, SEQ], F32).ap()
    tokens = lambda ap: ap.rearrange("a (t p) d -> p (a t) d", p=P)
    with Stage(nc, "trunk") as s:
        c = {n: s.sb(n, [P, P]) for n in ("ident", "ones", "upper", "lower", "strict", "block16", "iota")}
        h = s.sb("h", [P, TT, D])
        load, stored = s.sem("load"), s.sem("stored")
        make_constants(nc, c)
        with s.block() as block:
            @block.sync
            def _(sp):
                sp.dma_start(h[:], tokens(x)).then_inc(load, 16)
                sp.wait_ge(load, 16)
        gdn_layer(nc, c, h, a_w_in[0], a_conv_w[0], a_a_log, a_dt_bias, a_norm_g, a_w_out[0])
        normalize(nc, c, "ln00", h, ln_g[0, 0:1], ln_b[0, 0:1])
        with Stage(nc, "peer0") as s0:
            hT = s0.sb("hT", [P, KC, SEQ])
            transpose_tokens(nc, c, h, hT)
            peer_layer(nc, c, "p0", h, hT, peer_w_q[0], peer_sub_keys[0], peer_u[0], peer_v[0], gates)
        normalize(nc, c, "ln01", h, ln_g[0, 1:2], ln_b[0, 1:2])
        with Stage(nc, "cross") as s0:
            hT = s0.sb("hT", [P, KC, SEQ])
            transpose_tokens(nc, c, h, hT)
            mla_layer(nc, c, h, hT, positions, kv_w_a, kv_norm_g, kv_w_uk, kv_w_uv, b_w_qa[0], b_q_norm_g, b_w_qb[0], b_w_out[0])
            normalize(nc, c, "ln10", h, ln_g[1, 0:1], ln_b[1, 0:1])
            transpose_tokens(nc, c, h, hT)
            peer_layer(nc, c, "p1", h, hT, peer_w_q[1], peer_sub_keys[1], peer_u[1], peer_v[1], gates)
        normalize(nc, c, "ln11", h, ln_g[1, 1:2], ln_b[1, 1:2])
        with s.block() as block:
            @block.sync
            def _(sp):
                sp.dma_start(tokens(out), h[:]).then_inc(stored, 16)
                sp.wait_ge(stored, 16)


_INS = ["x", "positions", "a_w_in", "a_conv_w", "a_a_log", "a_dt_bias", "a_norm_g", "a_w_out", "kv_w_a", "kv_norm_g",
        "kv_w_uk", "kv_w_uv", "b_w_qa", "b_q_norm_g", "b_w_qb", "b_w_out", "peer_w_q", "peer_sub_keys", "peer_u",
        "peer_v", "ln_g", "ln_b"]


def kernel(**inputs):
    import numpy as _np
    import concourse.bacc as _bacc
    from concourse import mybir as _mybir
    from concourse.bass_utils import run_bass_kernel_spmd as _run

    nc = _bacc.Bacc("TRN2", target_bir_lowering=False, num_devices=1)
    arrays, args = {}, []
    for name in _INS:
        a = _np.ascontiguousarray(inputs[name])
        arrays[f"in_{name}_dram"] = a
        args.append(nc.dram_tensor(f"in_{name}_dram", a.shape, _mybir.dt.from_np(a.dtype), kind="ExternalInput").ap())
    args.append(nc.dram_tensor("out_dram", (1, SEQ, D), _mybir.dt.float32, kind="ExternalOutput").ap())
    yoco_trunk(nc, *args)
    r = _run(nc, [arrays], core_ids=[0])
    return r.results[0]["out_dram"]
```

```python
import math
from contextlib import ExitStack

import concourse.bass as bass
import concourse.mybir as mybir

F32 = mybir.dt.float32
F32R = mybir.dt.float32r
U32 = mybir.dt.uint32
I32 = mybir.dt.int32
ALU = mybir.AluOpType
ACT = mybir.ActivationFunctionType
AX = mybir.AxisListType

P = 128
SEQ = 512
TT = SEQ // P
D = 1024
KC = D // P
BANK = 512
HALVES = D // BANK
DEPTH = 2
ALPHA = (2 * DEPTH) ** 0.25
LN_EPS = 1e-5
RMS_EPS = 1e-6

HEADS = 8
NKEYS = 128
TOPK = 16
SETS = 2 * HEADS
NEG = -3.0e38
EARLY_TILE = 6
EARLY_SELECT = TT * EARLY_TILE
GRID = 64
GRIDS = SEQ // GRID
EARLY = EARLY_SELECT + GRIDS


class Chain:

    def __init__(self, eng, sem, before=0, alone=None):
        self.eng, self.sem, self.before, self.count, self.alone = eng, sem, before, 0, alone

    def link(self, ins):
        self.count += 1
        ins.then_inc(self.sem, 1)
        self.eng.wait_ge(self.sem, self.before + self.count)
        if self.alone is not None:
            self.eng.sem_inc(self.alone, 1)

    def end(self, count):
        assert self.count == count, self.count


def starts_at_one(eng, *sems):
    for sem in sems:
        eng.sem_inc(sem, 1)


class Stage:

    def __init__(self, nc, name):
        self.nc, self.name, self.ctx, self.sems = nc, name, ExitStack(), []

    def __enter__(self):
        self.ctx.__enter__()
        return self

    def __exit__(self, *e):
        if self.sems:
            self.nc.clear_and_free_semaphores(self.sems)
            self.nc.all_engine_barrier()
        return self.ctx.__exit__(*e)

    def sb(self, name, shape, dt=F32):
        return self.ctx.enter_context(self.nc.sbuf_tensor(f"{self.name}_{name}", shape, dt))

    def ps(self, name, shape, dt=F32):
        return self.ctx.enter_context(self.nc.psum_tensor(f"{self.name}_{name}", shape, dt))

    def sem(self, name):
        self.sems.append(self.nc.alloc_semaphore(name=f"{self.name}_{name}"))
        return self.sems[-1]

    def block(self):
        return self.nc.Block()


def make_constants(nc, c):
    with Stage(nc, "const") as s:
        zeroed, made, itoa, copied = s.sem("zeroed"), s.sem("made"), s.sem("iota"), s.sem("copied")
        iota_i = s.sb("iota_i", [P, P], I32)
        with s.block() as block:
            @block.gpsimd
            def _(pool):
                nc.gpsimd.memset(c["ident"][:], 0.0).then_inc(zeroed, 1)
                nc.gpsimd.memset(c["ones"][:], 1.0).then_inc(zeroed, 1)
                nc.gpsimd.iota(iota_i[:], pattern=[[1, P]], base=0, channel_multiplier=0).then_inc(itoa, 1)
                pool.wait_ge(zeroed, 2)
                nc.gpsimd.affine_select(out=c["ident"][:], in_=c["ident"][:], compare_op=ALU.not_equal, fill=1.0,
                                        base=0, pattern=[[-1, P]], channel_multiplier=1).then_inc(made, 1)
                nc.gpsimd.affine_select(out=c["upper"][:], in_=c["ones"][:], compare_op=ALU.is_ge, fill=0.0,
                                        base=0, pattern=[[1, P]], channel_multiplier=-1).then_inc(made, 1)
                nc.gpsimd.affine_select(out=c["lower"][:], in_=c["ones"][:], compare_op=ALU.is_ge, fill=0.0,
                                        base=0, pattern=[[-1, P]], channel_multiplier=1).then_inc(made, 1)
                nc.gpsimd.affine_select(out=c["strict"][:], in_=c["ones"][:], compare_op=ALU.is_gt, fill=0.0,
                                        base=0, pattern=[[-1, P]], channel_multiplier=1).then_inc(made, 1)
                nc.gpsimd.affine_select(out=c["block16"][:].rearrange("p (b j) -> p b j", j=16),
                                        in_=c["ones"][:].rearrange("p (b j) -> p b j", j=16),
                                        compare_op=ALU.is_ge, fill=0.0,
                                        base=0, pattern=[[-16, P // 16], [0, 16]], channel_multiplier=1).then_inc(made, 1)
                pool.wait_ge(made, 5)
                nc.gpsimd.affine_select(out=c["block16"][:].rearrange("p (b j) -> p b j", j=16),
                                        in_=c["block16"][:].rearrange("p (b j) -> p b j", j=16),
                                        compare_op=ALU.is_ge, fill=0.0,
                                        base=15, pattern=[[16, P // 16], [0, 16]], channel_multiplier=-1).then_inc(made, 1)

            @block.vector
            def _(dve):
                dve.wait_ge(itoa, 1)
                nc.vector.tensor_copy(c["iota"][:], iota_i[:]).then_inc(copied, 1)
                dve.wait_ge(made, 6)
                dve.wait_ge(copied, 1)


def transpose_tokens(nc, c, h, hT):
    with Stage(nc, f"t{nc.next_id()}") as s:
        flipped, taken = s.sem("flipped"), s.sem("taken")
        bank = [s.ps(f"bank{i}", [P, BANK]) for i in range(2)]
        with s.block() as block:
            @block.tensor
            def _(pe):
                for k in range(KC):
                    if k >= 2:
                        pe.wait_ge(taken, k - 1)
                    for t in range(TT):
                        last = nc.tensor.transpose(bank[k % 2][:, t * P:(t + 1) * P], h[:, t, k * P:(k + 1) * P],
                                                   c["ident"][:])
                    last.then_inc(flipped, 1)

            @block.vector
            def _(dve):
                for k in range(KC):
                    dve.wait_ge(flipped, k + 1)
                    nc.vector.tensor_copy(hT[:, k, :], bank[k % 2][:]).then_inc(taken, 1)
                dve.wait_ge(taken, KC)


def transpose_tokens_split(nc, c, h, hTh, hTl):
    with Stage(nc, f"t{nc.next_id()}") as s:
        flipped, high, low = s.sem("flipped"), s.sem("high"), s.sem("low")
        bank = [s.ps(f"bank{i}", [P, BANK]) for i in range(4)]
        with s.block() as block:
            @block.tensor
            def _(pe):
                for k in range(KC):
                    if k >= 4:
                        pe.wait_ge(low, k - 3)
                    for t in range(TT):
                        last = nc.tensor.transpose(bank[k % 4][:, t * P:(t + 1) * P], h[:, t, k * P:(k + 1) * P],
                                                   c["ident"][:])
                    last.then_inc(flipped, 1)

            @block.scalar
            def _(act):
                for k in range(KC):
                    act.wait_ge(flipped, k + 1)
                    nc.scalar.copy(hTh[:, k, :], bank[k % 4][:]).then_inc(high, 1)

            @block.vector
            def _(dve):
                for k in range(KC):
                    dve.wait_ge(high, k + 1)
                    nc.vector.tensor_tensor(hTl[:, k, :], bank[k % 4][:], hTh[:, k, :].bitcast(F32), ALU.subtract).then_inc(low, 1)
                dve.wait_ge(low, KC)


SLAB = 256
SLAB_TILES = SLAB // P


class Slabs:

    def __init__(self, nc, s, view, used):
        self.nc, self.view, self.used = nc, view, used
        self.raw = [s.sb(f"raw{i}", [P, KC, SLAB]) for i in range(2)]
        self.high = [s.sb(f"high{i}", [P, KC, SLAB], F32R) for i in range(2)]
        self.low = [s.sb(f"low{i}", [P, KC, SLAB], F32R) for i in range(2)]
        self.loaded = [s.sem("loaded0"), s.sem("loaded1")]
        self.high_ready, self.low_ready = s.sem("high_ready"), s.sem("low_ready")

    def load(self, sp, base, n):
        sp.wait_ge(self.low_ready, base + n + 1)
        at = base + n
        src = self.view[at] if isinstance(at, int) else self.view[bass.ds(at, 1)]
        sp.dma_start(self.raw[n % 2][:], src).then_inc(self.loaded[n % 2], 16)

    def split_high(self, act, base, n, half_base):
        act.wait_ge(self.loaded[n % 2], 16 * (half_base + n // 2 + 1))
        act.wait_ge(self.used, (base + n) * SLAB_TILES + SLAB_TILES)
        flat = lambda ap: ap.rearrange("p k n -> p (k n)")
        self.nc.scalar.copy(flat(self.high[n % 2][:]), flat(self.raw[n % 2][:])).then_inc(self.high_ready, 1)

    def split_low(self, pool, base, n):
        pool.wait_ge(self.high_ready, base + n + 1)
        flat = lambda ap: ap.rearrange("p k n -> p (k n)")
        self.nc.gpsimd.tensor_tensor(flat(self.low[n % 2][:]), flat(self.raw[n % 2][:]), flat(self.high[n % 2][:]).bitcast(F32),
                                     ALU.subtract).then_inc(self.low_ready, 1)

    def wait(self, pe, base, n):
        pe.wait_ge(self.low_ready, base + n + 3)

    def columns(self, nc, out, n, tile, xTh, xTl):
        at = slice(tile * P, (tile + 1) * P)
        for k in range(KC):
            for m, (w, x) in enumerate(((self.high, xTh), (self.high, xTl), (self.low, xTh))):
                last = nc.tensor.matmul(out, w[n % 2][:, k, at], x[:, k, :], start=(k == 0 and m == 0), stop=(k == KC - 1 and m == 2))
        return last

    def tokens(self, nc, out, n, t, xTh, xTl):
        at = slice(t * P, (t + 1) * P)
        for k in range(KC):
            for m, (x, w) in enumerate(((xTh, self.high), (xTh, self.low), (xTl, self.high))):
                last = nc.tensor.matmul(out, x[:, k, at], w[n % 2][:, k, :], start=(k == 0 and m == 0), stop=(k == KC - 1 and m == 2))
        return last


def peer_select(nc, c, name, hTh, hTl, w_q, sub_keys, giT, u_tab, early):
    ROUND_SLABS = 4
    ROUNDS = SETS // (ROUND_SLABS * SLAB_TILES)
    with Stage(nc, name) as s:
        keys = s.sb("keys", [P, SETS, P])
        keysT = s.sb("keysT", [P, SETS, P])
        qT = [s.sb(f"qT{i}", [P, SEQ]) for i in range(2)]
        masked = s.sb("masked", [P, TT, NKEYS])
        best = s.sb("best", [P, TT, TOPK])
        besti = s.sb("besti", [P, TT, TOPK], U32)
        val = s.sb("val", [P, SETS, TT, TOPK])
        num = s.sb("num", [P, SETS, TT, TOPK])
        cand = s.sb("cand", [P, HEADS, TOPK * TOPK])
        candm = s.sb("candm", [P, HEADS, TOPK * TOPK])
        top = s.sb("top", [P, HEADS, TOPK])
        topi = s.sb("topi", [P, HEADS, TOPK], U32)
        digit = s.sb("digit", [P, HEADS * TOPK], U32)
        digitf = s.sb("digitf", [P, HEADS * TOPK])
        valt = s.sb("valt", [P, SETS, TOPK])
        numt = s.sb("numt", [P, SETS, TOPK])
        hot = s.sb("hot", [P, HEADS, TOPK * TOPK])
        mass = s.sb("mass", [P, HEADS])
        picks = s.sb("picks", [P, 3, HEADS * TOPK])
        load_k, kflip, ktaken = s.sem("load_k"), s.sem("kflip"), s.sem("ktaken")
        projected, qready, scored, ranked = s.sem("projected"), s.sem("qready"), s.sem("scored"), s.sem("ranked")
        chain, passed = s.sem("chain"), s.sem("passed")
        logits, expd, picked, turned, done = s.sem("logits"), s.sem("expd"), s.sem("picked"), s.sem("turned"), s.sem("done")
        qps = [s.ps(f"qps{i}", [P, SEQ]) for i in range(2)]
        sps = [s.ps(f"sps{i}", [P, TT, NKEYS]) for i in range(2)]
        tps = s.ps("tps", [P, 4, P])
        gps = s.ps("gps", [P, 3, P])
        slabs = Slabs(nc, s, w_q.rearrange("(k p) (s n) -> s p k n", p=P, n=SLAB), projected)
        ROUND1 = ROUND_SLABS * SLAB_TILES
        RING = 2
        u, uT = ([raw[:].rearrange("p k n -> p (k n)")[:, a * D:(a + 1) * D] for a in range(2)] for raw in slabs.raw)
        uTh, uTl = ([part[:, :, 0:P] for part in parts] for parts in (slabs.high, slabs.low))
        hps = qps
        ups = [s.ps(f"ups{i}", [P, BANK]) for i in range(2)]
        gel = [s.sb(f"gel{i}", [P, SEQ]) for i in range(2)]
        load_u = [s.sem(f"load_u{i}") for i in range(RING)]
        kept = [s.sem(f"kept{i}") for i in range(2)]
        u_flip, u_turned, u_high, u_low = (s.sem(n) for n in ("u_flip", "u_turned", "u_high", "u_low"))
        hid, gelued = s.sem("hid"), s.sem("gelued")
        u_v = u_tab.rearrange("(b p) d -> b p d", p=P)
        with s.block() as block:
            @block.sync
            def _(sp):
                with sp.Fori(0, ROUNDS) as i:
                    for n in range(ROUND_SLABS):
                        slabs.load(sp, i * ROUND_SLABS, n)
                sp.wait_ge(slabs.low_ready, ROUNDS * ROUND_SLABS + 2)

                def load(i, b):
                    sp.wait_ge(u_flip, i * (2 * EARLY_TILE) + 2 * b + 2)
                    sp.dma_start(u[b % RING], u_v[bass.ds(i * EARLY_TILE + b, 1)]).then_inc(load_u[b % RING], 16)

                load(0, 0)
                with sp.Fori(0, TT) as i:
                    for b in range(EARLY_TILE):
                        load(i, b + 1)

            @block.gpsimd
            def _(pool):
                pool.sem_inc(slabs.low_ready, 2)
                with pool.Fori(0, ROUNDS) as i:
                    for n in range(ROUND_SLABS):
                        slabs.split_low(pool, i * ROUND_SLABS, n)
                pool.sem_inc(u_low, 2)

                def split_low(i, b):
                    pool.wait_ge(u_high, i * EARLY_TILE + b + 1)
                    pool.wait_ge(hid, i * EARLY_TILE + b + 1)
                    nc.gpsimd.tensor_tensor(uTl[b % 2], uT[b % 2].rearrange("p (k n) -> p k n", n=P),
                                            uTh[b % 2].bitcast(F32), ALU.subtract).then_inc(u_low, 1)

                split_low(0, 0)
                with pool.Fori(0, TT) as i:
                    for b in range(EARLY_TILE):
                        split_low(i, b + 1)

            @block.tensor
            def _(pe):
                pe.sem_inc(projected, 2 * SLAB_TILES)
                pe.sem_inc(u_flip, 2 * RING)
                starts_at_one(pe, turned)
                pe.wait_ge(load_k, 16)
                for q in range(SETS // 4):
                    if q:
                        pe.wait_ge(ktaken, q)
                    for j in range(4):
                        last = nc.tensor.transpose(tps[:, j, :], keys[:, 4 * q + j, :], c["ident"][:])
                    last.then_inc(kflip, 1)
                pe.wait_ge(ktaken, SETS // 4)
                with pe.Fori(0, ROUNDS) as i:
                    def score(n):
                        pe.wait_ge(qready, i * ROUND1 + n + 1)
                        pe.wait_ge(ranked, i * ROUND1 + n + 1)
                        for t in range(TT):
                            last = nc.tensor.matmul(sps[n % 2][:, t, :], qT[n % 2][:, t * P:(t + 1) * P],
                                                    keysT[:, bass.ds(i * ROUND1 + n, 1), :], start=True, stop=True)
                        last.then_inc(scored, 1)

                    for b in range(ROUND_SLABS):
                        slabs.wait(pe, i * ROUND_SLABS, b)
                        for j in range(SLAB_TILES):
                            n = b * SLAB_TILES + j
                            slabs.columns(nc, qps[n % 2][:], b, j, hTh, hTl).then_inc(projected, 1)
                            if n >= 1:
                                score(n - 1)
                    score(ROUND1 - 1)

                def flip_block(i, b):
                    pe.wait_ge(load_u[b % RING], 16 * (i * (EARLY_TILE // RING) + b // RING + 1))
                    pe.wait_ge(u_turned, i * (2 * EARLY_TILE) + 2 * b + 1)
                    for half in range(2):
                        for j in range(4):
                            k = 4 * half + j
                            last = nc.tensor.transpose(ups[half][:, j * P:(j + 1) * P], u[b % RING][:, k * P:(k + 1) * P],
                                                       c["ident"][:])
                        last.then_inc(u_flip, 1)

                pe.sem_inc(hid, 2)
                flip_block(0, 0)
                with pe.Fori(0, TT) as i:
                    for b in range(EARLY_TILE):
                        flip_block(i, b + 1)
                        pe.wait_ge(u_low, i * EARLY_TILE + b + 3)
                        pe.wait_ge(gelued, i * EARLY_TILE + b + 1)
                        for k in range(KC):
                            for n, (w, x) in enumerate(((uTh, hTh), (uTh, hTl), (uTl, hTh))):
                                last = nc.tensor.matmul(hps[b % 2][:], w[b % 2][:, k, :], x[:, k, :],
                                                        start=(k == 0 and n == 0), stop=(k == KC - 1 and n == 2))
                        last.then_inc(hid, 1)
                    pe.wait_ge(picked, i + 1)
                    pe.wait_ge(done, i + 1)
                    for j in range(3):
                        last = nc.tensor.transpose(gps[:, j, :], picks[:, j, :], c["ident"][:])
                    last.then_inc(turned, 1)

            @block.scalar
            def _(act):
                act.dma_start(keys[:], sub_keys.rearrange("h p n d -> n (h p) d")).then_inc(load_k, 16)
                with act.Fori(0, ROUNDS) as i:
                    slabs.split_high(act, i * ROUND_SLABS, 0, i * (ROUND_SLABS // 2))
                    for b in range(ROUND_SLABS):
                        if b + 1 < ROUND_SLABS:
                            slabs.split_high(act, i * ROUND_SLABS, b + 1, i * (ROUND_SLABS // 2))
                        for n in range(b * SLAB_TILES, (b + 1) * SLAB_TILES):
                            act.wait_ge(projected, i * ROUND1 + n + 2 * SLAB_TILES + 1)
                            if n >= 2:
                                act.wait_ge(scored, i * ROUND1 + n - 1)
                            nc.scalar.copy(qT[n % 2][:], qps[n % 2][:]).then_inc(qready, 1)
                act.sem_inc(gelued, 2)
                starts_at_one(act, done, u_turned)
                for b in range(2):
                    act.sem_inc(kept[b], 16)

                def split_u(i, b):
                    for half in range(2):
                        act.wait_ge(u_flip, i * (2 * EARLY_TILE) + 2 * b + half + 2 * RING + 1)
                        if half == 0:
                            act.wait_ge(u_low, i * EARLY_TILE + b + 1)
                        nc.scalar.copy(uT[b % 2][:, half * BANK:(half + 1) * BANK], ups[half][:]).then_inc(u_turned, 1)
                    act.wait_ge(u_turned, i * (2 * EARLY_TILE) + 2 * b + 3)
                    act.wait_ge(hid, i * EARLY_TILE + b + 1)
                    nc.scalar.copy(uTh[b % 2], uT[b % 2].rearrange("p (k n) -> p k n", n=P)).then_inc(u_high, 1)

                split_u(0, 0)
                with act.Fori(0, TT) as i:
                    def keep(b):
                        act.wait_ge(gelued, i * EARLY_TILE + b + 3)
                        act.dma_start(early[bass.ds(i * EARLY_TILE + b, 1)], gel[b % 2][:]).then_inc(kept[b % 2], 16)

                    for b in range(EARLY_TILE):
                        split_u(i, b + 1)
                        if b:
                            keep(b - 1)
                        act.wait_ge(hid, i * EARLY_TILE + b + 3)
                        act.wait_ge(kept[b % 2], 16 * (i * (EARLY_TILE // 2) + b // 2 + 1))
                        nc.scalar.activation(gel[b % 2][:], hps[b % 2][:], ACT.Gelu).then_inc(gelued, 1)
                        if b == EARLY_TILE // 2:
                            act.wait_ge(logits, i + 1)
                            nc.scalar.activation(picks[:, 0, :], picks[:, 0, :], ACT.Exp).then_inc(expd, 1)
                    keep(EARLY_TILE - 1)
                    act.wait_ge(turned, i + 2)
                    nc.scalar.copy(giT[:, :, bass.ds(i * P, P)], gps[:]).then_inc(done, 1)
                for b in range(2):
                    act.wait_ge(kept[b], 16 * (EARLY_SELECT // 2 + 1))
                act.wait_ge(done, TT + 1)

            @block.vector
            def _(dve):
                nc.vector.memset(mass[:], 0.0).then_inc(ranked, 2)
                for q in range(SETS // 4):
                    dve.wait_ge(kflip, q + 1)
                    nc.vector.tensor_copy(keysT[:, 4 * q:4 * q + 4, :], tps[:]).then_inc(ktaken, 1)
                PER_SET = 5
                with dve.Fori(0, ROUNDS) as i:
                    ch = Chain(dve, chain, i * (ROUND1 * PER_SET), passed)
                    for n in range(ROUND1):
                        sc, e = sps[n % 2], i * ROUND1 + n
                        dve.wait_ge(scored, e + 1)
                        dve.sem_inc(passed, 1)
                        for t in range(TT):
                            last = nc.vector.max(best[:, t, 0:8], sc[:, t, :])
                        ch.link(last)
                        for t in range(TT):
                            nc.vector.max_index(besti[:, t, 0:8], best[:, t, 0:8], sc[:, t, :])
                            last = nc.vector.match_replace(masked[:, t, :], best[:, t, 0:8], sc[:, t, :], NEG)
                        ch.link(last)
                        for t in range(TT):
                            last = nc.vector.max(best[:, t, 8:16], masked[:, t, :])
                        ch.link(last)
                        for t in range(TT):
                            last = nc.vector.max_index(besti[:, t, 8:16], best[:, t, 8:16], masked[:, t, :])
                        ch.link(last)
                        ch.link(nc.vector.tensor_copy(val[:, bass.ds(e, 1), :, :], best[:].unsqueeze(1)))
                        nc.vector.tensor_copy(num[:, bass.ds(e, 1), :, :], besti[:].unsqueeze(1)).then_inc(ranked, 1)
                        dve.wait_ge(ranked, e + 3)
                    ch.end(ROUND1 * PER_SET)
                PER_TILE = 18
                with dve.Fori(0, TT) as i:
                    ch = Chain(dve, chain, SETS * PER_SET + i * PER_TILE, passed)
                    nc.vector.tensor_copy(valt[:].unsqueeze(2), val[:, :, bass.ds(i, 1), :])
                    ch.link(nc.vector.tensor_copy(numt[:].unsqueeze(2), num[:, :, bass.ds(i, 1), :]))
                    v4 = valt[:].rearrange("p (h s) k -> p h s k", s=2)
                    n4 = numt[:].rearrange("p (h s) k -> p h s k", s=2)
                    cand4 = cand[:].rearrange("p h (a b) -> p h a b", a=TOPK)
                    hot4 = hot[:].rearrange("p h (a b) -> p h a b", a=TOPK)
                    for hh in range(HEADS):
                        last = nc.vector.tensor_tensor(cand4[:, hh],
                                                       v4[:, hh, 0].unsqueeze(2).broadcast_to([P, TOPK, TOPK]),
                                                       v4[:, hh, 1].unsqueeze(1).broadcast_to([P, TOPK, TOPK]), ALU.add)
                    ch.link(last)
                    for hh in range(HEADS):
                        last = nc.vector.max(top[:, hh, 0:8], cand[:, hh, :])
                    ch.link(last)
                    for hh in range(HEADS):
                        nc.vector.max_index(topi[:, hh, 0:8], top[:, hh, 0:8], cand[:, hh, :])
                        last = nc.vector.match_replace(candm[:, hh, :], top[:, hh, 0:8], cand[:, hh, :], NEG)
                    ch.link(last)
                    for hh in range(HEADS):
                        last = nc.vector.max(top[:, hh, 8:16], candm[:, hh, :])
                    ch.link(last)
                    for hh in range(HEADS):
                        last = nc.vector.max_index(topi[:, hh, 8:16], top[:, hh, 8:16], candm[:, hh, :])
                    ch.link(last)
                    g3 = picks[:, 0, :].rearrange("p (h k) -> p h k", k=TOPK)
                    dve.wait_ge(turned, i + 1)
                    last = nc.vector.tensor_tensor(g3, top[:], top[:, :, 0:1].broadcast_to([P, HEADS, TOPK]), ALU.subtract)
                    last.then_inc(logits, 1)
                    for side, (op, k) in enumerate(((ALU.logical_shift_right, 4), (ALU.bitwise_and, 15))):
                        ch.link(nc.vector.tensor_scalar(digit[:], topi[:].rearrange("p h k -> p (h k)"), k, None, op))
                        ch.link(nc.vector.tensor_copy(digitf[:], digit[:]))
                        ch.link(nc.vector.tensor_tensor(hot[:].rearrange("p h (k a) -> p (h k) a", a=TOPK),
                                                        digitf[:].unsqueeze(2).broadcast_to([P, HEADS * TOPK, TOPK]),
                                                        c["iota"][:, 0:TOPK].unsqueeze(1).broadcast_to([P, HEADS * TOPK, TOPK]),
                                                        ALU.is_equal))
                        for hh in range(HEADS):
                            last = nc.vector.tensor_tensor(hot4[:, hh], hot4[:, hh],
                                                           n4[:, hh, side].unsqueeze(1).broadcast_to([P, TOPK, TOPK]), ALU.mult)
                        ch.link(last)
                        ch.link(nc.vector.tensor_reduce(picks[:, 1 + side, :], hot[:].rearrange("p h (k a) -> p (h k) a", a=TOPK),
                                                        axis=AX.X, op=ALU.add))
                    dve.wait_ge(expd, i + 1)
                    ch.link(nc.vector.tensor_reduce(mass[:], g3, axis=AX.X, op=ALU.add))
                    ch.link(nc.vector.reciprocal(mass[:], mass[:]))
                    last = nc.vector.tensor_tensor(g3, g3, mass[:].unsqueeze(2).broadcast_to([P, HEADS, TOPK]), ALU.mult)
                    last.then_inc(picked, 1)
                    ch.end(PER_TILE)


def peer_gates(nc, c, name, h, giT, gates, hTh, hTl, u_tab, early):
    BATCH = 4
    BATCHES = GRID // BATCH
    SLOTS = 4
    HIGH_AT, LOW_AT, HID_AT = (0, 1), (3, 5), 4
    assert 2 * (BATCHES - HID_AT) == 3 * KC
    with Stage(nc, name) as s:
        first = [s.sb(f"first{i}", [P, BATCH, NKEYS]) for i in range(SLOTS)]
        second = [s.sb(f"second{i}", [P, BATCH, NKEYS]) for i in range(SLOTS)]
        grid = [s.sb(f"grid{i}", [P, NKEYS, GRID]) for i in range(2)]
        raised, zero = s.sb("raised", [P, 1]), s.sb("zero", [P, 1])
        u, uT = s.sb("u", [P, D]), s.sb("uT", [P, KC, P])
        uTh, uTl = s.sb("uTh", [P, KC, P], F32R), s.sb("uTl", [P, KC, P], F32R)
        gel = s.sb("gel", [P, SEQ])
        bank = [s.ps(f"bank{i}", [P, BATCH, P]) for i in range(SLOTS)]
        ups = [s.ps(f"ups{i}", [P, BANK]) for i in range(2)]
        hps = s.ps("hps", [P, SEQ])
        first_hot, second_hot, spread, filled = (s.sem(n) for n in ("first_hot", "second_hot", "spread", "filled"))
        stored = [s.sem(f"stored{i}") for i in range(2)]
        zeroed, weighted, scaled = s.sem("zeroed"), s.sem("weighted"), s.sem("scaled")
        load_u, u_flip, u_high, u_low = (s.sem(n) for n in ("load_u", "u_flip", "u_high", "u_low"))
        hid, gelued, kept = s.sem("hid"), s.sem("gelued"), s.sem("kept")
        u_v = u_tab.rearrange("(b p) d -> b p d", p=P)
        rows = lambda ap: ap.rearrange("p k n -> p (k n)")
        assert BATCH * P == BANK
        with s.block() as block:
            @block.vector
            def _(dve):
                with dve.Fori(0, GRIDS * BATCHES // SLOTS) as i:
                    for r in range(SLOTS):
                        dve.wait_ge(spread, i * SLOTS + r + 1)
                        at = (i * SLOTS + r) * BATCH
                        for side, hot, done in ((1, first, first_hot), (2, second, second_hot)):
                            nc.vector.tensor_tensor(hot[r][:], c["iota"][:].unsqueeze(1).broadcast_to([P, BATCH, NKEYS]),
                                                    giT[:, side, bass.ds(at, BATCH)].unsqueeze(2).broadcast_to([P, BATCH, NKEYS]),
                                                    ALU.is_equal).then_inc(done, 1)

            @block.gpsimd
            def _(pool):
                nc.gpsimd.memset(zero[:], 0.0).then_inc(zeroed, 1)
                starts_at_one(pool, u_low)
                with pool.Fori(0, GRIDS) as n:
                    for q in range(BATCHES):
                        at, r = n * GRID + q * BATCH, q % SLOTS
                        pool.wait_ge(first_hot, n * BATCHES + q + 1)
                        nc.gpsimd.tensor_tensor(first[r][:], first[r][:],
                                                giT[:, 0, bass.ds(at, BATCH)].unsqueeze(2).broadcast_to([P, BATCH, NKEYS]),
                                                ALU.mult).then_inc(weighted, 1)
                        if q in LOW_AT:
                            half = LOW_AT.index(q)
                            at = slice(4 * half, 4 * half + 4)
                            pool.wait_ge(u_high, 2 * n + half + 2)
                            nc.gpsimd.tensor_tensor(rows(uTl[:, at, :]), rows(uT[:, at, :]), rows(uTh[:, at, :]).bitcast(F32),
                                                    ALU.subtract).then_inc(u_low, 1)

            @block.tensor
            def _(pe):
                pe.sem_inc(spread, SLOTS)
                starts_at_one(pe, u_flip, hid)
                with pe.Fori(0, GRIDS) as n:
                    pe.wait_ge(load_u, 16 * n + 16)
                    pe.wait_ge(u_high, 2 * n + 1)
                    for half in range(2):
                        for j in range(4):
                            k = 4 * half + j
                            last = nc.tensor.transpose(ups[half][:, j * P:(j + 1) * P], u[:, k * P:(k + 1) * P], c["ident"][:])
                        last.then_inc(u_flip, 1)
                    for q in range(BATCHES):
                        r = q % SLOTS
                        pe.wait_ge(weighted, n * BATCHES + q + 1)
                        pe.wait_ge(second_hot, n * BATCHES + q + 1)
                        pe.wait_ge(filled, n * BATCHES + q + 1)
                        for m in range(BATCH):
                            last = nc.tensor.matmul(bank[r][:, m, :], second[r][:, m, :], first[r][:, m, :],
                                                    start=True, stop=True)
                        last.then_inc(spread, 1)
                        for step in range(2 * (q - HID_AT), 2 * (q - HID_AT) + 2) if q >= HID_AT else ():
                            k, m = step // 3, step % 3
                            if m == 0 and k % 4 == 0:
                                pe.wait_ge(u_low, 2 * n + k // 4 + 2)
                            if step == 0:
                                pe.wait_ge(gelued, n + 1)
                            w, x = ((uTh, hTh), (uTh, hTl), (uTl, hTh))[m]
                            last = nc.tensor.matmul(hps[:], w[:, k, :], x[:, k, :], start=(step == 0), stop=(step == 3 * KC - 1))
                            if step == 3 * KC - 1:
                                last.then_inc(hid, 1)

            @block.scalar
            def _(act):
                nc.scalar.mul(h[:], h[:], ALPHA).then_inc(scaled, 1)
                act.wait_ge(zeroed, 1)
                nc.scalar.copy(raised[:], zero[:]).then_inc(filled, SLOTS)
                starts_at_one(act, u_high, gelued)
                for sem in (stored[0], stored[1], kept):
                    act.sem_inc(sem, 16)
                with act.Fori(0, GRIDS // 2) as pair:
                    for odd in range(2):
                        n = 2 * pair + odd
                        act.wait_ge(stored[odd], 16 * pair + 16)
                        for q in range(BATCHES):
                            act.wait_ge(spread, n * BATCHES + q + SLOTS + 1)
                            nc.scalar.copy(grid[odd][:, :, BATCH * q:BATCH * (q + 1)],
                                           bank[q % SLOTS][:].rearrange("p t n -> p n t")).then_inc(filled, 1)
                            if q in HIGH_AT:
                                half = HIGH_AT.index(q)
                                at = slice(4 * half, 4 * half + 4)
                                act.wait_ge(u_flip, 2 * n + half + 2)
                                act.wait_ge(u_low, 2 * n + half + 1)
                                nc.scalar.copy(rows(uT[:, at, :]), ups[half][:])
                                if half == 0:
                                    act.wait_ge(hid, n + 1)
                                nc.scalar.copy(rows(uTh[:, at, :]), ups[half][:]).then_inc(u_high, 1)
                        act.wait_ge(hid, n + 2)
                        act.wait_ge(kept, 16 * n + 16)
                        nc.scalar.activation(gel[:], hps[:], ACT.Gelu).then_inc(gelued, 1)
                        act.wait_ge(filled, n * BATCHES + BATCHES + SLOTS)
                        act.dma_start(gates[:, bass.ds(n, 1), :, :], grid[odd][:].unsqueeze(1)).then_inc(stored[odd], 16)
                        act.wait_ge(gelued, n + 2)
                        act.dma_start(early[bass.ds(n + EARLY_SELECT, 1)], gel[:]).then_inc(kept, 16)
                for odd in range(2):
                    act.wait_ge(stored[odd], 16 * (GRIDS // 2 + 1))
                act.wait_ge(kept, 16 * (GRIDS + 1))
                act.wait_ge(scaled, 1)

            @block.sync
            def _(sp):
                with sp.Fori(0, GRIDS) as n:
                    sp.wait_ge(u_flip, 2 * n + 1)
                    sp.dma_start(u[:], u_v[bass.ds(n + EARLY_SELECT, 1)]).then_inc(load_u, 16)


def peer_experts(nc, c, name, hTh, hTl, acc, u_tab, v_tab, gates, early):
    BLOCKS = NKEYS
    GROUP = 4
    OUTS = TT * HALVES
    ROUND = 2 * GROUP
    FIRST = EARLY // ROUND
    assert EARLY % ROUND == 0
    with Stage(nc, name) as s:
        u = [s.sb(f"u{i}", [P, D]) for i in range(GROUP)]
        v = [s.sb(f"v{i}", [P, D]) for i in range(GROUP)]
        vh = [s.sb(f"vh{i}", [P, D], F32R) for i in range(ROUND)]
        vl = [s.sb(f"vl{i}", [P, D], F32R) for i in range(ROUND)]
        g = [s.sb(f"g{i}", [P, GRIDS, 1, GRID]) for i in range(GROUP)]
        uTh = [s.sb(f"uTh{i}", [P, KC, P], F32R) for i in range(2)]
        uTl = [s.sb(f"uTl{i}", [P, KC, P], F32R) for i in range(2)]
        act_h = [s.sb(f"acth{i}", [P, SEQ], F32R) for i in range(ROUND)]
        act_l = [s.sb(f"actl{i}", [P, SEQ], F32R) for i in range(ROUND)]
        gel = [s.sb(f"gel{i}", [P, SEQ]) for i in range(2)]
        eased = s.sb("eased", [P, 1])
        tps = [s.ps(f"tps{i}", [P, BANK]) for i in range(2)]
        hps = [s.ps(f"hps{i}", [P, SEQ]) for i in range(2)]
        ops = [s.ps(f"ops{i}", [P, BANK]) for i in range(4)]
        load_u = [s.sem(f"load_u{i}") for i in range(GROUP)]
        load_v = [s.sem(f"load_v{i}") for i in range(GROUP)]
        load_g = [s.sem(f"load_g{i}") for i in range(GROUP)]
        flip, u_high, u_low = s.sem("flip"), s.sem("u_high"), s.sem("u_low")
        v_high, v_low = s.sem("v_high"), s.sem("v_low")
        hid, gelued, gated, gated_high, gated_low = (s.sem(n) for n in ("hid", "gelued", "gated", "gated_high", "gated_low"))
        summed, added = s.sem("summed"), s.sem("added")
        u_v = u_tab.rearrange("(b p) d -> b p d", p=P)
        v_v = v_tab.rearrange("(b p) d -> b p d", p=P)
        f32 = lambda ap: ap.bitcast(F32)
        rows = lambda ap: ap.rearrange("p k n -> p (k n)")
        with s.block() as block:
            @block.sync
            def _(sp):
                def load(i, is_early):
                    for b in range(ROUND):
                        at = i * ROUND + b
                        sp.wait_ge(gated, i * ROUND + b - GROUP + 2 if b >= GROUP else i * ROUND + 1)
                        if is_early:
                            sp.dma_start(u[b % GROUP][:, 0:SEQ], early[bass.ds(at, 1)]).then_inc(load_u[b % GROUP], 16)
                        else:
                            sp.dma_start(u[b % GROUP][:], u_v[bass.ds(at, 1)]).then_inc(load_u[b % GROUP], 16)
                        sp.dma_start(g[b % GROUP][:], gates[:, :, bass.ds(at, 1), :]).then_inc(load_g[b % GROUP], 16)
                        sp.wait_ge(v_low, i * ROUND + b - GROUP + 2 if b >= GROUP else i * ROUND + 1)
                        sp.dma_start(v[b % GROUP][:], v_v[bass.ds(at, 1)]).then_inc(load_v[b % GROUP], 16)

                with sp.Fori(0, FIRST) as i:
                    load(i, True)
                with sp.Fori(FIRST, BLOCKS // ROUND) as i:
                    load(i, False)

            @block.tensor
            def _(pe):
                pe.sem_inc(summed, OUTS + 1)
                starts_at_one(pe, flip)

                def outputs(i, grp):
                    for part in range(OUTS // 4):
                        for x in range(GROUP):
                            b = GROUP * grp + x
                            if part == 0:
                                pe.wait_ge(v_low, i * ROUND + b + 2)
                                pe.wait_ge(gated_low, i * ROUND + b + 1)
                            for o in range(4):
                                t, half = (4 * part + o) // HALVES, (4 * part + o) % HALVES
                                if x == 0:
                                    pe.wait_ge(added, i * 2 * OUTS + grp * OUTS + 4 * part + o + OUTS - 3)
                                for n, (lhsT, rhs) in enumerate(((act_h, vh), (act_h, vl), (act_l, vh))):
                                    last = nc.tensor.matmul(ops[o][:], lhsT[b][:, t * P:(t + 1) * P],
                                                            rhs[b][:, half * BANK:(half + 1) * BANK],
                                                            start=(x == 0 and n == 0), stop=(x == GROUP - 1 and n == 2))
                                if x == GROUP - 1:
                                    last.then_inc(summed, 1)

                with pe.Fori(0, FIRST) as i:
                    outputs(i, 0)
                    outputs(i, 1)
                with pe.Fori(0, BLOCKS // ROUND - FIRST) as j:
                    def flip_block(b):
                        pe.wait_ge(load_u[b % GROUP], 16 * (2 * j + 2 * FIRST + b // GROUP + 1))
                        pe.wait_ge(u_low, 2 * (j * ROUND + b) + 1)
                        for half in range(2):
                            for n in range(4):
                                k = 4 * half + n
                                last = nc.tensor.transpose(tps[half][:, n * P:(n + 1) * P], u[b % GROUP][:, k * P:(k + 1) * P],
                                                           c["ident"][:])
                            last.then_inc(flip, 1)

                    for grp in range(2):
                        if grp == 0:
                            flip_block(0)
                        for x in range(GROUP):
                            b = GROUP * grp + x
                            if b + 1 < ROUND:
                                flip_block(b + 1)
                            pe.wait_ge(u_low, 2 * (j * ROUND + b) + 3)
                            if b >= 2:
                                pe.wait_ge(gelued, j * ROUND + b - 1)
                            for k in range(KC):
                                for n, (lhsT, rhs) in enumerate(((uTh, hTh), (uTh, hTl), (uTl, hTh))):
                                    last = nc.tensor.matmul(hps[b % 2][:], lhsT[b % 2][:, k, :], rhs[:, k, :],
                                                            start=(k == 0 and n == 0), stop=(k == KC - 1 and n == 2))
                            last.then_inc(hid, 1)
                        outputs(j + FIRST, grp)

            @block.scalar
            def _(act):
                def split_v(i, b):
                    act.wait_ge(load_v[b % GROUP], 16 * (2 * i + b // GROUP + 1))
                    act.wait_ge(summed, (2 * i + b // GROUP) * OUTS + 1)
                    nc.scalar.copy(vh[b][:], v[b % GROUP][:]).then_inc(v_high, 1)

                def gated_part(i, b):
                    act.wait_ge(gated, i * ROUND + b + 2)
                    nc.scalar.copy(act_h[b][:], gel[b % 2][:]).then_inc(gated_high, 1)

                with act.Fori(0, FIRST) as i:
                    for b in range(ROUND):
                        split_v(i, b)
                        gated_part(i, b)
                with act.Fori(0, BLOCKS // ROUND - FIRST) as j:
                    i = j + FIRST

                    def split_u(b):
                        for half in range(2):
                            act.wait_ge(flip, 2 * (j * ROUND + b) + half + 2)
                            if b >= 2 and half == 0:
                                act.wait_ge(hid, j * ROUND + b - 1)
                            nc.scalar.copy(rows(uTh[b % 2][:, 4 * half:4 * half + 4, :]), tps[half][:]).then_inc(u_high, 1)

                    for grp in range(2):
                        if grp == 0:
                            split_u(0)
                        for x in range(GROUP):
                            b = GROUP * grp + x
                            split_v(i, b)
                            if b + 1 < ROUND:
                                split_u(b + 1)
                            if x:
                                gated_part(i, b - 1)
                            act.wait_ge(hid, j * ROUND + b + 1)
                            if b >= 2:
                                act.wait_ge(gated_low, i * ROUND + b - 1)
                            nc.scalar.activation(gel[b % 2][:], hps[b % 2][:], ACT.Gelu).then_inc(gelued, 1)
                        gated_part(i, GROUP * grp + GROUP - 1)

            @block.gpsimd
            def _(pool):
                starts_at_one(pool, v_low)
                with pool.Fori(0, BLOCKS // ROUND) as i:
                    for b in range(ROUND):
                        pool.wait_ge(v_high, i * ROUND + b + 1)
                        nc.gpsimd.tensor_tensor(vl[b][:], v[b % GROUP][:], f32(vh[b][:]), ALU.subtract).then_inc(v_low, 1)

            @block.vector
            def _(dve):
                nc.vector.memset(eased[:], 0.0).then_inc(added, OUTS)
                starts_at_one(dve, gated, u_low)

                def gate(i, b, values):
                    dve.wait_ge(load_g[b % GROUP], 16 * (2 * i + b // GROUP + 1))
                    nc.vector.tensor_tensor(gel[b % 2][:], values, g[b % GROUP][:].rearrange("p s a n -> p (s a n)"), ALU.mult).then_inc(gated, 1)
                    dve.wait_ge(gated_high, i * ROUND + b + 1)
                    nc.vector.tensor_tensor(act_l[b][:], gel[b % 2][:], f32(act_h[b][:]), ALU.subtract).then_inc(gated_low, 1)

                def gather(i, grp, outs):
                    for o in outs:
                        dve.wait_ge(summed, (2 * i + grp) * OUTS + OUTS + o + 2)
                        dve.wait_ge(added, (2 * i + grp) * OUTS + o + 1)
                        t, half = o // HALVES, o % HALVES
                        nc.vector.tensor_tensor(acc[:, t, half * BANK:(half + 1) * BANK],
                                                acc[:, t, half * BANK:(half + 1) * BANK], ops[o % 4][:],
                                                ALU.add).then_inc(added, 1)

                with dve.Fori(0, FIRST) as i:
                    for b in range(GROUP):
                        dve.wait_ge(load_u[b], 16 * (2 * i + 1))
                        gate(i, b, u[b][:, 0:SEQ])
                    gather(i, 0, range(4))
                    for b in range(GROUP, ROUND):
                        dve.wait_ge(load_u[b % GROUP], 16 * (2 * i + 2))
                        gate(i, b, u[b % GROUP][:, 0:SEQ])
                    gather(i, 0, range(4, OUTS))
                    gather(i, 1, range(OUTS))
                with dve.Fori(0, BLOCKS // ROUND - FIRST) as j:
                    def split_u(b):
                        for half in range(2):
                            dve.wait_ge(u_high, 2 * (j * ROUND + b) + half + 1)
                            if b >= 2 and half == 0:
                                dve.wait_ge(hid, j * ROUND + b - 1)
                            nc.vector.tensor_tensor(rows(uTl[b % 2][:, 4 * half:4 * half + 4, :]), tps[half][:],
                                                    f32(rows(uTh[b % 2][:, 4 * half:4 * half + 4, :])),
                                                    ALU.subtract).then_inc(u_low, 1)

                    for grp in range(2):
                        if grp == 0:
                            split_u(0)
                        for x in range(GROUP):
                            b = GROUP * grp + x
                            if b + 1 < ROUND:
                                split_u(b + 1)
                            dve.wait_ge(gelued, j * ROUND + b + 1)
                            gate(j + FIRST, b, gel[b % 2][:])
                        gather(j + FIRST, grp, range(OUTS))


GDN_HEADS = 8
GDN_QKV = 3 * GDN_HEADS
CONV = 4


def gdn_project(nc, c, name, xTh, xTl, w_in, conv_w, qkvT, z, logits):
    ROUND_SLABS = 4
    ROUNDS = GDN_QKV // (ROUND_SLABS * SLAB_TILES)
    ROUND = ROUND_SLABS * SLAB_TILES
    QKV_SLABS, Z_SLABS = ROUNDS * ROUND_SLABS, GDN_HEADS * P // SLAB
    LOGITS = 2 * GDN_HEADS
    with Stage(nc, name) as s:
        tail = s.sb("tail", [P, KC, LOGITS])
        tail_h, tail_l = s.sb("tail_h", [P, KC, LOGITS], F32R), s.sb("tail_l", [P, KC, LOGITS], F32R)
        taps = s.sb("taps", [P, P])
        tapsT = s.sb("tapsT", [P, CONV * GDN_QKV])
        conv = [s.sb(f"conv{i}", [P, SEQ]) for i in range(2)]
        pp = [s.ps(f"pp{i}", [P, BANK]) for i in range(4)]
        taps_ps = s.ps("taps_ps", [P, CONV * GDN_QKV])
        load_taps, taps_turned, taps_ready = s.sem("load_taps"), s.sem("taps_turned"), s.sem("taps_ready")
        projected, mixed, convolved, silued = s.sem("projected"), s.sem("mixed"), s.sem("convolved"), s.sem("silued")
        zmade, ztaken, tail_high, tail_low = s.sem("zmade"), s.sem("ztaken"), s.sem("tail_high"), s.sem("tail_low")
        slabs = Slabs(nc, s, w_in[:, 0:(QKV_SLABS + Z_SLABS) * SLAB].rearrange("(k p) (s n) -> s p k n", p=P, n=SLAB), projected)
        with s.block() as block:
            @block.sync
            def _(sp):
                sp.dma_start(taps[0:CONV * GDN_QKV, :], conv_w.rearrange("j (t c) -> (j t) c", c=P)).then_inc(load_taps, 16)
                with nc.allow_non_contiguous_dma(reason="sixteen columns"):
                    sp.dma_start(tail[:], w_in[:, (QKV_SLABS + Z_SLABS) * SLAB:].rearrange("(k p) n -> p k n", p=P)).then_inc(load_taps, 16)
                with sp.Fori(0, ROUNDS) as i:
                    for n in range(ROUND_SLABS):
                        slabs.load(sp, i * ROUND_SLABS, n)
                for n in range(Z_SLABS):
                    slabs.load(sp, QKV_SLABS, n)

            @block.gpsimd
            def _(pool):
                pool.sem_inc(slabs.low_ready, 2)
                with pool.Fori(0, ROUNDS) as i:
                    for n in range(ROUND_SLABS):
                        slabs.split_low(pool, i * ROUND_SLABS, n)
                for n in range(Z_SLABS):
                    slabs.split_low(pool, QKV_SLABS, n)
                pool.wait_ge(tail_high, 1)
                nc.gpsimd.tensor_tensor(tail_l[:], tail[:], tail_h[:].bitcast(F32), ALU.subtract).then_inc(tail_low, 1)

            @block.tensor
            def _(pe):
                pe.sem_inc(projected, 2 * SLAB_TILES)
                pe.wait_ge(load_taps, 32)
                n = CONV * GDN_QKV
                nc.tensor.transpose(taps_ps[:], taps[0:n, :], c["ident"][0:n, 0:n]).then_inc(taps_turned, 1)
                with pe.Fori(0, ROUNDS) as i:
                    for b in range(ROUND_SLABS):
                        slabs.wait(pe, i * ROUND_SLABS, b)
                        for j in range(SLAB_TILES):
                            n = b * SLAB_TILES + j
                            pe.wait_ge(convolved, i * ROUND + n + 1)
                            slabs.columns(nc, pp[n % 4][:], b, j, xTh, xTl).then_inc(projected, 1)
                pe.wait_ge(convolved, GDN_QKV + 4)
                for b in range(Z_SLABS):
                    slabs.wait(pe, QKV_SLABS, b)
                    for t in range(TT):
                        n = b * TT + t
                        if n >= 4:
                            pe.wait_ge(ztaken, n - 3)
                        last = slabs.tokens(nc, pp[n % 4][:, 0:SLAB], b, t, xTh, xTl)
                        last.then_inc(zmade, 1)
                    pe.wait_ge(zmade, (b + 1) * TT)
                    pe.sem_inc(projected, SLAB_TILES)
                pe.wait_ge(ztaken, Z_SLABS * TT - 3)
                pe.wait_ge(tail_low, 1)
                for t in range(TT):
                    at = slice(t * P, (t + 1) * P)
                    for k in range(KC):
                        for m, (x, w) in enumerate(((xTh, tail_h), (xTh, tail_l), (xTl, tail_h))):
                            last = nc.tensor.matmul(pp[0][:, t * LOGITS:(t + 1) * LOGITS], x[:, k, at], w[:, k, :],
                                                    start=(k == 0 and m == 0), stop=(k == KC - 1 and m == 2))
                last.then_inc(zmade, 1)

            @block.vector
            def _(dve):
                dve.wait_ge(taps_turned, 1)
                nc.vector.tensor_copy(tapsT[:], taps_ps[:]).then_inc(taps_ready, 1)
                dve.wait_ge(taps_ready, 1)
                nc.vector.memset(conv[0][:, 0:1], 0.0).then_inc(convolved, 4)
                with dve.Fori(0, ROUNDS) as i:
                    ch = Chain(dve, mixed, i * (ROUND * (CONV - 1)))
                    for n in range(ROUND):
                        at = i * ROUND + n
                        src, dst = pp[n % 4], conv[n % 2]
                        dve.wait_ge(projected, at + 2 * SLAB_TILES + 1)
                        dve.wait_ge(silued, at + 1)

                        def tap(j):
                            return tapsT[:, bass.ds(at + j * GDN_QKV, 1)]

                        ch.link(nc.vector.tensor_scalar(dst[:], src[:], tap(CONV - 1), None, ALU.mult))
                        for back in range(1, CONV):
                            last = nc.vector.scalar_tensor_tensor(dst[:, back:], src[:, 0:SEQ - back], tap(CONV - 1 - back),
                                                                  dst[:, back:], ALU.mult, ALU.add)
                            if back < CONV - 1:
                                ch.link(last)
                        last.then_inc(convolved, 1)
                    ch.end(ROUND * (CONV - 1))

            @block.scalar
            def _(act):
                act.wait_ge(taps_ready, 1)
                nc.scalar.copy(conv[1][:, 0:1], tapsT[:, 0:1]).then_inc(silued, 2)
                slabs.split_high(act, 0, 0, 0)
                with act.Fori(0, ROUNDS) as i:
                    for b in range(ROUND_SLABS):
                        slabs.split_high(act, i * ROUND_SLABS, b + 1, i * (ROUND_SLABS // 2))
                        for n in range(b * SLAB_TILES, (b + 1) * SLAB_TILES):
                            at = i * ROUND + n
                            act.wait_ge(convolved, at + 5)
                            nc.scalar.activation(qkvT[:, bass.ds(at, 1), :], conv[n % 2][:].unsqueeze(1), ACT.Silu).then_inc(silued, 1)
                nc.scalar.copy(tail_h[:], tail[:]).then_inc(tail_high, 1)
                for b in range(Z_SLABS):
                    if b + 1 < Z_SLABS:
                        slabs.split_high(act, QKV_SLABS, b + 1, QKV_SLABS // 2)
                    for t in range(TT):
                        n = b * TT + t
                        act.wait_ge(zmade, n + 1)
                        nc.scalar.activation(z[:, t, b * SLAB:(b + 1) * SLAB], pp[n % 4][:, 0:SLAB], ACT.Silu).then_inc(ztaken, 1)
                act.wait_ge(zmade, Z_SLABS * TT + 1)
                nc.scalar.copy(logits[:], pp[0][:, 0:TT * LOGITS].rearrange("p (t n) -> p t n", t=TT)).then_inc(ztaken, 1)
                act.wait_ge(ztaken, Z_SLABS * TT + 1)


def gdn_normalize(nc, c, name, qkvT):
    GROUP = 4
    SETS_QK = 2 * GDN_HEADS
    ROUNDS = SETS_QK // GROUP
    with Stage(nc, name) as s:
        sq = [s.sb(f"sq{i}", [P, SEQ]) for i in range(GROUP)]
        diag = [s.sb(f"diag{i}", [P, TT, P]) for i in range(GROUP)]
        factor = s.sb("factor", [P, SETS_QK * TT])
        eps = [s.sb(f"eps{i}", [P, 1]) for i in range(2)]
        total = s.ps("total", [P, SETS_QK * TT])
        wide = [s.ps(f"wide{i}", [P, SEQ]) for i in range(GROUP)]
        squared, summed, rooted, inverted = s.sem("squared"), s.sem("summed"), s.sem("rooted"), s.sem("inverted")
        placed, spread, scaled, ready = s.sem("placed"), s.sem("spread"), s.sem("scaled"), s.sem("ready")
        with s.block() as block:
            @block.scalar
            def _(act):
                with act.Fori(0, ROUNDS) as i:
                    for n in range(GROUP):
                        act.wait_ge(summed, i * GROUP + n + 1)
                        nc.scalar.activation(sq[n][:].unsqueeze(1), qkvT[:, bass.ds(i * GROUP + n, 1), :],
                                             ACT.Square).then_inc(squared, 1)
                act.wait_ge(ready, 2)
                act.wait_ge(summed, SETS_QK + GROUP)
                half = SETS_QK * TT // 2
                nc.scalar.activation(factor[:, 0:half], total[:, 0:half], ACT.Sqrt, bias=eps[0][:], scale=float(P))
                nc.scalar.activation(factor[:, half:2 * half], total[:, half:2 * half], ACT.Sqrt, bias=eps[1][:],
                                     scale=1.0).then_inc(rooted, 1)

            @block.gpsimd
            def _(pool):
                pool.wait_ge(inverted, 1)
                with pool.Fori(0, ROUNDS) as i:
                    for n in range(GROUP):
                        pool.wait_ge(spread, i * GROUP + n + 1)
                        nc.gpsimd.tensor_tensor(diag[n][:], c["ident"][:].unsqueeze(1).broadcast_to([P, TT, P]),
                                                factor[:, bass.ds(i * (GROUP * TT) + n * TT, TT)].unsqueeze(2).broadcast_to([P, TT, P]),
                                                ALU.mult).then_inc(placed, 1)

            @block.tensor
            def _(pe):
                pe.sem_inc(summed, GROUP)
                pe.sem_inc(spread, GROUP)
                with pe.Fori(0, ROUNDS) as i:
                    for n in range(GROUP):
                        pe.wait_ge(squared, i * GROUP + n + 1)
                        for t in range(TT):
                            last = nc.tensor.matmul(total[:, bass.ds(i * (GROUP * TT) + n * TT + t, 1)], sq[n][:, t * P:(t + 1) * P],
                                                    c["ones"][:, 0:1], start=True, stop=True)
                        last.then_inc(summed, 1)
                with pe.Fori(0, ROUNDS) as i:
                    for n in range(GROUP):
                        pe.wait_ge(placed, i * GROUP + n + 1)
                        pe.wait_ge(scaled, i * GROUP + n + 1)
                        nc.tensor.matmul(wide[n][:], c["ones"][:], diag[n][:].rearrange("p t n -> p (t n)"),
                                         start=True, stop=True).then_inc(spread, 1)

            @block.vector
            def _(dve):
                nc.vector.memset(eps[0][:], P * RMS_EPS).then_inc(ready, 1)
                nc.vector.memset(eps[1][:], RMS_EPS).then_inc(ready, 1)
                dve.sem_inc(scaled, GROUP)
                dve.wait_ge(rooted, 1)
                nc.vector.reciprocal(factor[:], factor[:]).then_inc(inverted, 1)
                with dve.Fori(0, ROUNDS) as i:
                    for n in range(GROUP):
                        dve.wait_ge(spread, i * GROUP + n + GROUP + 1)
                        at = qkvT[:, bass.ds(i * GROUP + n, 1), :]
                        nc.vector.tensor_tensor(at, at, wide[n][:].unsqueeze(1), ALU.mult).then_inc(scaled, 1)
                dve.wait_ge(scaled, SETS_QK + GROUP)


def gdn_gates(nc, c, name, logits, a_log, dt_bias, gate):
    H = GDN_HEADS
    with Stage(nc, name) as s:
        arow, brow = s.sb("arow", [P, H]), s.sb("brow", [P, H])
        x, e, t = s.sb("x", [P, TT, H]), s.sb("e", [P, TT, H]), s.sb("t", [P, TT, H])
        sums = s.ps("sums", [P, 2, TT * H])
        load, chain, acted, summed = s.sem("load"), s.sem("chain"), s.sem("acted"), s.sem("summed")
        wide = lambda ap: ap.unsqueeze(1).broadcast_to([P, TT, H])
        flat = lambda ap: ap.rearrange("p t h -> p (t h)")
        with s.block() as block:
            @block.sync
            def _(sp):
                sp.dma_start(arow[:], a_log.broadcast_to([P, H])).then_inc(load, 16)
                sp.dma_start(brow[:], dt_bias.broadcast_to([P, H])).then_inc(load, 16)

            @block.vector
            def _(dve):
                ch = Chain(dve, chain)
                dve.wait_ge(load, 32)
                ch.link(nc.vector.tensor_tensor(x[:], logits[:, :, H:2 * H], wide(brow[:]), ALU.add))
                ch.link(nc.vector.tensor_scalar(t[:], x[:], -1.0, None, ALU.mult))
                ch.link(nc.vector.tensor_tensor(t[:], t[:], x[:], ALU.min))
                dve.wait_ge(acted, 4)
                ch.link(nc.vector.tensor_scalar(gate["beta"][:], gate["beta"][:], 1.0, None, ALU.add))
                ch.link(nc.vector.reciprocal(gate["beta"][:], gate["beta"][:]))
                ch.link(nc.vector.tensor_scalar(x[:], x[:], 0.0, None, ALU.max))
                ch.link(nc.vector.tensor_tensor(x[:], x[:], e[:], ALU.add))
                ch.link(nc.vector.tensor_tensor(x[:], x[:], wide(arow[:]), ALU.mult))
                ch.link(nc.vector.tensor_scalar(gate["g"][:], x[:], -1.0, None, ALU.mult))
                dve.wait_ge(summed, 1)
                ch.link(nc.vector.tensor_copy(flat(gate["sum"][:]), sums[:, 0, :]))
                ch.link(nc.vector.tensor_copy(flat(gate["last"][:]), sums[:, 1, :]))
                ch.link(nc.vector.tensor_tensor(gate["rest"][:], gate["last"][:], gate["sum"][:], ALU.subtract))
                dve.wait_ge(acted, 7)
                ch.link(nc.vector.tensor_tensor(gate["beta_exp"][:], gate["beta"][:], gate["exp"][:], ALU.mult))

            @block.scalar
            def _(act):
                act.wait_ge(load, 32)
                nc.scalar.activation(arow[:], arow[:], ACT.Exp).then_inc(acted, 1)
                nc.scalar.activation(gate["beta"][:], logits[:, :, 0:H], ACT.Exp, scale=-1.0).then_inc(acted, 1)
                act.wait_ge(chain, 3)
                nc.scalar.activation(e[:], t[:], ACT.Exp).then_inc(acted, 1)
                act.wait_ge(acted, 3)
                nc.scalar.activation(e[:], e[:], ACT.Ln, bias=c["ones"][:, 0:1]).then_inc(acted, 1)
                act.wait_ge(chain, 12)
                nc.scalar.activation(gate["exp"][:], gate["sum"][:], ACT.Exp).then_inc(acted, 1)
                nc.scalar.activation(gate["last"][:], gate["last"][:], ACT.Exp).then_inc(acted, 1)
                nc.scalar.activation(gate["rest"][:], gate["rest"][:], ACT.Exp).then_inc(acted, 1)

            @block.tensor
            def _(pe):
                pe.wait_ge(chain, 9)
                nc.tensor.matmul(sums[:, 0, :], c["upper"][:], flat(gate["g"][:]), start=True, stop=True)
                nc.tensor.matmul(sums[:, 1, :], c["ones"][:], flat(gate["g"][:]), start=True, stop=True).then_inc(summed, 1)


class Steps:

    def __init__(self, names, heads):
        self.names, self.heads = names.split(), heads
        assert len(set(self.names)) == len(self.names)

    def after(self, i, name, j):
        return i * (len(self.names) * self.heads) + self.names.index(name) * self.heads + j + 2

    def rounds(self, i):
        return i * (len(self.names) * self.heads) + 1


def gdn_recur(nc, c, name, qkvT, gate, o):
    G = 2
    H, C = GDN_HEADS, TT
    PE_STEPS = Steps("row kk knat vnat qk decT LT L2 U2 Y1 L4 U4 Y2 L8 Y3 YT N NT W0 N2 N2T W1 N4T W2 wT "
                     + " ".join(f"v{n} s{n} o{n}" for n in range(C)), G)
    ACT_STEPS = Steps("gB kS vS dec expRow decMT U L2 L4 L8 YT N N2 N4T wT " + " ".join(f"v{n} o{n}" for n in range(C)), G)
    DVE_STEPS = Steps("gap decM qg kbg kdec vb L0 L attnT LD UD UO Y0 U2 Y1 U4 Y2 Y3 NT W0 N2T W1 W2 "
                      + " ".join(f"s{n}" for n in range(C)), G)
    with Stage(nc, name) as s:
        names = ("gB kS vS gap decM qg kbg kdec vb L attnT decMT LD U UO Y0 Y1 Y2 Y3 L2 U2 expRow vnew").split()
        b = {n: [s.sb(f"{n}{j}", [P, C, P]) for j in range(G)] for n in names}
        for new, old in (("L4", "LD"), ("U4", "expRow"), ("L8", "gap"), ("YT", "gB"), ("N", "L"), ("NT", "decM"),
                         ("W0", "Y0"), ("N2", "L2"), ("N2T", "U2"), ("W1", "Y1"), ("N4T", "Y2"), ("W2", "kS"), ("wT", "decMT")):
            b[new] = b[old]
        UD = [s.sb(f"UD{j}", [P, C, P]) for j in range(G)]
        b["UD"] = UD
        state = [s.sb(f"state{j}", [P, P]) for j in range(G)]
        bank = [[s.ps(f"bank{j}_{k}", [P, C, P]) for k in range(8 // G)] for j in range(G)]
        pe_done, act_done, dve_done = s.sem("pe_done"), s.sem("act_done"), s.sem("dve_done")
        ident4 = c["ident"][:].unsqueeze(1).broadcast_to([P, C, P])
        block4 = c["block16"][:].unsqueeze(1).broadcast_to([P, C, P])
        lower4 = c["lower"][:].unsqueeze(1).broadcast_to([P, C, P])
        strict4 = c["strict"][:].unsqueeze(1).broadcast_to([P, C, P])

        def ps(step, j):
            return bank[j][PE_STEPS.names.index(step) % len(bank[j])]

        with s.block() as block:
            @block.tensor
            def _(pe):
                starts_at_one(pe, pe_done)
                with pe.Fori(0, H // G) as i:

                    def from_act(step, j):
                        pe.wait_ge(act_done, ACT_STEPS.after(i, step, j))

                    def from_dve(step, j):
                        pe.wait_ge(dve_done, DVE_STEPS.after(i, step, j))

                    def each(step, lhsT, rhs, acts=(), dves=()):
                        for j in range(G):
                            for a in acts:
                                from_act(a, j)
                            for d in dves:
                                from_dve(d, j)
                            for n in range(C):
                                last = nc.tensor.matmul(ps(step, j)[:, n, :], lhsT(j, n), rhs(j, n), start=True, stop=True)
                            last.then_inc(pe_done, 1)

                    def turn(step, src, acts=(), dves=()):
                        for j in range(G):
                            for a in acts:
                                from_act(a, j)
                            for d in dves:
                                from_dve(d, j)
                            for n in range(C):
                                last = nc.tensor.transpose(ps(step, j)[:, n, :], src(j, n), c["ident"][:])
                            last.then_inc(pe_done, 1)

                    def of(m):
                        return lambda j, n: b[m][j][:, n, :]

                    each("row", of("gB"), lambda j, n: c["upper"][:], acts=["gB"])
                    each("kk", of("kS"), of("kS"), acts=["kS"])
                    turn("knat", of("kS"))
                    turn("vnat", of("vS"), acts=["vS"])
                    each("qk", of("kS"), lambda j, n: qkvT[:, bass.ds(i * G + j, 1), n * P:(n + 1) * P],
                         acts=["expRow"], dves=["gap"])
                    turn("decT", of("decM"), dves=["L0"])
                    turn("LT", of("L"), dves=["L", "kdec"])
                    each("L2", of("UD"), of("LD"), dves=["UD", "vb"])
                    each("U2", of("LD"), of("UD"), dves=["attnT"])
                    each("Y1", of("L2"), of("Y0"), acts=["L2", "decMT"], dves=["Y0"])
                    each("L4", of("U2"), of("L2"), acts=["U"], dves=["U2"])
                    each("U4", of("L2"), of("U2"))
                    each("Y2", of("L4"), of("Y1"), acts=["L4"], dves=["Y1"])
                    each("L8", of("U4"), of("L4"), dves=["U4"])
                    each("Y3", of("L8"), of("Y2"), acts=["L8"], dves=["Y2"])
                    turn("YT", of("Y3"), dves=["Y3"])
                    each("N", of("YT"), of("UO"), acts=["YT"], dves=["UO"])
                    each("NT", of("UO"), of("YT"))
                    each("W0", of("NT"), of("Y3"), dves=["NT"])
                    each("N2", of("NT"), of("N"), acts=["N"])
                    each("N2T", of("N"), of("NT"))
                    each("W1", of("N2T"), of("W0"), dves=["N2T", "W0"])
                    each("N4T", of("N2"), of("N2T"), acts=["N2"])
                    each("W2", of("N4T"), of("W1"), acts=["N4T"], dves=["W1"])
                    each("wT", of("kbg"), of("W2"), dves=["W2"])
                    for n in range(C):
                        for j in range(G):
                            new = ps(f"v{n}", j)[:, 0, :]
                            last = nc.tensor.matmul(new, b["W2"][j][:, n, :], b["vb"][j][:, n, :], start=True, stop=(n == 0))
                            if n:
                                from_act("wT", j)
                                from_dve(f"s{n - 1}", j)
                                last = nc.tensor.matmul(new, b["wT"][j][:, n, :], state[j][:], start=False, stop=True)
                            last.then_inc(pe_done, 1)
                        for j in range(G):
                            from_act(f"v{n}", j)
                            nc.tensor.matmul(ps(f"s{n}", j)[:, 0, :], b["kdec"][j][:, n, :], b["vnew"][j][:, n, :],
                                             start=True, stop=True).then_inc(pe_done, 1)
                        for j in range(G):
                            if n:
                                nc.tensor.matmul(ps(f"o{n}", j)[:, 0, :], b["qg"][j][:, n, :], state[j][:],
                                                 start=True, stop=False)
                            nc.tensor.matmul(ps(f"o{n}", j)[:, 0, :], b["attnT"][j][:, n, :], b["vnew"][j][:, n, :],
                                             start=(n == 0), stop=True).then_inc(pe_done, 1)

            @block.scalar
            def _(act):
                starts_at_one(act, act_done)
                with act.Fori(0, H // G) as i:
                    def do(step, make, pes=(), dves=(), acts=()):
                        for j in range(G):
                            for p in pes:
                                act.wait_ge(pe_done, PE_STEPS.after(i, p, j))
                            for d in dves:
                                act.wait_ge(dve_done, DVE_STEPS.after(i, d, j))
                            for a in acts:
                                act.wait_ge(act_done, ACT_STEPS.after(i, a, j))
                            make(j).then_inc(act_done, 1)

                    def copy(step):
                        do(step, lambda j: nc.scalar.copy(b[step][j][:], ps(step, j)[:]), pes=[step])

                    act.wait_ge(pe_done, PE_STEPS.rounds(i))
                    act.wait_ge(dve_done, DVE_STEPS.rounds(i))
                    do("gB", lambda j: nc.scalar.copy(b["gB"][j][:], gate["g"][:, :, bass.ds(i * G + j, 1)].broadcast_to([P, C, P])))
                    for part, step in ((1, "kS"), (2, "vS")):
                        do(step, lambda j: nc.scalar.copy(b[step][j][:].rearrange("p n t -> p (n t)").unsqueeze(1),
                                                          qkvT[:, bass.ds(i * G + j + part * H, 1), :]))
                    do("dec", lambda j: nc.scalar.activation(b["gap"][j][:], b["gap"][j][:], ACT.Exp, scale=-1.0), dves=["gap"])
                    do("expRow", lambda j: nc.scalar.activation(b["expRow"][j][:], ps("row", j)[:], ACT.Exp), pes=["row"])
                    do("decMT", lambda j: nc.scalar.copy(b["decMT"][j][:], ps("decT", j)[:]), pes=["decT"])
                    do("U", lambda j: nc.scalar.copy(b["U"][j][:], ps("LT", j)[:]), pes=["LT"])
                    copy("L2")
                    do("L4", lambda j: nc.scalar.copy(b["L4"][j][:], ps("L4", j)[:]), pes=["L4"])
                    copy("L8")
                    copy("YT")
                    copy("N")
                    copy("N2")
                    copy("N4T")
                    do("wT", lambda j: nc.scalar.mul(b["wT"][j][:], ps("wT", j)[:], -1.0), pes=["wT"])
                    for n in range(C):
                        do(f"v{n}", lambda j: nc.scalar.copy(b["vnew"][j][:, n, :], ps(f"v{n}", j)[:, 0, :]), pes=[f"v{n}"])
                        do(f"o{n}", lambda j: nc.scalar.copy(o[:, n, bass.ds((i * G + j) * P, P)], ps(f"o{n}", j)[:, 0, :]), pes=[f"o{n}"])
                act.wait_ge(act_done, ACT_STEPS.rounds(H // G))

            @block.vector
            def _(dve):
                starts_at_one(dve, dve_done)
                with dve.Fori(0, H // G) as i:
                    def do(step, make, pes=(), acts=(), dves=()):
                        for j in range(G):
                            for p in pes:
                                dve.wait_ge(pe_done, PE_STEPS.after(i, p, j))
                            for a in acts:
                                dve.wait_ge(act_done, ACT_STEPS.after(i, a, j))
                            for d in dves:
                                dve.wait_ge(dve_done, DVE_STEPS.after(i, d, j))
                            make(j).then_inc(dve_done, 1)

                    def col(m, j):
                        return gate[m][:, :, bass.ds(i * G + j, 1)].broadcast_to([P, C, P])

                    tt = nc.vector.tensor_tensor

                    def gaps(j):
                        for n in range(C):
                            last = nc.vector.tensor_scalar(b["gap"][j][:, n, :], ps("row", j)[:, n, :],
                                                           gate["sum"][:, n, bass.ds(i * G + j, 1)], 0.0, ALU.subtract, ALU.max)
                        return last

                    def lows(j):
                        for n in range(C):
                            last = nc.vector.scalar_tensor_tensor(b["L"][j][:, n, :], ps("kk", j)[:, n, :],
                                                                  gate["beta"][:, n, bass.ds(i * G + j, 1)],
                                                                  b["decM"][j][:, n, :], ALU.mult, ALU.mult)
                        return last

                    do("gap", gaps, pes=["row"])
                    do("decM", lambda j: tt(b["decM"][j][:], b["gap"][j][:], lower4, ALU.mult), acts=["dec"])
                    do("qg", lambda j: tt(b["qg"][j][:].rearrange("p n t -> p (n t)").unsqueeze(1),
                                          qkvT[:, bass.ds(i * G + j, 1), :],
                                          b["expRow"][j][:].rearrange("p n t -> p (n t)").unsqueeze(1), ALU.mult), acts=["expRow"])
                    do("kbg", lambda j: tt(b["kbg"][j][:], ps("knat", j)[:], col("beta_exp", j), ALU.mult), pes=["knat"])
                    do("kdec", lambda j: tt(b["kdec"][j][:], ps("knat", j)[:], col("rest", j), ALU.mult))
                    do("vb", lambda j: tt(b["vb"][j][:], ps("vnat", j)[:], col("beta", j), ALU.mult), pes=["vnat"])
                    do("L0", lows, pes=["kk"], dves=["decM"])
                    do("L", lambda j: tt(b["L"][j][:], b["L"][j][:], strict4, ALU.mult), dves=["L0"])
                    do("attnT", lambda j: tt(b["attnT"][j][:], ps("qk", j)[:], b["decMT"][j][:], ALU.mult), pes=["qk"], acts=["decMT"])
                    do("LD", lambda j: tt(b["LD"][j][:], b["L"][j][:], block4, ALU.mult), dves=["L"])
                    do("UD", lambda j: tt(b["UD"][j][:], b["U"][j][:], block4, ALU.mult), acts=["U"])
                    do("UO", lambda j: tt(b["UO"][j][:], b["U"][j][:], b["UD"][j][:], ALU.subtract), dves=["UD"])
                    do("Y0", lambda j: tt(b["Y0"][j][:], ident4, b["UD"][j][:], ALU.subtract))
                    do("U2", lambda j: nc.vector.tensor_copy(b["U2"][j][:], ps("U2", j)[:]), pes=["U2"])
                    do("Y1", lambda j: tt(b["Y1"][j][:], b["Y0"][j][:], ps("Y1", j)[:], ALU.add), pes=["Y1"])
                    do("U4", lambda j: nc.vector.tensor_copy(b["U4"][j][:], ps("U4", j)[:]), pes=["U4"])
                    do("Y2", lambda j: tt(b["Y2"][j][:], b["Y1"][j][:], ps("Y2", j)[:], ALU.add), pes=["Y2"], dves=["Y1"])
                    do("Y3", lambda j: tt(b["Y3"][j][:], b["Y2"][j][:], ps("Y3", j)[:], ALU.add), pes=["Y3"], dves=["Y2"])
                    do("NT", lambda j: nc.vector.tensor_copy(b["NT"][j][:], ps("NT", j)[:]), pes=["NT"])
                    do("W0", lambda j: tt(b["W0"][j][:], b["Y3"][j][:], ps("W0", j)[:], ALU.subtract), pes=["W0"])
                    do("N2T", lambda j: nc.vector.tensor_copy(b["N2T"][j][:], ps("N2T", j)[:]), pes=["N2T"])
                    do("W1", lambda j: tt(b["W1"][j][:], b["W0"][j][:], ps("W1", j)[:], ALU.add), pes=["W1"], dves=["W0"])
                    do("W2", lambda j: tt(b["W2"][j][:], b["W1"][j][:], ps("W2", j)[:], ALU.add), pes=["W2"], dves=["W1"])
                    do("s0", lambda j: nc.vector.tensor_copy(state[j][:], ps("s0", j)[:, 0, :]), pes=["s0"])
                    for n in range(1, C):
                        do(f"s{n}", lambda j: nc.vector.scalar_tensor_tensor(
                            state[j][:], state[j][:], gate["last"][:, n, bass.ds(i * G + j, 1)], ps(f"s{n}", j)[:, 0, :],
                            ALU.mult, ALU.add), pes=[f"s{n}", f"o{n}"], dves=[f"s{n - 1}"])
                dve.wait_ge(dve_done, DVE_STEPS.rounds(H // G))


def gdn_gate_out(nc, c, name, o, z, norm_g):
    H, L = GDN_HEADS, TT * GDN_HEADS
    with Stage(nc, name) as s:
        sq = s.sb("sq", [P, L, P])
        ss = s.sb("ss", [P, L])
        grow = s.sb("grow", [P, P])
        eps = s.sb("eps", [P, 1])
        load, ready, squared, summed, rooted = (s.sem(n) for n in ("load", "ready", "squared", "summed", "rooted"))
        inverted, scaled, gained, gated = (s.sem(n) for n in ("inverted", "scaled", "gained", "gated"))
        o3 = o[:].rearrange("p t (h d) -> p (t h) d", d=P)
        z3 = z[:].rearrange("p t (h d) -> p (t h) d", d=P)
        tile = lambda t: slice(t * H, (t + 1) * H)
        with s.block() as block:
            @block.sync
            def _(sp):
                sp.dma_start(grow[:], norm_g.broadcast_to([P, P])).then_inc(load, 16)

            @block.scalar
            def _(act):
                for t in range(TT):
                    nc.scalar.activation(sq[:, tile(t), :], o3[:, tile(t), :], ACT.Square).then_inc(squared, 1)
                act.wait_ge(ready, 1)
                act.wait_ge(summed, TT)
                nc.scalar.activation(ss[:], ss[:], ACT.Sqrt, bias=eps[:], scale=1.0 / P).then_inc(rooted, 1)

            @block.gpsimd
            def _(pool):
                pool.wait_ge(load, 16)
                for t in range(TT):
                    nc.gpsimd.tensor_tensor(z3[:, tile(t), :], z3[:, tile(t), :], grow[:].unsqueeze(1).broadcast_to([P, H, P]),
                                            ALU.mult).then_inc(gained, 1)

            @block.vector
            def _(dve):
                nc.vector.memset(eps[:], RMS_EPS).then_inc(ready, 1)
                for t in range(TT):
                    dve.wait_ge(squared, t + 1)
                    nc.vector.tensor_reduce(ss[:, tile(t)], sq[:, tile(t), :], axis=AX.X, op=ALU.add).then_inc(summed, 1)
                dve.wait_ge(rooted, 1)
                nc.vector.reciprocal(ss[:], ss[:]).then_inc(inverted, 1)
                dve.wait_ge(inverted, 1)
                for t in range(TT):
                    nc.vector.tensor_tensor(o3[:, tile(t), :], o3[:, tile(t), :],
                                            ss[:, tile(t)].unsqueeze(2).broadcast_to([P, H, P]), ALU.mult).then_inc(scaled, 1)
                for t in range(TT):
                    dve.wait_ge(scaled, t + 1)
                    dve.wait_ge(gained, t + 1)
                    nc.vector.tensor_tensor(o3[:, tile(t), :], o3[:, tile(t), :], z3[:, tile(t), :], ALU.mult).then_inc(gated, 1)
                dve.wait_ge(gated, TT)


class TileNorm:

    def __init__(self, nc, s, h, ln_g, ln_b):
        self.nc, self.h, self.ln_g, self.ln_b = nc, h, ln_g, ln_b
        self.gain, self.bias = s.sb("gain", [P, D]), s.sb("bias", [P, D])
        self.stats, self.mv = s.sb("stats", [P, TT, 2, 6]), s.sb("mv", [P, TT, 2])
        self.inv, self.shift, self.eps = s.sb("inv", [P, TT]), s.sb("shift", [P, TT]), s.sb("eps", [P, 1])
        self.loaded, self.own, self.measured, self.rooted, self.inverted, self.centred, self.gained, self.done = (
            s.sem(n) for n in ("norm_loaded", "own", "measured", "rooted", "inverted", "centred", "gained", "done"))

    def load(self, sp):
        sp.dma_start(self.gain[:], self.ln_g.broadcast_to([P, D])).then_inc(self.loaded, 16)
        sp.dma_start(self.bias[:], self.ln_b.broadcast_to([P, D])).then_inc(self.loaded, 16)

    def begin(self, dve):
        self.chain = Chain(dve, self.own)
        self.chain.link(self.nc.vector.memset(self.eps[:], LN_EPS))

    def stat_step(self, dve, t):
        v, h = self.nc.vector, self.h
        for half in range(2):
            last = v.bn_stats(self.stats[:, t, half, :], h[:, t, half * BANK:(half + 1) * BANK])
        self.chain.link(last)
        v.bn_aggr(self.mv[:, t, :], self.stats[:, t, :, :]).then_inc(self.measured, 1)

    def invert_step(self, dve, t):
        v, inv, at = self.nc.vector, self.inv, slice(t, t + 1)
        dve.wait_ge(self.rooted, t + 1)
        self.chain.link(v.reciprocal(inv[:, at], inv[:, at]))
        v.scalar_tensor_tensor(self.shift[:, at], self.mv[:, t, 0:1], -1.0, inv[:, at], ALU.mult, ALU.mult).then_inc(self.inverted, 1)

    def gain_step(self, dve, t):
        dve.wait_ge(self.loaded, 32)
        dve.wait_ge(self.centred, t + 1)
        self.nc.vector.tensor_tensor(self.h[:, t, :], self.h[:, t, :], self.gain[:], ALU.mult).then_inc(self.gained, 1)

    def on_act(self, act):
        for t in range(TT):
            act.wait_ge(self.measured, t + 1)
            self.nc.scalar.activation(self.inv[:, t:t + 1], self.mv[:, t, 1:2], ACT.Sqrt, bias=self.eps[:]).then_inc(self.rooted, 1)
            act.wait_ge(self.inverted, t + 1)
            self.nc.scalar.activation(self.h[:, t, :], self.h[:, t, :], ACT.Identity, bias=self.shift[:, t:t + 1],
                                      scale=self.inv[:, t:t + 1]).then_inc(self.centred, 1)

    def on_pool(self, pool):
        pool.wait_ge(self.loaded, 32)
        for t in range(TT):
            pool.wait_ge(self.gained, t + 1)
            self.nc.gpsimd.tensor_tensor(self.h[:, t, :], self.h[:, t, :], self.bias[:], ALU.add).then_inc(self.done, 1)
        pool.wait_ge(self.done, TT)


def project_out(nc, c, name, oT, w_out, h, ln_g, ln_b):
    QUARTER = D // 4
    with Stage(nc, name) as s:
        w = s.sb("w", [P, KC, D])
        bank = [s.ps(f"bank{i}", [P, BANK]) for i in range(2 * TT)]
        load = [s.sem(f"load{i}") for i in range(4)]
        made, added = s.sem("made"), s.sem("added")
        norm = TileNorm(nc, s, h, ln_g, ln_b)
        with s.block() as block:
            @block.sync
            def _(sp):
                for q in range(4):
                    at = slice(q * QUARTER, (q + 1) * QUARTER)
                    sp.dma_start(w[:, :, at], w_out.rearrange("(k p) n -> p k n", p=P)[:, :, at]).then_inc(load[q], 16)
                norm.load(sp)

            @block.tensor
            def _(pe):
                for half in range(2):
                    for t in range(TT):
                        for q in range(2):
                            if t == 0:
                                pe.wait_ge(load[2 * half + q], 16)
                            col = half * BANK + q * QUARTER
                            for k in range(KC):
                                last = nc.tensor.matmul(bank[half * TT + t][:, q * QUARTER:(q + 1) * QUARTER],
                                                        oT[:, k, t * P:(t + 1) * P], w[:, k, col:col + QUARTER],
                                                        start=(k == 0), stop=(k == KC - 1))
                        last.then_inc(made, 1)

            @block.vector
            def _(dve):
                norm.begin(dve)

                def add(half, t):
                    dve.wait_ge(made, half * TT + t + 1)
                    piece = h[:, t, half * BANK:(half + 1) * BANK]
                    nc.vector.scalar_tensor_tensor(piece, piece, ALPHA, bank[half * TT + t][:], ALU.mult, ALU.add).then_inc(added, 1)

                for t in range(TT):
                    add(0, t)
                for t in range(TT):
                    add(1, t)
                    dve.wait_ge(added, TT + t + 1)
                    norm.stat_step(dve, t)
                    norm.invert_step(dve, t)
                    if t:
                        norm.gain_step(dve, t - 1)
                norm.gain_step(dve, TT - 1)

            @block.scalar
            def _(act):
                norm.on_act(act)

            @block.gpsimd
            def _(pool):
                norm.on_pool(pool)


def normalize(nc, c, name, h, ln_g, ln_b):
    with Stage(nc, name) as s:
        norm = TileNorm(nc, s, h, ln_g, ln_b)
        with s.block() as block:
            @block.sync
            def _(sp):
                norm.load(sp)

            @block.vector
            def _(dve):
                norm.begin(dve)
                norm.stat_step(dve, 0)
                for t in range(TT):
                    if t + 1 < TT:
                        norm.stat_step(dve, t + 1)
                    norm.invert_step(dve, t)
                    if t:
                        norm.gain_step(dve, t - 1)
                norm.gain_step(dve, TT - 1)

            @block.scalar
            def _(act):
                norm.on_act(act)

            @block.gpsimd
            def _(pool):
                norm.on_pool(pool)


def gdn_layer(nc, c, h, w_in, conv_w, a_log, dt_bias, norm_g, w_out, ln_g, ln_b):
    with Stage(nc, "gdn") as s:
        o, z = s.sb("o", [P, TT, D]), s.sb("z", [P, TT, D])
        gate = {n: s.sb(n, [P, TT, GDN_HEADS]) for n in ("g", "sum", "last", "rest", "exp", "beta", "beta_exp")}
        with Stage(nc, "gdn_in") as s1:
            qkvT = s1.sb("qkvT", [P, GDN_QKV, SEQ])
            logits = s1.sb("logits", [P, TT, 2 * GDN_HEADS])
            with Stage(nc, "gdn_x") as s2:
                xTh, xTl = s2.sb("xTh", [P, KC, SEQ], F32R), s2.sb("xTl", [P, KC, SEQ], F32R)
                transpose_tokens_split(nc, c, h, xTh, xTl)
                gdn_project(nc, c, "gdnp", xTh, xTl, w_in, conv_w, qkvT, z, logits)
            gdn_normalize(nc, c, "gdnn", qkvT)
            gdn_gates(nc, c, "gdng", logits, a_log, dt_bias, gate)
            gdn_recur(nc, c, "gdnr", qkvT, gate, o)
        gdn_gate_out(nc, c, "gdno", o, z, norm_g)
        with Stage(nc, "gdn_out") as s1:
            oT = s1.sb("oT", [P, KC, SEQ])
            transpose_tokens(nc, c, o, oT)
            project_out(nc, c, "gdnq", oT, w_out, h, ln_g, ln_b)


MLA_HEADS, NOPE, ROPE, VDIM = 16, 64, 32, 64
QK = NOPE + ROPE
HALF = ROPE // 2
KV_RANK, Q_RANK = 256, 384
THETA = 10000.0
TWO_PI = 2.0 * math.pi


def parts_of(x, bits, n):
    parts = []
    for _ in range(n - 1):
        unit = 2.0 ** (math.floor(math.log2(abs(x))) + 1 - bits)
        parts.append(math.floor(x / unit) * unit)
        x -= parts[-1]
    return parts + [x]


def rope_tables(nc, c, name, positions, cos, sin):
    MAGIC = 1.5 * 2.0 ** 23
    EDGE = 3.1415925
    with Stage(nc, name) as s:
        posi, pos = s.sb("posi", [P, TT], I32), s.sb("pos", [P, TT])
        freq = s.sb("freq", [P, HALF])
        ang, turns, low = s.sb("ang", [P, TT, HALF]), s.sb("turns", [P, TT, HALF]), s.sb("low", [P, TT, HALF])
        load, chain, acted = s.sem("load"), s.sem("chain"), s.sem("acted")
        with s.block() as block:
            @block.sync
            def _(sp):
                with nc.allow_non_contiguous_dma(reason="one position per partition"):
                    sp.dma_start(posi[:], positions.rearrange("a (t p) -> p (a t)", p=P)).then_inc(load, 16)

            @block.vector
            def _(dve):
                ch = Chain(dve, chain)
                for i in range(HALF):
                    last = nc.vector.memset(freq[:, i:i + 1], THETA ** (-i / HALF))
                dve.wait_ge(load, 16)
                ch.link(nc.vector.tensor_copy(pos[:], posi[:]))
                ch.link(nc.vector.tensor_tensor(ang[:], pos[:].unsqueeze(2).broadcast_to([P, TT, HALF]),
                                                freq[:].unsqueeze(1).broadcast_to([P, TT, HALF]), ALU.mult))
                for out, quarter in ((sin, 0.0), (cos, 0.25)):
                    ch.link(nc.vector.tensor_scalar(turns[:], ang[:], 1.0 / TWO_PI, quarter, ALU.mult, ALU.add))
                    ch.link(nc.vector.tensor_scalar(turns[:], turns[:], MAGIC, None, ALU.add))
                    ch.link(nc.vector.tensor_scalar(turns[:], turns[:], MAGIC, None, ALU.subtract))
                    src = ang
                    for part in parts_of(TWO_PI, 9, 3):
                        ch.link(nc.vector.scalar_tensor_tensor(low[:], turns[:], -part, src[:], ALU.mult, ALU.add))
                        src = low
                    ch.link(nc.vector.tensor_scalar(low[:], low[:], quarter * TWO_PI, EDGE, ALU.add, ALU.min))
                    ch.link(nc.vector.tensor_scalar(out[:], low[:], -EDGE, None, ALU.max))

            @block.scalar
            def _(act):
                act.wait_ge(chain, 2 + 8)
                nc.scalar.activation(sin[:], sin[:], ACT.Sin).then_inc(acted, 1)
                act.wait_ge(chain, 2 + 16)
                nc.scalar.activation(cos[:], cos[:], ACT.Sin).then_inc(acted, 1)
                act.wait_ge(acted, 2)


def mla_project(nc, c, name, hT, w_kv_a, kv_norm_g, w_uk, w_uv, w_qa, q_norm_g, w_qb, cos, sin, q, k, v):
    KV = KV_RANK + ROPE
    with Stage(nc, name) as s:
        wkv, wqa = s.sb("wkv", [P, KC, KV]), s.sb("wqa", [P, KC, Q_RANK])
        wuk, wuv = s.sb("wuk", [P, KV_RANK // P, D]), s.sb("wuv", [P, KV_RANK // P, D])
        wqb = s.sb("wqb", [P, Q_RANK // P, MLA_HEADS * QK])
        gkv, gq = s.sb("gkv", [P, KV_RANK]), s.sb("gq", [P, Q_RANK])
        kv, qa = s.sb("kv", [P, TT, KV]), s.sb("qa", [P, TT, Q_RANK])
        sq = s.sb("sq", [P, TT, Q_RANK])
        ss, sr, eps = s.sb("ss", [P, TT]), s.sb("sr", [P, TT]), s.sb("eps", [P, 1])
        kvT, qaT = s.sb("kvT", [P, KV_RANK // P, SEQ]), s.sb("qaT", [P, Q_RANK // P, SEQ])
        kr = s.sb("kr", [P, TT, ROPE])
        tmp = [sq[:, :, 0:MLA_HEADS * HALF].rearrange("p t (h d) -> p t h d", d=HALF), s.sb("tmp", [P, TT, MLA_HEADS, HALF])[:]]
        bank = [s.ps(f"bank{i}", [P, BANK]) for i in range(4)]
        load = [s.sem(f"load{i}") for i in range(4)]
        made, taken, chain, rooted = s.sem("made"), s.sem("taken"), s.sem("chain"), s.sem("rooted")
        kvready, qaready = s.sem("kvready"), s.sem("qaready")
        rows = lambda w: w.rearrange("(k p) n -> p k n", p=P)
        with s.block() as block:
            @block.sync
            def _(sp):
                sp.dma_start(wkv[:], rows(w_kv_a)).then_inc(load[0], 16)
                sp.dma_start(wqa[:], rows(w_qa)).then_inc(load[1], 16)
                sp.dma_start(gkv[:], kv_norm_g.unsqueeze(0).broadcast_to([P, KV_RANK])).then_inc(load[2], 16)
                sp.dma_start(gq[:], q_norm_g.broadcast_to([P, Q_RANK])).then_inc(load[2], 16)
                sp.dma_start(wuk[:], rows(w_uk)).then_inc(load[3], 16)
                sp.dma_start(wuv[:], rows(w_uv)).then_inc(load[3], 16)
                sp.dma_start(wqb[:], rows(w_qb)).then_inc(load[3], 16)

            NT = (KV_RANK + Q_RANK) // P
            up = [("k", b) for b in range(2)] + [("v", b) for b in range(2)] + [("q", b) for b in range(3)]

            @block.tensor
            def _(pe):
                n = 0

                def slot():
                    if n >= 4:
                        pe.wait_ge(taken, n - 3)
                    return bank[n % 4]

                for w, width, sem in ((wkv, KV, load[0]), (wqa, Q_RANK, load[1])):
                    pe.wait_ge(sem, 16)
                    for t in range(TT):
                        out = slot()
                        for kc in range(KC):
                            last = nc.tensor.matmul(out[:, 0:width], hT[:, kc, t * P:(t + 1) * P], w[:, kc, :],
                                                    start=(kc == 0), stop=(kc == KC - 1))
                        last.then_inc(made, 1)
                        n += 1
                for src, chunks, ready in ((kv, KV_RANK // P, kvready), (qa, Q_RANK // P, qaready)):
                    pe.wait_ge(ready, 1)
                    for kc in range(chunks):
                        out = slot()
                        for t in range(TT):
                            last = nc.tensor.transpose(out[:, t * P:(t + 1) * P], src[:, t, kc * P:(kc + 1) * P], c["ident"][:])
                        last.then_inc(made, 1)
                        n += 1
                pe.wait_ge(load[3], 48)
                pe.wait_ge(taken, n)
                for t in range(TT):
                    for what, b in up:
                        srcT, w = {"k": (kvT, wuk), "v": (kvT, wuv), "q": (qaT, wqb)}[what]
                        chunks = srcT.shape[1]
                        out = slot()
                        for kc in range(chunks):
                            last = nc.tensor.matmul(out[:], srcT[:, kc, t * P:(t + 1) * P], w[:, kc, b * BANK:(b + 1) * BANK],
                                                    start=(kc == 0), stop=(kc == chunks - 1))
                        last.then_inc(made, 1)
                        n += 1

            @block.scalar
            def _(act):
                n = 0
                for dst, width in ((kv, KV), (qa, Q_RANK)):
                    for t in range(TT):
                        act.wait_ge(made, n + 1)
                        nc.scalar.copy(dst[:, t, :], bank[n % 4][:, 0:width]).then_inc(taken, 1)
                        n += 1
                for done in (3, 8):
                    act.wait_ge(chain, done)
                    width = KV_RANK if done == 3 else Q_RANK
                    nc.scalar.activation(sr[:], ss[:], ACT.Sqrt, bias=eps[:], scale=1.0 / width).then_inc(rooted, 1)
                for dstT in (kvT, qaT):
                    for kc in range(dstT.shape[1]):
                        act.wait_ge(made, n + 1)
                        nc.scalar.copy(dstT[:, kc, :], bank[n % 4][:]).then_inc(taken, 1)
                        n += 1
                for t in range(TT):
                    for what, b in up:
                        act.wait_ge(made, n + 1)
                        if what == "k":
                            dst = k[:, t, 8 * b:8 * b + 8, 0:NOPE]
                            src = bank[n % 4][:].rearrange("p (h d) -> p h d", d=NOPE)
                        else:
                            flat = v[:, t, :] if what == "v" else q[:, t].rearrange("p h d -> p (h d)")
                            dst, src = flat[:, b * BANK:(b + 1) * BANK], bank[n % 4][:]
                        nc.scalar.copy(dst, src).then_inc(taken, 1)
                        n += 1

            @block.vector
            def _(dve):
                ch = Chain(dve, chain)
                ch.link(nc.vector.memset(eps[:], RMS_EPS))
                n = 0
                for at, (m, width, g, ready) in enumerate(((kv, KV_RANK, gkv, kvready), (qa, Q_RANK, gq, qaready))):
                    x = m[:, :, 0:width]
                    dve.wait_ge(taken, TT * (at + 1))
                    ch.link(nc.vector.tensor_tensor(sq[:, :, 0:width], x, x, ALU.mult))
                    ch.link(nc.vector.tensor_reduce(ss[:], sq[:, :, 0:width], axis=AX.X, op=ALU.add))
                    dve.wait_ge(rooted, at + 1)
                    ch.link(nc.vector.reciprocal(sr[:], sr[:]))
                    ch.link(nc.vector.tensor_tensor(x, x, sr[:].unsqueeze(2).broadcast_to([P, TT, width]), ALU.mult))
                    dve.wait_ge(load[2], 32)
                    last = nc.vector.tensor_tensor(x, x, g[:].unsqueeze(1).broadcast_to([P, TT, width]), ALU.mult)
                    last.then_inc(ready, 1)
                    if at == 0:
                        ch.link(nc.vector.memset(ss[:, 0:1], 0.0))

                def rotate(out, x, heads):
                    cs = cos[:].unsqueeze(2).broadcast_to([P, TT, heads, HALF])
                    sn = sin[:].unsqueeze(2).broadcast_to([P, TT, heads, HALF])
                    x1, x2 = x[:, :, :, 0:HALF], x[:, :, :, HALF:ROPE]
                    a, b = tmp[0][:, :, 0:heads, :], tmp[1][:, :, 0:heads, :]
                    nc.vector.tensor_tensor(a, x2, sn, ALU.mult)
                    ch.link(nc.vector.tensor_tensor(b, x1, sn, ALU.mult))
                    nc.vector.tensor_tensor(out[:, :, :, 0:HALF], x1, cs, ALU.mult)
                    ch.link(nc.vector.tensor_tensor(out[:, :, :, HALF:ROPE], x2, cs, ALU.mult))
                    nc.vector.tensor_tensor(out[:, :, :, 0:HALF], out[:, :, :, 0:HALF], a, ALU.subtract)
                    ch.link(nc.vector.tensor_tensor(out[:, :, :, HALF:ROPE], out[:, :, :, HALF:ROPE], b, ALU.add))

                rotate(kr[:].unsqueeze(2), kv[:, :, KV_RANK:].unsqueeze(2), 1)
                ch.link(nc.vector.tensor_copy(k[:, :, :, NOPE:], kr[:].unsqueeze(2).broadcast_to([P, TT, MLA_HEADS, ROPE])))
                dve.wait_ge(taken, 2 * TT + NT + TT * len(up))
                rotate(q[:, :, :, NOPE:], q[:, :, :, NOPE:], MLA_HEADS)


def mla_attend(nc, c, name, q, k, v, o):
    G = 2
    SCALE = QK ** -0.5
    PE_STEPS = Steps("qT kT s3 s0 s2 s1 p3 p02 p1 o", G)
    ACT_STEPS = Steps("qs ks qT e3 e0 e2 e1 p3", G)
    DVE_STEPS = Steps("kT x3 x0 x2 x1 nb p02 p1 rr o", G)
    with Stage(nc, name) as s:
        far = s.sb("far", [P, P])
        qs, ks = ([s.sb(f"{n}{j}", [P, TT, QK]) for j in range(G)] for n in ("qs", "ks"))
        qT, kT = ([s.sb(f"{n}{j}", [P, SEQ]) for j in range(G)] for n in ("qT", "kT"))
        prob = [[s.sb(f"prob{j}_{i}", [P, (i + 1) * P]) for i in range(TT)] for j in range(G)]
        probT = [[s.sb(f"probT{j}_{i}", [P, i + 1, P]) for i in range(TT)] for j in range(G)]
        mx, nb, rs = ([s.sb(f"{n}{j}", [P, TT]) for j in range(G)] for n in ("mx", "nb", "rs"))
        A, B, Cb, E = ([s.ps(f"{n}{j}", [P, BANK]) for j in range(G)] for n in ("A", "B", "C", "E"))
        pe_done, act_done, dve_done, masked = s.sem("pe_done"), s.sem("act_done"), s.sem("dve_done"), s.sem("masked")
        spot = {3: (A, 0), 0: (B, 0), 2: (B, P), 1: (Cb, 0)}

        def score(i, j):
            m, at = spot[i]
            return m[j][:, at:at + (i + 1) * P]

        with s.block() as block:
            @block.tensor
            def _(pe):
                pe.wait_ge(masked, 1)
                starts_at_one(pe, pe_done)
                with pe.Fori(0, MLA_HEADS // G) as r:
                    def act_at(step, j):
                        pe.wait_ge(act_done, ACT_STEPS.after(r, step, j))

                    def dve_at(step, j):
                        pe.wait_ge(dve_done, DVE_STEPS.after(r, step, j))

                    for src, dst, step in ((qs, E, "qs"), (ks, A, "ks")):
                        for j in range(G):
                            act_at(step, j)
                            for t in range(TT):
                                last = nc.tensor.transpose(dst[j][0:QK, t * P:(t + 1) * P], src[j][:, t, :], c["ident"][:])
                            last.then_inc(pe_done, 1)
                    for i in (3, 0, 2, 1):
                        for j in range(G):
                            if i == 3:
                                act_at("qT", j)
                                dve_at("kT", j)
                            sc = score(i, j)
                            nc.tensor.matmul(sc, qT[j][0:QK, i * P:(i + 1) * P], kT[j][0:QK, 0:(i + 1) * P], start=True, stop=False)
                            nc.tensor.matmul(sc[:, i * P:], c["ident"][:], far[:], start=False, stop=True).then_inc(pe_done, 1)
                    for step, dst, tiles, ready in (("p3", A, (3,), "e3"), ("p02", B, (0, 2), "e2"), ("p1", E, (1,), "e1")):
                        for j in range(G):
                            act_at(ready, j)
                            col = 0
                            for i in tiles:
                                for kt in range(i + 1):
                                    last = nc.tensor.transpose(dst[j][:, col:col + P], prob[j][i][:, kt * P:(kt + 1) * P], c["ident"][:])
                                    col += P
                            last.then_inc(pe_done, 1)
                    for j in range(G):
                        act_at("p3", j)
                        dve_at("p1", j)
                        for i in range(TT):
                            for kt in range(i + 1):
                                last = nc.tensor.matmul(Cb[j][:, 256 + i * VDIM:256 + (i + 1) * VDIM], probT[j][i][:, kt, :],
                                                        v[:, kt, bass.ds((r * G + j) * VDIM, VDIM)], start=(kt == 0), stop=(kt == i))
                        last.then_inc(pe_done, 1)

            @block.scalar
            def _(act):
                starts_at_one(act, act_done)
                with act.Fori(0, MLA_HEADS // G) as r:
                    def pe_at(step, j):
                        act.wait_ge(pe_done, PE_STEPS.after(r, step, j))

                    for dst, src in ((qs, q), (ks, k)):
                        for j in range(G):
                            act.wait_ge(pe_done, PE_STEPS.rounds(r))
                            nc.scalar.copy(dst[j][:].unsqueeze(2), src[:, :, bass.ds(r * G + j, 1), :]).then_inc(act_done, 1)
                    for j in range(G):
                        pe_at("qT", j)
                        nc.scalar.copy(qT[j][0:QK, :], E[j][0:QK, :]).then_inc(act_done, 1)
                    for i in (3, 0, 2, 1):
                        for j in range(G):
                            if i == 3:
                                act.wait_ge(dve_done, DVE_STEPS.after(r, "nb", j))
                            nc.scalar.activation(prob[j][i][:], score(i, j), ACT.Exp, bias=nb[j][:, i:i + 1], scale=SCALE,
                                                 accum_out=rs[j][:, i:i + 1]).then_inc(act_done, 1)
                    for j in range(G):
                        pe_at("p3", j)
                        nc.scalar.copy(probT[j][3][:].rearrange("p k q -> p (k q)"), A[j][:]).then_inc(act_done, 1)

            @block.vector
            def _(dve):
                nc.vector.tensor_scalar(far[:], c["lower"][:], -1.0, 1.0e30, ALU.add, ALU.mult).then_inc(masked, 1)
                starts_at_one(dve, dve_done)
                with dve.Fori(0, MLA_HEADS // G) as r:
                    def pe_at(step, j):
                        dve.wait_ge(pe_done, PE_STEPS.after(r, step, j))

                    for j in range(G):
                        pe_at("kT", j)
                        nc.vector.tensor_copy(kT[j][0:QK, :], A[j][0:QK, :]).then_inc(dve_done, 1)
                    for i in (3, 0, 2, 1):
                        for j in range(G):
                            pe_at("s2" if i == 0 else f"s{i}", j)
                            nc.vector.tensor_reduce(mx[j][:, i:i + 1], score(i, j), axis=AX.X, op=ALU.max).then_inc(dve_done, 1)
                    for j in range(G):
                        dve.wait_ge(dve_done, DVE_STEPS.after(r, "x1", j))
                        nc.vector.tensor_scalar(nb[j][:], mx[j][:], -SCALE, None, ALU.mult).then_inc(dve_done, 1)
                    for j in range(G):
                        pe_at("p02", j)
                        nc.vector.tensor_copy(probT[j][0][:, 0, :], B[j][:, 0:P])
                        nc.vector.tensor_copy(probT[j][2][:].rearrange("p k q -> p (k q)"), B[j][:, P:]).then_inc(dve_done, 1)
                    for j in range(G):
                        pe_at("p1", j)
                        nc.vector.tensor_copy(probT[j][1][:].rearrange("p k q -> p (k q)"), E[j][:, 0:2 * P]).then_inc(dve_done, 1)
                    for j in range(G):
                        dve.wait_ge(act_done, ACT_STEPS.after(r, "e1", j))
                        nc.vector.reciprocal(rs[j][:], rs[j][:]).then_inc(dve_done, 1)
                    for j in range(G):
                        pe_at("o", j)
                        dve.wait_ge(dve_done, DVE_STEPS.after(r, "rr", j))
                        nc.vector.tensor_tensor(o[:, :, bass.ds((r * G + j) * VDIM, VDIM)],
                                                Cb[j][:, 256:].rearrange("p (t d) -> p t d", d=VDIM),
                                                rs[j][:].unsqueeze(2).broadcast_to([P, TT, VDIM]), ALU.mult).then_inc(dve_done, 1)
                dve.wait_ge(dve_done, DVE_STEPS.rounds(MLA_HEADS // G))


def mla_layer(nc, c, h, hT, positions, w_kv_a, kv_norm_g, w_uk, w_uv, w_qa, q_norm_g, w_qb, w_out, ln_g, ln_b):
    with Stage(nc, "mla") as s:
        v = s.sb("v", [P, TT, MLA_HEADS * VDIM])
        o = s.sb("o", [P, TT, MLA_HEADS * VDIM])
        with Stage(nc, "mla_in") as s1:
            q, k = (s1.sb(n, [P, TT, MLA_HEADS, QK]) for n in ("q", "k"))
            cos, sin = (s1.sb(n, [P, TT, HALF]) for n in ("cos", "sin"))
            rope_tables(nc, c, "mlar", positions, cos, sin)
            mla_project(nc, c, "mlap", hT, w_kv_a, kv_norm_g, w_uk, w_uv, w_qa, q_norm_g, w_qb, cos, sin, q, k, v)
            mla_attend(nc, c, "mlaa", q, k, v, o)
        with Stage(nc, "mla_out") as s1:
            oT = s1.sb("oT", [P, KC, SEQ])
            transpose_tokens(nc, c, o, oT)
            project_out(nc, c, "mlaq", oT, w_out, h, ln_g, ln_b)


def peer_layer(nc, c, name, h, w_q, sub_keys, u_tab, v_tab, gates, early):
    with Stage(nc, f"{name}h") as s:
        hTh, hTl = s.sb("hTh", [P, KC, SEQ], F32R), s.sb("hTl", [P, KC, SEQ], F32R)
        transpose_tokens_split(nc, c, h, hTh, hTl)
        with Stage(nc, f"{name}k") as s1:
            giT = s1.sb("giT", [P, 3, SEQ])
            peer_select(nc, c, f"{name}s", hTh, hTl, w_q, sub_keys, giT, u_tab, early)
            peer_gates(nc, c, f"{name}g", h, giT, gates, hTh, hTl, u_tab, early)
        peer_experts(nc, c, f"{name}e", hTh, hTl, h, u_tab, v_tab, gates, early)


def yoco_trunk(nc, x, positions, a_w_in, a_conv_w, a_a_log, a_dt_bias, a_norm_g, a_w_out, kv_w_a, kv_norm_g, kv_w_uk,
               kv_w_uv, b_w_qa, b_q_norm_g, b_w_qb, b_w_out, peer_w_q, peer_sub_keys, peer_u, peer_v, ln_g, ln_b, out):
    gates = nc.dram_tensor("gates", [P, GRIDS, NKEYS, GRID], F32).ap()
    early = nc.dram_tensor("early", [EARLY, P, SEQ], F32).ap()
    tokens = lambda ap: ap.rearrange("a (t p) d -> p (a t) d", p=P)
    with Stage(nc, "trunk") as s:
        c = {n: s.sb(n, [P, P]) for n in ("ident", "ones", "upper", "lower", "strict", "block16", "iota")}
        h = s.sb("h", [P, TT, D])
        load, stored = s.sem("load"), s.sem("stored")
        make_constants(nc, c)
        with s.block() as block:
            @block.sync
            def _(sp):
                sp.dma_start(h[:], tokens(x)).then_inc(load, 16)
                sp.wait_ge(load, 16)
        gdn_layer(nc, c, h, a_w_in[0], a_conv_w[0], a_a_log, a_dt_bias, a_norm_g, a_w_out[0],
                  ln_g[0, 0:1], ln_b[0, 0:1])
        peer_layer(nc, c, "p0", h, peer_w_q[0], peer_sub_keys[0], peer_u[0], peer_v[0], gates, early)
        normalize(nc, c, "ln01", h, ln_g[0, 1:2], ln_b[0, 1:2])
        with Stage(nc, "cross") as s0:
            hT = s0.sb("hT", [P, KC, SEQ])
            transpose_tokens(nc, c, h, hT)
            mla_layer(nc, c, h, hT, positions, kv_w_a, kv_norm_g, kv_w_uk, kv_w_uv, b_w_qa[0], b_q_norm_g, b_w_qb[0], b_w_out[0],
                      ln_g[1, 0:1], ln_b[1, 0:1])
        peer_layer(nc, c, "p1", h, peer_w_q[1], peer_sub_keys[1], peer_u[1], peer_v[1], gates, early)
        normalize(nc, c, "ln11", h, ln_g[1, 1:2], ln_b[1, 1:2])
        with s.block() as block:
            @block.sync
            def _(sp):
                sp.dma_start(tokens(out), h[:]).then_inc(stored, 16)
                sp.wait_ge(stored, 16)


_INS = ["x", "positions", "a_w_in", "a_conv_w", "a_a_log", "a_dt_bias", "a_norm_g", "a_w_out", "kv_w_a", "kv_norm_g",
        "kv_w_uk", "kv_w_uv", "b_w_qa", "b_q_norm_g", "b_w_qb", "b_w_out", "peer_w_q", "peer_sub_keys", "peer_u",
        "peer_v", "ln_g", "ln_b"]


def kernel(**inputs):
    import numpy as _np
    import concourse.bacc as _bacc
    from concourse import mybir as _mybir
    from concourse.bass_utils import run_bass_kernel_spmd as _run

    nc = _bacc.Bacc("TRN2", target_bir_lowering=False, num_devices=1)
    arrays, args = {}, []
    for name in _INS:
        a = _np.ascontiguousarray(inputs[name])
        arrays[f"in_{name}_dram"] = a
        args.append(nc.dram_tensor(f"in_{name}_dram", a.shape, _mybir.dt.from_np(a.dtype), kind="ExternalInput").ap())
    args.append(nc.dram_tensor("out_dram", (1, SEQ, D), _mybir.dt.float32, kind="ExternalOutput").ap())
    yoco_trunk(nc, *args)
    r = _run(nc, [arrays], core_ids=[0])
    return r.results[0]["out_dram"]
```

```python
import math
from contextlib import ExitStack

import concourse.bass as bass
import concourse.mybir as mybir

F32 = mybir.dt.float32
F32R = mybir.dt.float32r
U32 = mybir.dt.uint32
I32 = mybir.dt.int32
ALU = mybir.AluOpType
ACT = mybir.ActivationFunctionType
AX = mybir.AxisListType

P = 128
SEQ = 512
TT = SEQ // P
D = 1024
KC = D // P
BANK = 512
HALVES = D // BANK
DEPTH = 2
ALPHA = (2 * DEPTH) ** 0.25
LN_EPS = 1e-5
RMS_EPS = 1e-6

HEADS = 8
NKEYS = 128
TOPK = 16
SETS = 2 * HEADS
NEG = -3.0e38
EARLY_TILE = 6
EARLY_SELECT = TT * EARLY_TILE
GRID = 64
GRIDS = SEQ // GRID
EARLY = EARLY_SELECT + GRIDS


class Chain:

    def __init__(self, eng, sem, before=0, alone=None):
        self.eng, self.sem, self.before, self.count, self.alone = eng, sem, before, 0, alone

    def link(self, ins):
        self.count += 1
        ins.then_inc(self.sem, 1)
        self.eng.wait_ge(self.sem, self.before + self.count)
        if self.alone is not None:
            self.eng.sem_inc(self.alone, 1)

    def end(self, count):
        assert self.count == count, self.count


def starts_at_one(eng, *sems):
    for sem in sems:
        eng.sem_inc(sem, 1)


class Stage:

    def __init__(self, nc, name):
        self.nc, self.name, self.ctx, self.sems = nc, name, ExitStack(), []

    def __enter__(self):
        self.ctx.__enter__()
        return self

    def __exit__(self, *e):
        if self.sems:
            self.nc.clear_and_free_semaphores(self.sems)
            self.nc.all_engine_barrier()
        return self.ctx.__exit__(*e)

    def sb(self, name, shape, dt=F32):
        return self.ctx.enter_context(self.nc.sbuf_tensor(f"{self.name}_{name}", shape, dt))

    def ps(self, name, shape, dt=F32):
        return self.ctx.enter_context(self.nc.psum_tensor(f"{self.name}_{name}", shape, dt))

    def sem(self, name):
        self.sems.append(self.nc.alloc_semaphore(name=f"{self.name}_{name}"))
        return self.sems[-1]

    def block(self):
        return self.nc.Block()


def make_constants(nc, c, h, x):
    with Stage(nc, "const") as s:
        zeroed, made, itoa, copied = s.sem("zeroed"), s.sem("made"), s.sem("iota"), s.sem("copied")
        load = s.sem("load")
        iota_i = s.sb("iota_i", [P, P], I32)
        with s.block() as block:
            @block.sync
            def _(sp):
                sp.dma_start(h[:], x).then_inc(load, 16)
                sp.wait_ge(load, 16)

            @block.gpsimd
            def _(pool):
                nc.gpsimd.memset(c["ident"][:], 0.0).then_inc(zeroed, 1)
                nc.gpsimd.memset(c["ones"][:], 1.0).then_inc(zeroed, 1)
                nc.gpsimd.iota(iota_i[:], pattern=[[1, P]], base=0, channel_multiplier=0).then_inc(itoa, 1)
                pool.wait_ge(zeroed, 2)
                nc.gpsimd.affine_select(out=c["ident"][:], in_=c["ident"][:], compare_op=ALU.not_equal, fill=1.0,
                                        base=0, pattern=[[-1, P]], channel_multiplier=1).then_inc(made, 1)
                nc.gpsimd.affine_select(out=c["upper"][:], in_=c["ones"][:], compare_op=ALU.is_ge, fill=0.0,
                                        base=0, pattern=[[1, P]], channel_multiplier=-1).then_inc(made, 1)
                nc.gpsimd.affine_select(out=c["lower"][:], in_=c["ones"][:], compare_op=ALU.is_ge, fill=0.0,
                                        base=0, pattern=[[-1, P]], channel_multiplier=1).then_inc(made, 1)
                nc.gpsimd.affine_select(out=c["strict"][:], in_=c["ones"][:], compare_op=ALU.is_gt, fill=0.0,
                                        base=0, pattern=[[-1, P]], channel_multiplier=1).then_inc(made, 1)
                nc.gpsimd.affine_select(out=c["block16"][:].rearrange("p (b j) -> p b j", j=16),
                                        in_=c["ones"][:].rearrange("p (b j) -> p b j", j=16),
                                        compare_op=ALU.is_ge, fill=0.0,
                                        base=0, pattern=[[-16, P // 16], [0, 16]], channel_multiplier=1).then_inc(made, 1)
                pool.wait_ge(made, 5)
                nc.gpsimd.affine_select(out=c["block16"][:].rearrange("p (b j) -> p b j", j=16),
                                        in_=c["block16"][:].rearrange("p (b j) -> p b j", j=16),
                                        compare_op=ALU.is_ge, fill=0.0,
                                        base=15, pattern=[[16, P // 16], [0, 16]], channel_multiplier=-1).then_inc(made, 1)

            @block.vector
            def _(dve):
                dve.wait_ge(itoa, 1)
                nc.vector.tensor_copy(c["iota"][:], iota_i[:]).then_inc(copied, 1)
                dve.wait_ge(made, 6)
                dve.wait_ge(copied, 1)


class SplitTranspose:

    def __init__(self, nc, s, c, h, hTh, hTl, bank):
        self.nc, self.c, self.h, self.hTh, self.hTl, self.bank = nc, c, h, hTh, hTl, bank
        self.flipped, self.high, self.low = s.sem("flipped"), s.sem("hT_high"), s.sem("hT_low")

    def on_pe(self, pe):
        for k in range(KC):
            if k >= 4:
                pe.wait_ge(self.low, k - 3)
            for t in range(TT):
                last = self.nc.tensor.transpose(self.bank[k % 4][:, t * P:(t + 1) * P], self.h[:, t, k * P:(k + 1) * P],
                                                self.c["ident"][:])
            last.then_inc(self.flipped, 1)

    def finished(self, pe):
        pe.wait_ge(self.low, KC)

    def on_act(self, act):
        for k in range(KC):
            act.wait_ge(self.flipped, k + 1)
            self.nc.scalar.copy(self.hTh[:, k, :], self.bank[k % 4][:]).then_inc(self.high, 1)

    def on_dve(self, dve):
        for k in range(KC):
            dve.wait_ge(self.high, k + 1)
            self.nc.vector.tensor_tensor(self.hTl[:, k, :], self.bank[k % 4][:], self.hTh[:, k, :].bitcast(F32),
                                         ALU.subtract).then_inc(self.low, 1)


SLAB = 256
SLAB_TILES = SLAB // P


class Slabs:

    def __init__(self, nc, s, view, used, share=SLAB_TILES):
        self.nc, self.view, self.used, self.share = nc, view, used, share
        self.raw = [s.sb(f"raw{i}", [P, KC, SLAB]) for i in range(2)]
        self.high = [s.sb(f"high{i}", [P, KC, SLAB], F32R) for i in range(2)]
        self.low = [s.sb(f"low{i}", [P, KC, SLAB], F32R) for i in range(2)]
        self.loaded = [s.sem("loaded0"), s.sem("loaded1")]
        self.high_ready, self.low_ready = s.sem("high_ready"), s.sem("low_ready")

    def load(self, sp, base, n):
        sp.wait_ge(self.low_ready, base + n + 1)
        at = base + n
        src = self.view[at] if isinstance(at, int) else self.view[bass.ds(at, 1)]
        sp.dma_start(self.raw[n % 2][:], src).then_inc(self.loaded[n % 2], 16)

    def split_high(self, act, base, n, half_base):
        act.wait_ge(self.loaded[n % 2], 16 * (half_base + n // 2 + 1))
        act.wait_ge(self.used, (base + n) * self.share + self.share)
        flat = lambda ap: ap.rearrange("p k n -> p (k n)")
        self.nc.scalar.copy(flat(self.high[n % 2][:]), flat(self.raw[n % 2][:])).then_inc(self.high_ready, 1)

    def split_low(self, pool, base, n):
        pool.wait_ge(self.high_ready, base + n + 1)
        flat = lambda ap: ap.rearrange("p k n -> p (k n)")
        self.nc.gpsimd.tensor_tensor(flat(self.low[n % 2][:]), flat(self.raw[n % 2][:]), flat(self.high[n % 2][:]).bitcast(F32),
                                     ALU.subtract).then_inc(self.low_ready, 1)

    def wait(self, pe, base, n):
        pe.wait_ge(self.low_ready, base + n + 3)

    def columns(self, nc, out, n, tile, xTh, xTl):
        at = slice(tile * P, (tile + 1) * P)
        for k in range(KC):
            for m, (w, x) in enumerate(((self.high, xTh), (self.high, xTl), (self.low, xTh))):
                last = nc.tensor.matmul(out, w[n % 2][:, k, at], x[:, k, :], start=(k == 0 and m == 0), stop=(k == KC - 1 and m == 2))
        return last

    def tokens(self, nc, out, n, t, xTh, xTl):
        at = slice(t * P, (t + 1) * P)
        for k in range(KC):
            for m, (x, w) in enumerate(((xTh, self.high), (xTh, self.low), (xTl, self.high))):
                last = nc.tensor.matmul(out, x[:, k, at], w[n % 2][:, k, :], start=(k == 0 and m == 0), stop=(k == KC - 1 and m == 2))
        return last


def peer_select(nc, c, name, h, hTh, hTl, w_q, sub_keys, giT, u_tab, early):
    ROUND_SLABS = 4
    ROUNDS = SETS // (ROUND_SLABS * SLAB_TILES)
    with Stage(nc, name) as s:
        keys = s.sb("keys", [P, SETS, P])
        keysT = s.sb("keysT", [P, SETS, P])
        qT = [s.sb(f"qT{i}", [P, SEQ]) for i in range(2)]
        masked = s.sb("masked", [P, TT, NKEYS])
        best = s.sb("best", [P, TT, TOPK])
        besti = s.sb("besti", [P, TT, TOPK], U32)
        val = s.sb("val", [P, SETS, TT, TOPK])
        num = s.sb("num", [P, SETS, TT, TOPK])
        cand = s.sb("cand", [P, HEADS, TOPK * TOPK])
        candm = s.sb("candm", [P, HEADS, TOPK * TOPK])
        top = s.sb("top", [P, HEADS, TOPK])
        topi = s.sb("topi", [P, HEADS, TOPK], U32)
        digit = s.sb("digit", [P, HEADS * TOPK], U32)
        digitf = s.sb("digitf", [P, HEADS * TOPK])
        valt = s.sb("valt", [P, SETS, TOPK])
        numt = s.sb("numt", [P, SETS, TOPK])
        hot = s.sb("hot", [P, HEADS, TOPK * TOPK])
        mass = s.sb("mass", [P, HEADS])
        picks = s.sb("picks", [P, 3, HEADS * TOPK])
        load_k, kflip, ktaken = s.sem("load_k"), s.sem("kflip"), s.sem("ktaken")
        projected, qready, scored, ranked = s.sem("projected"), s.sem("qready"), s.sem("scored"), s.sem("ranked")
        chain, passed = s.sem("chain"), s.sem("passed")
        logits, expd, picked, turned, done = s.sem("logits"), s.sem("expd"), s.sem("picked"), s.sem("turned"), s.sem("done")
        qps = [s.ps(f"qps{i}", [P, SEQ]) for i in range(2)]
        sps = [s.ps(f"sps{i}", [P, TT, NKEYS]) for i in range(2)]
        tps = s.ps("tps", [P, 4, P])
        gps = s.ps("gps", [P, 3, P])
        slabs = Slabs(nc, s, w_q.rearrange("(k p) (s n) -> s p k n", p=P, n=SLAB), projected)
        ROUND1 = ROUND_SLABS * SLAB_TILES
        RING = 2
        u, uT = ([raw[:].rearrange("p k n -> p (k n)")[:, a * D:(a + 1) * D] for a in range(2)] for raw in slabs.raw)
        uTh, uTl = ([part[:, :, 0:P] for part in parts] for parts in (slabs.high, slabs.low))
        hps = qps
        ups = [s.ps(f"ups{i}", [P, BANK]) for i in range(2)]
        turn = SplitTranspose(nc, s, c, h, hTh, hTl, ups + qps)
        gel = [s.sb(f"gel{i}", [P, SEQ]) for i in range(2)]
        load_u = [s.sem(f"load_u{i}") for i in range(RING)]
        kept = [s.sem(f"kept{i}") for i in range(2)]
        u_flip, u_turned, u_high, u_low = (s.sem(n) for n in ("u_flip", "u_turned", "u_high", "u_low"))
        hid, gelued = s.sem("hid"), s.sem("gelued")
        u_v = u_tab.rearrange("(b p) d -> b p d", p=P)
        with s.block() as block:
            @block.sync
            def _(sp):
                with sp.Fori(0, ROUNDS) as i:
                    for n in range(ROUND_SLABS):
                        slabs.load(sp, i * ROUND_SLABS, n)
                sp.wait_ge(slabs.low_ready, ROUNDS * ROUND_SLABS + 2)

                def load(i, b):
                    sp.wait_ge(u_flip, i * (2 * EARLY_TILE) + 2 * b + 2)
                    sp.dma_start(u[b % RING], u_v[bass.ds(i * EARLY_TILE + b, 1)]).then_inc(load_u[b % RING], 16)

                load(0, 0)
                with sp.Fori(0, TT) as i:
                    for b in range(EARLY_TILE):
                        load(i, b + 1)

            @block.gpsimd
            def _(pool):
                pool.sem_inc(slabs.low_ready, 2)
                with pool.Fori(0, ROUNDS) as i:
                    for n in range(ROUND_SLABS):
                        slabs.split_low(pool, i * ROUND_SLABS, n)
                pool.sem_inc(u_low, 2)

                def split_low(i, b):
                    pool.wait_ge(u_high, i * EARLY_TILE + b + 1)
                    pool.wait_ge(hid, i * EARLY_TILE + b + 1)
                    nc.gpsimd.tensor_tensor(uTl[b % 2], uT[b % 2].rearrange("p (k n) -> p k n", n=P),
                                            uTh[b % 2].bitcast(F32), ALU.subtract).then_inc(u_low, 1)

                split_low(0, 0)
                with pool.Fori(0, TT) as i:
                    for b in range(EARLY_TILE):
                        split_low(i, b + 1)

            @block.tensor
            def _(pe):
                pe.sem_inc(projected, 2 * SLAB_TILES)
                pe.sem_inc(u_flip, 2 * RING)
                starts_at_one(pe, turned)
                turn.on_pe(pe)
                pe.wait_ge(load_k, 16)
                for q in range(SETS // 4):
                    if q:
                        pe.wait_ge(ktaken, q)
                    for j in range(4):
                        last = nc.tensor.transpose(tps[:, j, :], keys[:, 4 * q + j, :], c["ident"][:])
                    last.then_inc(kflip, 1)
                pe.wait_ge(ktaken, SETS // 4)
                turn.finished(pe)
                with pe.Fori(0, ROUNDS) as i:
                    def score(n):
                        pe.wait_ge(qready, i * ROUND1 + n + 1)
                        pe.wait_ge(ranked, i * ROUND1 + n + 1)
                        for t in range(TT):
                            last = nc.tensor.matmul(sps[n % 2][:, t, :], qT[n % 2][:, t * P:(t + 1) * P],
                                                    keysT[:, bass.ds(i * ROUND1 + n, 1), :], start=True, stop=True)
                        last.then_inc(scored, 1)

                    for b in range(ROUND_SLABS):
                        slabs.wait(pe, i * ROUND_SLABS, b)
                        for j in range(SLAB_TILES):
                            n = b * SLAB_TILES + j
                            slabs.columns(nc, qps[n % 2][:], b, j, hTh, hTl).then_inc(projected, 1)
                            if n >= 1:
                                score(n - 1)
                    score(ROUND1 - 1)

                def flip_block(i, b):
                    pe.wait_ge(load_u[b % RING], 16 * (i * (EARLY_TILE // RING) + b // RING + 1))
                    pe.wait_ge(u_turned, i * (2 * EARLY_TILE) + 2 * b + 1)
                    for half in range(2):
                        for j in range(4):
                            k = 4 * half + j
                            last = nc.tensor.transpose(ups[half][:, j * P:(j + 1) * P], u[b % RING][:, k * P:(k + 1) * P],
                                                       c["ident"][:])
                        last.then_inc(u_flip, 1)

                pe.sem_inc(hid, 2)
                flip_block(0, 0)
                with pe.Fori(0, TT) as i:
                    for b in range(EARLY_TILE):
                        flip_block(i, b + 1)
                        pe.wait_ge(u_low, i * EARLY_TILE + b + 3)
                        pe.wait_ge(gelued, i * EARLY_TILE + b + 1)
                        for k in range(KC):
                            for n, (w, x) in enumerate(((uTh, hTh), (uTh, hTl), (uTl, hTh))):
                                last = nc.tensor.matmul(hps[b % 2][:], w[b % 2][:, k, :], x[:, k, :],
                                                        start=(k == 0 and n == 0), stop=(k == KC - 1 and n == 2))
                        last.then_inc(hid, 1)
                    pe.wait_ge(picked, i + 1)
                    pe.wait_ge(done, i + 1)
                    for j in range(3):
                        last = nc.tensor.transpose(gps[:, j, :], picks[:, j, :], c["ident"][:])
                    last.then_inc(turned, 1)

            @block.scalar
            def _(act):
                act.dma_start(keys[:], sub_keys.rearrange("h p n d -> n (h p) d")).then_inc(load_k, 16)
                turn.on_act(act)

                def project(i, is_last):
                    for b in range(ROUND_SLABS):
                        if not (is_last and b + 1 == ROUND_SLABS):
                            slabs.split_high(act, i * ROUND_SLABS, b + 1, i * (ROUND_SLABS // 2))
                        for n in range(b * SLAB_TILES, (b + 1) * SLAB_TILES):
                            act.wait_ge(projected, i * ROUND1 + n + 2 * SLAB_TILES + 1)
                            if n >= 2:
                                act.wait_ge(scored, i * ROUND1 + n - 1)
                            nc.scalar.copy(qT[n % 2][:], qps[n % 2][:]).then_inc(qready, 1)

                slabs.split_high(act, 0, 0, 0)
                with act.Fori(0, ROUNDS - 1) as i:
                    project(i, False)
                project(ROUNDS - 1, True)
                act.sem_inc(gelued, 2)
                starts_at_one(act, done, u_turned)
                for b in range(2):
                    act.sem_inc(kept[b], 16)

                def split_u(i, b):
                    for half in range(2):
                        act.wait_ge(u_flip, i * (2 * EARLY_TILE) + 2 * b + half + 2 * RING + 1)
                        if half == 0:
                            act.wait_ge(u_low, i * EARLY_TILE + b + 1)
                        nc.scalar.copy(uT[b % 2][:, half * BANK:(half + 1) * BANK], ups[half][:]).then_inc(u_turned, 1)
                    act.wait_ge(u_turned, i * (2 * EARLY_TILE) + 2 * b + 3)
                    act.wait_ge(hid, i * EARLY_TILE + b + 1)
                    nc.scalar.copy(uTh[b % 2], uT[b % 2].rearrange("p (k n) -> p k n", n=P)).then_inc(u_high, 1)

                split_u(0, 0)
                with act.Fori(0, TT) as i:
                    def keep(b):
                        act.wait_ge(gelued, i * EARLY_TILE + b + 3)
                        act.dma_start(early[bass.ds(i * EARLY_TILE + b, 1)], gel[b % 2][:]).then_inc(kept[b % 2], 16)

                    for b in range(EARLY_TILE):
                        split_u(i, b + 1)
                        if b:
                            keep(b - 1)
                        act.wait_ge(hid, i * EARLY_TILE + b + 3)
                        act.wait_ge(kept[b % 2], 16 * (i * (EARLY_TILE // 2) + b // 2 + 1))
                        nc.scalar.activation(gel[b % 2][:], hps[b % 2][:], ACT.Gelu).then_inc(gelued, 1)
                        if b == EARLY_TILE // 2:
                            act.wait_ge(logits, i + 1)
                            nc.scalar.activation(picks[:, 0, :], picks[:, 0, :], ACT.Exp).then_inc(expd, 1)
                    keep(EARLY_TILE - 1)
                    act.wait_ge(turned, i + 2)
                    nc.scalar.copy(giT[:, :, bass.ds(i * P, P)], gps[:]).then_inc(done, 1)
                for b in range(2):
                    act.wait_ge(kept[b], 16 * (EARLY_SELECT // 2 + 1))
                act.wait_ge(done, TT + 1)

            @block.vector
            def _(dve):
                nc.vector.memset(mass[:], 0.0).then_inc(ranked, 2)
                turn.on_dve(dve)
                for q in range(SETS // 4):
                    dve.wait_ge(kflip, q + 1)
                    nc.vector.tensor_copy(keysT[:, 4 * q:4 * q + 4, :], tps[:]).then_inc(ktaken, 1)
                PER_SET = 5
                with dve.Fori(0, ROUNDS) as i:
                    ch = Chain(dve, chain, i * (ROUND1 * PER_SET), passed)
                    for n in range(ROUND1):
                        sc, e = sps[n % 2], i * ROUND1 + n
                        dve.wait_ge(scored, e + 1)
                        dve.sem_inc(passed, 1)
                        for t in range(TT):
                            last = nc.vector.max(best[:, t, 0:8], sc[:, t, :])
                        ch.link(last)
                        for t in range(TT):
                            nc.vector.max_index(besti[:, t, 0:8], best[:, t, 0:8], sc[:, t, :])
                            last = nc.vector.match_replace(masked[:, t, :], best[:, t, 0:8], sc[:, t, :], NEG)
                        ch.link(last)
                        for t in range(TT):
                            last = nc.vector.max(best[:, t, 8:16], masked[:, t, :])
                        ch.link(last)
                        for t in range(TT):
                            last = nc.vector.max_index(besti[:, t, 8:16], best[:, t, 8:16], masked[:, t, :])
                        ch.link(last)
                        ch.link(nc.vector.tensor_copy(val[:, bass.ds(e, 1), :, :], best[:].unsqueeze(1)))
                        nc.vector.tensor_copy(num[:, bass.ds(e, 1), :, :], besti[:].unsqueeze(1)).then_inc(ranked, 1)
                        dve.wait_ge(ranked, e + 3)
                    ch.end(ROUND1 * PER_SET)
                PER_TILE = 18
                with dve.Fori(0, TT) as i:
                    ch = Chain(dve, chain, SETS * PER_SET + i * PER_TILE, passed)
                    nc.vector.tensor_copy(valt[:].unsqueeze(2), val[:, :, bass.ds(i, 1), :])
                    ch.link(nc.vector.tensor_copy(numt[:].unsqueeze(2), num[:, :, bass.ds(i, 1), :]))
                    v4 = valt[:].rearrange("p (h s) k -> p h s k", s=2)
                    n4 = numt[:].rearrange("p (h s) k -> p h s k", s=2)
                    cand4 = cand[:].rearrange("p h (a b) -> p h a b", a=TOPK)
                    hot4 = hot[:].rearrange("p h (a b) -> p h a b", a=TOPK)
                    each = [P, HEADS, TOPK, TOPK]
                    ch.link(nc.vector.tensor_tensor(cand4, v4[:, :, 0].unsqueeze(3).broadcast_to(each),
                                                    v4[:, :, 1].unsqueeze(2).broadcast_to(each), ALU.add))
                    for hh in range(HEADS):
                        last = nc.vector.max(top[:, hh, 0:8], cand[:, hh, :])
                    ch.link(last)
                    for hh in range(HEADS):
                        nc.vector.max_index(topi[:, hh, 0:8], top[:, hh, 0:8], cand[:, hh, :])
                        last = nc.vector.match_replace(candm[:, hh, :], top[:, hh, 0:8], cand[:, hh, :], NEG)
                    ch.link(last)
                    for hh in range(HEADS):
                        last = nc.vector.max(top[:, hh, 8:16], candm[:, hh, :])
                    ch.link(last)
                    for hh in range(HEADS):
                        last = nc.vector.max_index(topi[:, hh, 8:16], top[:, hh, 8:16], candm[:, hh, :])
                    ch.link(last)
                    g3 = picks[:, 0, :].rearrange("p (h k) -> p h k", k=TOPK)
                    dve.wait_ge(turned, i + 1)
                    last = nc.vector.tensor_tensor(g3, top[:], top[:, :, 0:1].broadcast_to([P, HEADS, TOPK]), ALU.subtract)
                    last.then_inc(logits, 1)
                    for side, (op, k) in enumerate(((ALU.logical_shift_right, 4), (ALU.bitwise_and, 15))):
                        ch.link(nc.vector.tensor_scalar(digit[:], topi[:].rearrange("p h k -> p (h k)"), k, None, op))
                        ch.link(nc.vector.tensor_copy(digitf[:], digit[:]))
                        ch.link(nc.vector.tensor_tensor(hot[:].rearrange("p h (k a) -> p (h k) a", a=TOPK),
                                                        digitf[:].unsqueeze(2).broadcast_to([P, HEADS * TOPK, TOPK]),
                                                        c["iota"][:, 0:TOPK].unsqueeze(1).broadcast_to([P, HEADS * TOPK, TOPK]),
                                                        ALU.is_equal))
                        ch.link(nc.vector.tensor_tensor(hot4, hot4, n4[:, :, side].unsqueeze(2).broadcast_to(each), ALU.mult))
                        ch.link(nc.vector.tensor_reduce(picks[:, 1 + side, :], hot[:].rearrange("p h (k a) -> p (h k) a", a=TOPK),
                                                        axis=AX.X, op=ALU.add))
                    dve.wait_ge(expd, i + 1)
                    ch.link(nc.vector.tensor_reduce(mass[:], g3, axis=AX.X, op=ALU.add))
                    ch.link(nc.vector.reciprocal(mass[:], mass[:]))
                    last = nc.vector.tensor_tensor(g3, g3, mass[:].unsqueeze(2).broadcast_to([P, HEADS, TOPK]), ALU.mult)
                    last.then_inc(picked, 1)
                    ch.end(PER_TILE)


def peer_gates(nc, c, name, h, giT, gates, hTh, hTl, u_tab, early):
    BATCH = 4
    BATCHES = GRID // BATCH
    SLOTS = 4
    HIGH_AT, LOW_AT, HID_AT = (0, 1), (3, 5), 4
    assert 2 * (BATCHES - HID_AT) == 3 * KC
    with Stage(nc, name) as s:
        first = [s.sb(f"first{i}", [P, BATCH, NKEYS]) for i in range(SLOTS)]
        second = [s.sb(f"second{i}", [P, BATCH, NKEYS]) for i in range(SLOTS)]
        grid = [s.sb(f"grid{i}", [P, NKEYS, GRID]) for i in range(2)]
        u, uT = s.sb("u", [P, D]), s.sb("uT", [P, KC, P])
        uTh, uTl = s.sb("uTh", [P, KC, P], F32R), s.sb("uTl", [P, KC, P], F32R)
        gel = s.sb("gel", [P, SEQ])
        bank = [s.ps(f"bank{i}", [P, BATCH, P]) for i in range(SLOTS)]
        ups = [s.ps(f"ups{i}", [P, BANK]) for i in range(2)]
        hps = s.ps("hps", [P, SEQ])
        first_hot, second_hot, spread, filled = (s.sem(n) for n in ("first_hot", "second_hot", "spread", "filled"))
        stored = [s.sem(f"stored{i}") for i in range(2)]
        weighted, scaled = s.sem("weighted"), s.sem("scaled")
        load_u, u_flip, u_high, u_low = (s.sem(n) for n in ("load_u", "u_flip", "u_high", "u_low"))
        hid, gelued, kept = s.sem("hid"), s.sem("gelued"), s.sem("kept")
        u_v = u_tab.rearrange("(b p) d -> b p d", p=P)
        rows = lambda ap: ap.rearrange("p k n -> p (k n)")
        assert BATCH * P == BANK
        with s.block() as block:
            @block.vector
            def _(dve):
                with dve.Fori(0, GRIDS * BATCHES // SLOTS) as i:
                    for r in range(SLOTS):
                        dve.wait_ge(spread, i * SLOTS + r + 1)
                        at = (i * SLOTS + r) * BATCH
                        for side, hot, done in ((1, first, first_hot), (2, second, second_hot)):
                            nc.vector.tensor_tensor(hot[r][:], c["iota"][:].unsqueeze(1).broadcast_to([P, BATCH, NKEYS]),
                                                    giT[:, side, bass.ds(at, BATCH)].unsqueeze(2).broadcast_to([P, BATCH, NKEYS]),
                                                    ALU.is_equal).then_inc(done, 1)

            @block.gpsimd
            def _(pool):
                starts_at_one(pool, u_low)
                with pool.Fori(0, GRIDS) as n:
                    for q in range(BATCHES):
                        at, r = n * GRID + q * BATCH, q % SLOTS
                        pool.wait_ge(first_hot, n * BATCHES + q + 1)
                        nc.gpsimd.tensor_tensor(first[r][:], first[r][:],
                                                giT[:, 0, bass.ds(at, BATCH)].unsqueeze(2).broadcast_to([P, BATCH, NKEYS]),
                                                ALU.mult).then_inc(weighted, 1)
                        if q in LOW_AT:
                            half = LOW_AT.index(q)
                            at = slice(4 * half, 4 * half + 4)
                            pool.wait_ge(u_high, 2 * n + half + 2)
                            nc.gpsimd.tensor_tensor(rows(uTl[:, at, :]), rows(uT[:, at, :]), rows(uTh[:, at, :]).bitcast(F32),
                                                    ALU.subtract).then_inc(u_low, 1)

            @block.tensor
            def _(pe):
                pe.sem_inc(spread, SLOTS)
                starts_at_one(pe, u_flip, hid)
                with pe.Fori(0, GRIDS) as n:
                    pe.wait_ge(load_u, 16 * n + 16)
                    pe.wait_ge(u_high, 2 * n + 1)
                    for half in range(2):
                        for j in range(4):
                            k = 4 * half + j
                            last = nc.tensor.transpose(ups[half][:, j * P:(j + 1) * P], u[:, k * P:(k + 1) * P], c["ident"][:])
                        last.then_inc(u_flip, 1)
                    for q in range(BATCHES):
                        r = q % SLOTS
                        pe.wait_ge(weighted, n * BATCHES + q + 1)
                        pe.wait_ge(second_hot, n * BATCHES + q + 1)
                        pe.wait_ge(filled, n * BATCHES + q + 1)
                        for m in range(BATCH):
                            last = nc.tensor.matmul(bank[r][:, m, :], second[r][:, m, :], first[r][:, m, :],
                                                    start=True, stop=True)
                        last.then_inc(spread, 1)
                        for step in range(2 * (q - HID_AT), 2 * (q - HID_AT) + 2) if q >= HID_AT else ():
                            k, m = step // 3, step % 3
                            if m == 0 and k % 4 == 0:
                                pe.wait_ge(u_low, 2 * n + k // 4 + 2)
                            if step == 0:
                                pe.wait_ge(gelued, n + 1)
                            w, x = ((uTh, hTh), (uTh, hTl), (uTl, hTh))[m]
                            last = nc.tensor.matmul(hps[:], w[:, k, :], x[:, k, :], start=(step == 0), stop=(step == 3 * KC - 1))
                            if step == 3 * KC - 1:
                                last.then_inc(hid, 1)

            @block.scalar
            def _(act):
                act.sem_inc(filled, SLOTS)
                nc.scalar.mul(h[:], h[:], ALPHA).then_inc(scaled, 1)
                starts_at_one(act, u_high, gelued)
                for sem in (stored[0], stored[1], kept):
                    act.sem_inc(sem, 16)
                with act.Fori(0, GRIDS // 2) as pair:
                    for odd in range(2):
                        n = 2 * pair + odd
                        act.wait_ge(stored[odd], 16 * pair + 16)
                        for q in range(BATCHES):
                            act.wait_ge(spread, n * BATCHES + q + SLOTS + 1)
                            nc.scalar.copy(grid[odd][:, :, BATCH * q:BATCH * (q + 1)],
                                           bank[q % SLOTS][:].rearrange("p t n -> p n t")).then_inc(filled, 1)
                            if q in HIGH_AT:
                                half = HIGH_AT.index(q)
                                at = slice(4 * half, 4 * half + 4)
                                act.wait_ge(u_flip, 2 * n + half + 2)
                                act.wait_ge(u_low, 2 * n + half + 1)
                                nc.scalar.copy(rows(uT[:, at, :]), ups[half][:])
                                if half == 0:
                                    act.wait_ge(hid, n + 1)
                                nc.scalar.copy(rows(uTh[:, at, :]), ups[half][:]).then_inc(u_high, 1)
                        act.wait_ge(hid, n + 2)
                        act.wait_ge(kept, 16 * n + 16)
                        nc.scalar.activation(gel[:], hps[:], ACT.Gelu).then_inc(gelued, 1)
                        act.wait_ge(filled, n * BATCHES + BATCHES + SLOTS)
                        act.dma_start(gates[:, bass.ds(n, 1), :, :], grid[odd][:].unsqueeze(1)).then_inc(stored[odd], 16)
                        act.wait_ge(gelued, n + 2)
                        act.dma_start(early[bass.ds(n + EARLY_SELECT, 1)], gel[:]).then_inc(kept, 16)
                for odd in range(2):
                    act.wait_ge(stored[odd], 16 * (GRIDS // 2 + 1))
                act.wait_ge(kept, 16 * (GRIDS + 1))
                act.wait_ge(scaled, 1)

            @block.sync
            def _(sp):
                with sp.Fori(0, GRIDS) as n:
                    sp.wait_ge(u_flip, 2 * n + 1)
                    sp.dma_start(u[:], u_v[bass.ds(n + EARLY_SELECT, 1)]).then_inc(load_u, 16)


def peer_experts(nc, c, name, hTh, hTl, acc, u_tab, v_tab, gates, early):
    BLOCKS = NKEYS
    GROUP = 4
    OUTS = TT * HALVES
    ROUND = 2 * GROUP
    FIRST = EARLY // ROUND
    assert EARLY % ROUND == 0
    with Stage(nc, name) as s:
        u = [s.sb(f"u{i}", [P, D]) for i in range(GROUP)]
        v = [s.sb(f"v{i}", [P, D]) for i in range(GROUP)]
        vh = [s.sb(f"vh{i}", [P, D], F32R) for i in range(ROUND)]
        vl = [s.sb(f"vl{i}", [P, D], F32R) for i in range(ROUND)]
        g = [s.sb(f"g{i}", [P, GRIDS, 1, GRID]) for i in range(GROUP)]
        uTh = [s.sb(f"uTh{i}", [P, KC, P], F32R) for i in range(2)]
        uTl = [s.sb(f"uTl{i}", [P, KC, P], F32R) for i in range(2)]
        act_h = [s.sb(f"acth{i}", [P, SEQ], F32R) for i in range(ROUND)]
        act_l = [s.sb(f"actl{i}", [P, SEQ], F32R) for i in range(ROUND)]
        gel = [s.sb(f"gel{i}", [P, SEQ]) for i in range(2)]
        eased = s.sb("eased", [P, 1])
        tps = [s.ps(f"tps{i}", [P, BANK]) for i in range(2)]
        hps = [s.ps(f"hps{i}", [P, SEQ]) for i in range(2)]
        ops = [s.ps(f"ops{i}", [P, BANK]) for i in range(4)]
        load_u = [s.sem(f"load_u{i}") for i in range(GROUP)]
        load_v = [s.sem(f"load_v{i}") for i in range(GROUP)]
        load_g = [s.sem(f"load_g{i}") for i in range(GROUP)]
        flip, u_high, u_low = s.sem("flip"), s.sem("u_high"), s.sem("u_low")
        v_high, v_low = s.sem("v_high"), s.sem("v_low")
        hid, gelued, gated, gated_high, gated_low = (s.sem(n) for n in ("hid", "gelued", "gated", "gated_high", "gated_low"))
        summed, added = s.sem("summed"), s.sem("added")
        u_v = u_tab.rearrange("(b p) d -> b p d", p=P)
        v_v = v_tab.rearrange("(b p) d -> b p d", p=P)
        f32 = lambda ap: ap.bitcast(F32)
        rows = lambda ap: ap.rearrange("p k n -> p (k n)")
        with s.block() as block:
            @block.sync
            def _(sp):
                def load(i, is_early):
                    for b in range(ROUND):
                        at = i * ROUND + b
                        sp.wait_ge(gated, i * ROUND + b + 2)
                        if is_early:
                            sp.dma_start(u[b % GROUP][:, 0:SEQ], early[bass.ds(at, 1)]).then_inc(load_u[b % GROUP], 16)
                        else:
                            sp.dma_start(u[b % GROUP][:], u_v[bass.ds(at, 1)]).then_inc(load_u[b % GROUP], 16)
                        sp.dma_start(g[b % GROUP][:], gates[:, :, bass.ds(at, 1), :]).then_inc(load_g[b % GROUP], 16)
                        sp.wait_ge(v_low, i * ROUND + b + 2)
                        sp.dma_start(v[b % GROUP][:], v_v[bass.ds(at, 1)]).then_inc(load_v[b % GROUP], 16)

                with sp.Fori(0, FIRST) as i:
                    load(i, True)
                with sp.Fori(FIRST, BLOCKS // ROUND) as i:
                    load(i, False)
                sp.wait_ge(gated, BLOCKS + 2)
                sp.dma_start(u[0][:], u_v[0:1]).then_inc(load_u[0], 16)

            @block.tensor
            def _(pe):
                pe.sem_inc(summed, OUTS + 1)
                starts_at_one(pe, flip)

                def outputs(i, grp):
                    for part in range(OUTS // 4):
                        for x in range(GROUP):
                            b = GROUP * grp + x
                            if part == 0:
                                pe.wait_ge(v_low, i * ROUND + b + GROUP + 2)
                                pe.wait_ge(gated_low, i * ROUND + b + 1)
                            for o in range(4):
                                t, half = (4 * part + o) // HALVES, (4 * part + o) % HALVES
                                if x == 0:
                                    pe.wait_ge(added, i * 2 * OUTS + grp * OUTS + 4 * part + o + OUTS - 3)
                                for n, (lhsT, rhs) in enumerate(((act_h, vh), (act_h, vl), (act_l, vh))):
                                    last = nc.tensor.matmul(ops[o][:], lhsT[b][:, t * P:(t + 1) * P],
                                                            rhs[b][:, half * BANK:(half + 1) * BANK],
                                                            start=(x == 0 and n == 0), stop=(x == GROUP - 1 and n == 2))
                                if x == GROUP - 1:
                                    last.then_inc(summed, 1)

                with pe.Fori(0, FIRST) as i:
                    outputs(i, 0)
                    outputs(i, 1)

                def flip_block(j, b):
                    pe.wait_ge(load_u[b % GROUP], 16 * (2 * j + 2 * FIRST + b // GROUP + 1))
                    pe.wait_ge(u_low, 2 * (j * ROUND + b) + 1)
                    for half in range(2):
                        for n in range(4):
                            k = 4 * half + n
                            last = nc.tensor.transpose(tps[half][:, n * P:(n + 1) * P], u[b % GROUP][:, k * P:(k + 1) * P],
                                                       c["ident"][:])
                        last.then_inc(flip, 1)

                flip_block(0, 0)
                with pe.Fori(0, BLOCKS // ROUND - FIRST) as j:
                    for grp in range(2):
                        for x in range(GROUP):
                            b = GROUP * grp + x
                            flip_block(j, b + 1)
                            pe.wait_ge(u_low, 2 * (j * ROUND + b) + 3)
                            if b >= 2:
                                pe.wait_ge(gelued, j * ROUND + b - 1)
                            for k in range(KC):
                                for n, (lhsT, rhs) in enumerate(((uTh, hTh), (uTh, hTl), (uTl, hTh))):
                                    last = nc.tensor.matmul(hps[b % 2][:], lhsT[b % 2][:, k, :], rhs[:, k, :],
                                                            start=(k == 0 and n == 0), stop=(k == KC - 1 and n == 2))
                            last.then_inc(hid, 1)
                        outputs(j + FIRST, grp)

            @block.scalar
            def _(act):
                def split_v(i, b):
                    act.wait_ge(load_v[b % GROUP], 16 * (2 * i + b // GROUP + 1))
                    act.wait_ge(summed, (2 * i + b // GROUP) * OUTS + 1)
                    nc.scalar.copy(vh[b][:], v[b % GROUP][:]).then_inc(v_high, 1)

                def gated_part(i, b):
                    act.wait_ge(gated, i * ROUND + b + GROUP + 2)
                    nc.scalar.copy(act_h[b][:], gel[b % 2][:]).then_inc(gated_high, 1)

                with act.Fori(0, FIRST) as i:
                    for b in range(ROUND):
                        split_v(i, b)
                        gated_part(i, b)

                def split_u(j, b):
                    for half in range(2):
                        act.wait_ge(flip, 2 * (j * ROUND + b) + half + 2)
                        if b >= 2 and half == 0:
                            act.wait_ge(hid, j * ROUND + b - 1)
                        nc.scalar.copy(rows(uTh[b % 2][:, 4 * half:4 * half + 4, :]), tps[half][:]).then_inc(u_high, 1)

                split_u(0, 0)
                with act.Fori(0, BLOCKS // ROUND - FIRST) as j:
                    i = j + FIRST
                    for grp in range(2):
                        for x in range(GROUP):
                            b = GROUP * grp + x
                            split_v(i, b)
                            split_u(j, b + 1)
                            if x:
                                gated_part(i, b - 1)
                            act.wait_ge(hid, j * ROUND + b + 1)
                            if b >= 2:
                                act.wait_ge(gated_low, i * ROUND + b - 1)
                            nc.scalar.activation(gel[b % 2][:], hps[b % 2][:], ACT.Gelu).then_inc(gelued, 1)
                        gated_part(i, GROUP * grp + GROUP - 1)

            @block.gpsimd
            def _(pool):
                pool.sem_inc(v_low, GROUP + 1)
                with pool.Fori(0, BLOCKS // ROUND) as i:
                    for b in range(ROUND):
                        pool.wait_ge(v_high, i * ROUND + b + 1)
                        nc.gpsimd.tensor_tensor(vl[b][:], v[b % GROUP][:], f32(vh[b][:]), ALU.subtract).then_inc(v_low, 1)

            @block.vector
            def _(dve):
                nc.vector.memset(eased[:], 0.0).then_inc(added, OUTS)
                starts_at_one(dve, u_low)
                dve.sem_inc(gated, GROUP + 1)

                def gate(i, b, values):
                    dve.wait_ge(load_g[b % GROUP], 16 * (2 * i + b // GROUP + 1))
                    nc.vector.tensor_tensor(gel[b % 2][:], values, g[b % GROUP][:].rearrange("p s a n -> p (s a n)"), ALU.mult).then_inc(gated, 1)
                    dve.wait_ge(gated_high, i * ROUND + b + 1)
                    nc.vector.tensor_tensor(act_l[b][:], gel[b % 2][:], f32(act_h[b][:]), ALU.subtract).then_inc(gated_low, 1)

                def gather(i, grp, outs):
                    for o in outs:
                        dve.wait_ge(summed, (2 * i + grp) * OUTS + OUTS + o + 2)
                        dve.wait_ge(added, (2 * i + grp) * OUTS + o + 1)
                        t, half = o // HALVES, o % HALVES
                        nc.vector.tensor_tensor(acc[:, t, half * BANK:(half + 1) * BANK],
                                                acc[:, t, half * BANK:(half + 1) * BANK], ops[o % 4][:],
                                                ALU.add).then_inc(added, 1)

                def gate_early(i, grp):
                    for x in range(GROUP):
                        dve.wait_ge(load_u[x], 16 * (2 * i + grp + 1))
                        gate(i, GROUP * grp + x, u[x][:, 0:SEQ])

                gate_early(0, 0)
                with dve.Fori(0, FIRST - 1) as i:
                    gather(i, 0, range(4))
                    gate_early(i, 1)
                    gather(i, 0, range(4, OUTS))
                    gather(i, 1, range(4))
                    gate_early(i + 1, 0)
                    gather(i, 1, range(4, OUTS))
                gather(FIRST - 1, 0, range(4))
                gate_early(FIRST - 1, 1)
                gather(FIRST - 1, 0, range(4, OUTS))
                gather(FIRST - 1, 1, range(OUTS))

                def split_u(j, b):
                    for half in range(2):
                        dve.wait_ge(u_high, 2 * (j * ROUND + b) + half + 1)
                        if b >= 2 and half == 0:
                            dve.wait_ge(hid, j * ROUND + b - 1)
                        nc.vector.tensor_tensor(rows(uTl[b % 2][:, 4 * half:4 * half + 4, :]), tps[half][:],
                                                f32(rows(uTh[b % 2][:, 4 * half:4 * half + 4, :])),
                                                ALU.subtract).then_inc(u_low, 1)

                split_u(0, 0)
                with dve.Fori(0, BLOCKS // ROUND - FIRST) as j:
                    for grp in range(2):
                        for x in range(GROUP):
                            b = GROUP * grp + x
                            split_u(j, b + 1)
                            dve.wait_ge(gelued, j * ROUND + b + 1)
                            gate(j + FIRST, b, gel[b % 2][:])
                        gather(j + FIRST, grp, range(OUTS))


GDN_HEADS = 8
GDN_QKV = 3 * GDN_HEADS
CONV = 4


def gdn_project(nc, c, name, x, xTh, xTl, w_in, conv_w, qkvT, z, logits):
    ROUND_SLABS = 4
    ROUNDS = GDN_QKV // (ROUND_SLABS * SLAB_TILES)
    ROUND = ROUND_SLABS * SLAB_TILES
    QKV_SLABS, Z_SLABS = ROUNDS * ROUND_SLABS, GDN_HEADS * P // SLAB
    LOGITS = 2 * GDN_HEADS
    with Stage(nc, name) as s:
        tail = s.sb("tail", [P, KC, LOGITS])
        tail_h, tail_l = s.sb("tail_h", [P, KC, LOGITS], F32R), s.sb("tail_l", [P, KC, LOGITS], F32R)
        taps = s.sb("taps", [P, P])
        tapsT = s.sb("tapsT", [P, CONV * GDN_QKV])
        conv = [s.sb(f"conv{i}", [P, SEQ]) for i in range(2)]
        pp = [s.ps(f"pp{i}", [P, BANK]) for i in range(4)]
        taps_ps = s.ps("taps_ps", [P, CONV * GDN_QKV])
        load_taps, taps_turned, taps_ready = s.sem("load_taps"), s.sem("taps_turned"), s.sem("taps_ready")
        projected, mixed, convolved, silued = s.sem("projected"), s.sem("mixed"), s.sem("convolved"), s.sem("silued")
        zmade, ztaken, tail_high, tail_low = s.sem("zmade"), s.sem("ztaken"), s.sem("tail_high"), s.sem("tail_low")
        turn = SplitTranspose(nc, s, c, x, xTh, xTl, pp)
        slabs = Slabs(nc, s, w_in[:, 0:(QKV_SLABS + Z_SLABS) * SLAB].rearrange("(k p) (s n) -> s p k n", p=P, n=SLAB), projected)
        with s.block() as block:
            @block.sync
            def _(sp):
                sp.dma_start(taps[0:CONV * GDN_QKV, :], conv_w.rearrange("j (t c) -> (j t) c", c=P)).then_inc(load_taps, 16)
                with nc.allow_non_contiguous_dma(reason="sixteen columns"):
                    sp.dma_start(tail[:], w_in[:, (QKV_SLABS + Z_SLABS) * SLAB:].rearrange("(k p) n -> p k n", p=P)).then_inc(load_taps, 16)
                with sp.Fori(0, ROUNDS) as i:
                    for n in range(ROUND_SLABS):
                        slabs.load(sp, i * ROUND_SLABS, n)
                for n in range(Z_SLABS):
                    slabs.load(sp, QKV_SLABS, n)

            @block.gpsimd
            def _(pool):
                pool.sem_inc(slabs.low_ready, 2)
                with pool.Fori(0, ROUNDS) as i:
                    for n in range(ROUND_SLABS):
                        slabs.split_low(pool, i * ROUND_SLABS, n)
                for n in range(Z_SLABS):
                    slabs.split_low(pool, QKV_SLABS, n)
                pool.wait_ge(tail_high, 1)
                nc.gpsimd.tensor_tensor(tail_l[:], tail[:], tail_h[:].bitcast(F32), ALU.subtract).then_inc(tail_low, 1)

            @block.tensor
            def _(pe):
                pe.sem_inc(projected, 2 * SLAB_TILES)
                turn.on_pe(pe)
                pe.wait_ge(load_taps, 32)
                n = CONV * GDN_QKV
                nc.tensor.transpose(taps_ps[:], taps[0:n, :], c["ident"][0:n, 0:n]).then_inc(taps_turned, 1)
                turn.finished(pe)
                with pe.Fori(0, ROUNDS) as i:
                    for b in range(ROUND_SLABS):
                        slabs.wait(pe, i * ROUND_SLABS, b)
                        for j in range(SLAB_TILES):
                            n = b * SLAB_TILES + j
                            pe.wait_ge(convolved, i * ROUND + n + 1)
                            slabs.columns(nc, pp[n % 4][:], b, j, xTh, xTl).then_inc(projected, 1)
                pe.wait_ge(convolved, GDN_QKV + 4)
                for b in range(Z_SLABS):
                    slabs.wait(pe, QKV_SLABS, b)
                    for t in range(TT):
                        n = b * TT + t
                        if n >= 4:
                            pe.wait_ge(ztaken, n - 3)
                        last = slabs.tokens(nc, pp[n % 4][:, 0:SLAB], b, t, xTh, xTl)
                        last.then_inc(zmade, 1)
                    pe.wait_ge(zmade, (b + 1) * TT)
                    pe.sem_inc(projected, SLAB_TILES)
                pe.wait_ge(ztaken, Z_SLABS * TT - 3)
                pe.wait_ge(tail_low, 1)
                for t in range(TT):
                    at = slice(t * P, (t + 1) * P)
                    for k in range(KC):
                        for m, (x, w) in enumerate(((xTh, tail_h), (xTh, tail_l), (xTl, tail_h))):
                            last = nc.tensor.matmul(pp[0][:, t * LOGITS:(t + 1) * LOGITS], x[:, k, at], w[:, k, :],
                                                    start=(k == 0 and m == 0), stop=(k == KC - 1 and m == 2))
                last.then_inc(zmade, 1)

            @block.vector
            def _(dve):
                turn.on_dve(dve)
                dve.wait_ge(taps_turned, 1)
                nc.vector.tensor_copy(tapsT[:], taps_ps[:]).then_inc(taps_ready, 1)
                dve.wait_ge(taps_ready, 1)
                nc.vector.memset(conv[0][:, 0:1], 0.0).then_inc(convolved, 4)
                with dve.Fori(0, ROUNDS) as i:
                    ch = Chain(dve, mixed, i * (ROUND * (CONV - 1)))
                    for n in range(ROUND):
                        at = i * ROUND + n
                        src, dst = pp[n % 4], conv[n % 2]
                        dve.wait_ge(projected, at + 2 * SLAB_TILES + 1)
                        dve.wait_ge(silued, at + 1)

                        def tap(j):
                            return tapsT[:, bass.ds(at + j * GDN_QKV, 1)]

                        ch.link(nc.vector.tensor_scalar(dst[:], src[:], tap(CONV - 1), None, ALU.mult))
                        for back in range(1, CONV):
                            last = nc.vector.scalar_tensor_tensor(dst[:, back:], src[:, 0:SEQ - back], tap(CONV - 1 - back),
                                                                  dst[:, back:], ALU.mult, ALU.add)
                            if back < CONV - 1:
                                ch.link(last)
                        last.then_inc(convolved, 1)
                    ch.end(ROUND * (CONV - 1))

            @block.scalar
            def _(act):
                turn.on_act(act)
                act.wait_ge(taps_ready, 1)
                nc.scalar.copy(conv[1][:, 0:1], tapsT[:, 0:1]).then_inc(silued, 2)
                slabs.split_high(act, 0, 0, 0)
                with act.Fori(0, ROUNDS) as i:
                    for b in range(ROUND_SLABS):
                        slabs.split_high(act, i * ROUND_SLABS, b + 1, i * (ROUND_SLABS // 2))
                        for n in range(b * SLAB_TILES, (b + 1) * SLAB_TILES):
                            at = i * ROUND + n
                            act.wait_ge(convolved, at + 5)
                            nc.scalar.activation(qkvT[:, bass.ds(at, 1), :], conv[n % 2][:].unsqueeze(1), ACT.Silu).then_inc(silued, 1)
                nc.scalar.copy(tail_h[:], tail[:]).then_inc(tail_high, 1)
                for b in range(Z_SLABS):
                    if b + 1 < Z_SLABS:
                        slabs.split_high(act, QKV_SLABS, b + 1, QKV_SLABS // 2)
                    for t in range(TT):
                        n = b * TT + t
                        act.wait_ge(zmade, n + 1)
                        nc.scalar.activation(z[:, t, b * SLAB:(b + 1) * SLAB], pp[n % 4][:, 0:SLAB], ACT.Silu).then_inc(ztaken, 1)
                act.wait_ge(zmade, Z_SLABS * TT + 1)
                nc.scalar.copy(logits[:], pp[0][:, 0:TT * LOGITS].rearrange("p (t n) -> p t n", t=TT)).then_inc(ztaken, 1)
                act.wait_ge(ztaken, Z_SLABS * TT + 1)


def gdn_normalize(nc, c, name, qkvT):
    H, RING = GDN_HEADS, 4
    with Stage(nc, name) as s:
        sq = [s.sb(f"sq{i}", [P, SEQ]) for i in range(RING)]
        into = s.sb("into", [P, H, H])
        out_of = s.sb("out_of", [P, H, P])
        factor = s.sb("factor", [P, 2, SEQ])
        eps = [s.sb(f"eps{i}", [P, 1]) for i in range(2)]
        total = [s.ps(f"total{i}", [H, SEQ]) for i in range(2)]
        wide = [s.ps(f"wide{i}", [P, SEQ]) for i in range(RING)]
        squared, summed, rooted, inverted = s.sem("squared"), s.sem("summed"), s.sem("rooted"), s.sem("inverted")
        spread, scaled, ready, cleared = s.sem("spread"), s.sem("scaled"), s.sem("ready"), s.sem("cleared")
        with s.block() as block:
            @block.scalar
            def _(act):
                with act.Fori(0, 2 * H // RING) as i:
                    for n in range(RING):
                        act.wait_ge(summed, i * RING + n + 1)
                        nc.scalar.activation(sq[n][:].unsqueeze(1), qkvT[:, bass.ds(i * RING + n, 1), :],
                                             ACT.Square).then_inc(squared, 1)
                act.wait_ge(ready, 5)
                for part, scale in ((0, float(P)), (1, 1.0)):
                    act.wait_ge(summed, (part + 1) * H + RING)
                    nc.scalar.activation(factor[0:H, part, :], total[part][:], ACT.Sqrt, bias=eps[part][0:H, :],
                                         scale=scale).then_inc(rooted, 1)

            @block.tensor
            def _(pe):
                pe.sem_inc(summed, RING)
                pe.sem_inc(spread, RING)
                pe.wait_ge(ready, 5)
                for part in range(2):
                    for n in range(H):
                        pe.wait_ge(squared, part * H + n + 1)
                        nc.tensor.matmul(total[part][:], into[:, n, :], sq[n % RING][:], start=(n == 0),
                                         stop=(n == H - 1)).then_inc(summed, 1)
                for part in range(2):
                    pe.wait_ge(inverted, part + 1)
                    for n in range(H):
                        pe.wait_ge(scaled, part * H + n + 1)
                        nc.tensor.matmul(wide[n % RING][:], out_of[:, n, :], factor[:, part, :],
                                         start=True, stop=True).then_inc(spread, 1)

            @block.vector
            def _(dve):
                nc.vector.memset(eps[0][:], P * RMS_EPS).then_inc(ready, 1)
                nc.vector.memset(eps[1][:], RMS_EPS).then_inc(ready, 1)
                nc.vector.memset(into[:], 0.0).then_inc(cleared, 1)
                nc.vector.tensor_copy(out_of[:], c["ident"][:, 0:H].unsqueeze(2).broadcast_to([P, H, P])).then_inc(ready, 1)
                nc.vector.memset(factor[:], 0.0).then_inc(ready, 1)
                dve.wait_ge(cleared, 1)
                nc.vector.memset(into[:].rearrange("p a b -> p (a b)")[:, 0:H * H:H + 1], 1.0).then_inc(ready, 1)
                dve.sem_inc(scaled, RING)
                for part in range(2):
                    dve.wait_ge(rooted, part + 1)
                    nc.vector.reciprocal(factor[0:H, part, :], factor[0:H, part, :]).then_inc(inverted, 1)
                with dve.Fori(0, 2 * H // RING) as i:
                    for n in range(RING):
                        dve.wait_ge(spread, i * RING + n + RING + 1)
                        at = qkvT[:, bass.ds(i * RING + n, 1), :]
                        nc.vector.tensor_tensor(at, at, wide[n][:].unsqueeze(1), ALU.mult).then_inc(scaled, 1)
                dve.wait_ge(scaled, 2 * H + RING)


def gdn_gates(nc, c, name, logits, a_log, dt_bias, gate):
    H = GDN_HEADS
    with Stage(nc, name) as s:
        arow, brow = s.sb("arow", [P, H]), s.sb("brow", [P, H])
        x, e, t = s.sb("x", [P, TT, H]), s.sb("e", [P, TT, H]), s.sb("t", [P, TT, H])
        sums = s.ps("sums", [P, 2, TT * H])
        load, chain, acted, summed = s.sem("load"), s.sem("chain"), s.sem("acted"), s.sem("summed")
        wide = lambda ap: ap.unsqueeze(1).broadcast_to([P, TT, H])
        flat = lambda ap: ap.rearrange("p t h -> p (t h)")
        with s.block() as block:
            @block.sync
            def _(sp):
                sp.dma_start(arow[:], a_log.broadcast_to([P, H])).then_inc(load, 16)
                sp.dma_start(brow[:], dt_bias.broadcast_to([P, H])).then_inc(load, 16)

            @block.vector
            def _(dve):
                ch = Chain(dve, chain)
                dve.wait_ge(load, 32)
                ch.link(nc.vector.tensor_tensor(x[:], logits[:, :, H:2 * H], wide(brow[:]), ALU.add))
                ch.link(nc.vector.tensor_scalar(t[:], x[:], -1.0, None, ALU.mult))
                ch.link(nc.vector.tensor_tensor(t[:], t[:], x[:], ALU.min))
                dve.wait_ge(acted, 4)
                ch.link(nc.vector.tensor_scalar(gate["beta"][:], gate["beta"][:], 1.0, None, ALU.add))
                ch.link(nc.vector.reciprocal(gate["beta"][:], gate["beta"][:]))
                ch.link(nc.vector.tensor_scalar(x[:], x[:], 0.0, None, ALU.max))
                ch.link(nc.vector.tensor_tensor(x[:], x[:], e[:], ALU.add))
                ch.link(nc.vector.tensor_tensor(x[:], x[:], wide(arow[:]), ALU.mult))
                ch.link(nc.vector.tensor_scalar(gate["g"][:], x[:], -1.0, None, ALU.mult))
                dve.wait_ge(summed, 1)
                ch.link(nc.vector.tensor_copy(flat(gate["sum"][:]), sums[:, 0, :]))
                ch.link(nc.vector.tensor_copy(flat(gate["last"][:]), sums[:, 1, :]))
                ch.link(nc.vector.tensor_tensor(gate["rest"][:], gate["last"][:], gate["sum"][:], ALU.subtract))
                dve.wait_ge(acted, 7)
                ch.link(nc.vector.tensor_tensor(gate["beta_exp"][:], gate["beta"][:], gate["exp"][:], ALU.mult))

            @block.scalar
            def _(act):
                act.wait_ge(load, 32)
                nc.scalar.activation(arow[:], arow[:], ACT.Exp).then_inc(acted, 1)
                nc.scalar.activation(gate["beta"][:], logits[:, :, 0:H], ACT.Exp, scale=-1.0).then_inc(acted, 1)
                act.wait_ge(chain, 3)
                nc.scalar.activation(e[:], t[:], ACT.Exp).then_inc(acted, 1)
                act.wait_ge(acted, 3)
                nc.scalar.activation(e[:], e[:], ACT.Ln, bias=c["ones"][:, 0:1]).then_inc(acted, 1)
                act.wait_ge(chain, 12)
                nc.scalar.activation(gate["exp"][:], gate["sum"][:], ACT.Exp).then_inc(acted, 1)
                nc.scalar.activation(gate["last"][:], gate["last"][:], ACT.Exp).then_inc(acted, 1)
                nc.scalar.activation(gate["rest"][:], gate["rest"][:], ACT.Exp).then_inc(acted, 1)

            @block.tensor
            def _(pe):
                pe.wait_ge(chain, 9)
                nc.tensor.matmul(sums[:, 0, :], c["upper"][:], flat(gate["g"][:]), start=True, stop=True)
                nc.tensor.matmul(sums[:, 1, :], c["ones"][:], flat(gate["g"][:]), start=True, stop=True).then_inc(summed, 1)


class Steps:

    def __init__(self, names, heads):
        self.names, self.heads = names.split(), heads
        assert len(set(self.names)) == len(self.names)

    def after(self, i, name, j):
        return i * (len(self.names) * self.heads) + self.names.index(name) * self.heads + j + 2

    def rounds(self, i):
        return i * (len(self.names) * self.heads) + 1


def gdn_recur(nc, c, name, qkvT, gate, o):
    G = 2
    H, C = GDN_HEADS, TT
    PE_STEPS = Steps("row kk knat vnat qk decT LT L2 U2 Y1 L4 U4 Y2 L8 Y3 YT N NT W0 N2 N2T W1 N4T W2 wT "
                     + " ".join(f"v{n} s{n} o{n}" for n in range(C)), G)
    ACT_STEPS = Steps("gB kS vS dec expRow decMT U L2 L4 L8 YT N N2 N4T wT " + " ".join(f"v{n} o{n}" for n in range(C)), G)
    DVE_STEPS = Steps("gap decM qg kbg kdec vb L0 L attnT LD UD UO Y0 U2 Y1 U4 Y2 Y3 NT W0 N2T W1 W2 "
                      + " ".join(f"s{n}" for n in range(C)), G)
    with Stage(nc, name) as s:
        names = ("gB kS vS gap decM qg kbg kdec vb L attnT decMT LD U UO Y0 Y1 Y2 Y3 L2 U2 expRow vnew").split()
        b = {n: [s.sb(f"{n}{j}", [P, C, P]) for j in range(G)] for n in names}
        for new, old in (("L4", "LD"), ("U4", "expRow"), ("L8", "gap"), ("YT", "gB"), ("N", "L"), ("NT", "decM"),
                         ("W0", "Y0"), ("N2", "L2"), ("N2T", "U2"), ("W1", "Y1"), ("N4T", "Y2"), ("W2", "kS"), ("wT", "decMT")):
            b[new] = b[old]
        UD = [s.sb(f"UD{j}", [P, C, P]) for j in range(G)]
        b["UD"] = UD
        state = [s.sb(f"state{j}", [P, P]) for j in range(G)]
        bank = [[s.ps(f"bank{j}_{k}", [P, C, P]) for k in range(8 // G)] for j in range(G)]
        pe_done, act_done, dve_done = s.sem("pe_done"), s.sem("act_done"), s.sem("dve_done")
        ident4 = c["ident"][:].unsqueeze(1).broadcast_to([P, C, P])
        block4 = c["block16"][:].unsqueeze(1).broadcast_to([P, C, P])
        lower4 = c["lower"][:].unsqueeze(1).broadcast_to([P, C, P])
        strict4 = c["strict"][:].unsqueeze(1).broadcast_to([P, C, P])

        def ps(step, j):
            return bank[j][PE_STEPS.names.index(step) % len(bank[j])]

        with s.block() as block:
            @block.tensor
            def _(pe):
                starts_at_one(pe, pe_done)
                with pe.Fori(0, H // G) as i:

                    def from_act(step, j):
                        pe.wait_ge(act_done, ACT_STEPS.after(i, step, j))

                    def from_dve(step, j):
                        pe.wait_ge(dve_done, DVE_STEPS.after(i, step, j))

                    def each(step, lhsT, rhs, acts=(), dves=()):
                        for j in range(G):
                            for a in acts:
                                from_act(a, j)
                            for d in dves:
                                from_dve(d, j)
                            for n in range(C):
                                last = nc.tensor.matmul(ps(step, j)[:, n, :], lhsT(j, n), rhs(j, n), start=True, stop=True)
                            last.then_inc(pe_done, 1)

                    def turn(step, src, acts=(), dves=()):
                        for j in range(G):
                            for a in acts:
                                from_act(a, j)
                            for d in dves:
                                from_dve(d, j)
                            for n in range(C):
                                last = nc.tensor.transpose(ps(step, j)[:, n, :], src(j, n), c["ident"][:])
                            last.then_inc(pe_done, 1)

                    def of(m):
                        return lambda j, n: b[m][j][:, n, :]

                    each("row", of("gB"), lambda j, n: c["upper"][:], acts=["gB"])
                    each("kk", of("kS"), of("kS"), acts=["kS"])
                    turn("knat", of("kS"))
                    turn("vnat", of("vS"), acts=["vS"])
                    each("qk", of("kS"), lambda j, n: qkvT[:, bass.ds(i * G + j, 1), n * P:(n + 1) * P],
                         acts=["expRow"], dves=["gap"])
                    turn("decT", of("decM"), dves=["L0"])
                    turn("LT", of("L"), dves=["L", "kdec"])
                    each("L2", of("UD"), of("LD"), dves=["UD", "vb"])
                    each("U2", of("LD"), of("UD"), dves=["attnT"])
                    each("Y1", of("L2"), of("Y0"), acts=["L2", "decMT"], dves=["Y0"])
                    each("L4", of("U2"), of("L2"), acts=["U"], dves=["U2"])
                    each("U4", of("L2"), of("U2"))
                    each("Y2", of("L4"), of("Y1"), acts=["L4"], dves=["Y1"])
                    each("L8", of("U4"), of("L4"), dves=["U4"])
                    each("Y3", of("L8"), of("Y2"), acts=["L8"], dves=["Y2"])
                    turn("YT", of("Y3"), dves=["Y3"])
                    each("N", of("YT"), of("UO"), acts=["YT"], dves=["UO"])
                    each("NT", of("UO"), of("YT"))
                    each("W0", of("NT"), of("Y3"), dves=["NT"])
                    each("N2", of("NT"), of("N"), acts=["N"])
                    each("N2T", of("N"), of("NT"))
                    each("W1", of("N2T"), of("W0"), dves=["N2T", "W0"])
                    each("N4T", of("N2"), of("N2T"), acts=["N2"])
                    each("W2", of("N4T"), of("W1"), acts=["N4T"], dves=["W1"])
                    each("wT", of("kbg"), of("W2"), dves=["W2"])
                    for n in range(C):
                        for j in range(G):
                            new = ps(f"v{n}", j)[:, 0, :]
                            last = nc.tensor.matmul(new, b["W2"][j][:, n, :], b["vb"][j][:, n, :], start=True, stop=(n == 0))
                            if n:
                                from_act("wT", j)
                                from_dve(f"s{n - 1}", j)
                                last = nc.tensor.matmul(new, b["wT"][j][:, n, :], state[j][:], start=False, stop=True)
                            last.then_inc(pe_done, 1)
                        for j in range(G):
                            from_act(f"v{n}", j)
                            nc.tensor.matmul(ps(f"s{n}", j)[:, 0, :], b["kdec"][j][:, n, :], b["vnew"][j][:, n, :],
                                             start=True, stop=True).then_inc(pe_done, 1)
                        for j in range(G):
                            if n:
                                nc.tensor.matmul(ps(f"o{n}", j)[:, 0, :], b["qg"][j][:, n, :], state[j][:],
                                                 start=True, stop=False)
                            nc.tensor.matmul(ps(f"o{n}", j)[:, 0, :], b["attnT"][j][:, n, :], b["vnew"][j][:, n, :],
                                             start=(n == 0), stop=True).then_inc(pe_done, 1)

            @block.scalar
            def _(act):
                starts_at_one(act, act_done)
                with act.Fori(0, H // G) as i:
                    def do(step, make, pes=(), dves=(), acts=()):
                        for j in range(G):
                            for p in pes:
                                act.wait_ge(pe_done, PE_STEPS.after(i, p, j))
                            for d in dves:
                                act.wait_ge(dve_done, DVE_STEPS.after(i, d, j))
                            for a in acts:
                                act.wait_ge(act_done, ACT_STEPS.after(i, a, j))
                            make(j).then_inc(act_done, 1)

                    def copy(step):
                        do(step, lambda j: nc.scalar.copy(b[step][j][:], ps(step, j)[:]), pes=[step])

                    act.wait_ge(pe_done, PE_STEPS.rounds(i))
                    act.wait_ge(dve_done, DVE_STEPS.rounds(i))
                    do("gB", lambda j: nc.scalar.copy(b["gB"][j][:], gate["g"][:, :, bass.ds(i * G + j, 1)].broadcast_to([P, C, P])))
                    for part, step in ((1, "kS"), (2, "vS")):
                        do(step, lambda j: nc.scalar.copy(b[step][j][:].rearrange("p n t -> p (n t)").unsqueeze(1),
                                                          qkvT[:, bass.ds(i * G + j + part * H, 1), :]))
                    do("dec", lambda j: nc.scalar.activation(b["gap"][j][:], b["gap"][j][:], ACT.Exp, scale=-1.0), dves=["gap"])
                    do("expRow", lambda j: nc.scalar.activation(b["expRow"][j][:], ps("row", j)[:], ACT.Exp), pes=["row"])
                    do("decMT", lambda j: nc.scalar.copy(b["decMT"][j][:], ps("decT", j)[:]), pes=["decT"])
                    do("U", lambda j: nc.scalar.copy(b["U"][j][:], ps("LT", j)[:]), pes=["LT"])
                    copy("L2")
                    do("L4", lambda j: nc.scalar.copy(b["L4"][j][:], ps("L4", j)[:]), pes=["L4"])
                    copy("L8")
                    copy("YT")
                    copy("N")
                    copy("N2")
                    copy("N4T")
                    do("wT", lambda j: nc.scalar.mul(b["wT"][j][:], ps("wT", j)[:], -1.0), pes=["wT"])
                    for n in range(C):
                        do(f"v{n}", lambda j: nc.scalar.copy(b["vnew"][j][:, n, :], ps(f"v{n}", j)[:, 0, :]), pes=[f"v{n}"])
                        do(f"o{n}", lambda j: nc.scalar.copy(o[:, n, bass.ds((i * G + j) * P, P)], ps(f"o{n}", j)[:, 0, :]), pes=[f"o{n}"])
                act.wait_ge(act_done, ACT_STEPS.rounds(H // G))

            @block.vector
            def _(dve):
                starts_at_one(dve, dve_done)
                with dve.Fori(0, H // G) as i:
                    def do(step, make, pes=(), acts=(), dves=()):
                        for j in range(G):
                            for p in pes:
                                dve.wait_ge(pe_done, PE_STEPS.after(i, p, j))
                            for a in acts:
                                dve.wait_ge(act_done, ACT_STEPS.after(i, a, j))
                            for d in dves:
                                dve.wait_ge(dve_done, DVE_STEPS.after(i, d, j))
                            make(j).then_inc(dve_done, 1)

                    def col(m, j):
                        return gate[m][:, :, bass.ds(i * G + j, 1)].broadcast_to([P, C, P])

                    tt = nc.vector.tensor_tensor

                    def gaps(j):
                        for n in range(C):
                            last = nc.vector.tensor_scalar(b["gap"][j][:, n, :], ps("row", j)[:, n, :],
                                                           gate["sum"][:, n, bass.ds(i * G + j, 1)], 0.0, ALU.subtract, ALU.max)
                        return last

                    def lows(j):
                        for n in range(C):
                            last = nc.vector.scalar_tensor_tensor(b["L"][j][:, n, :], ps("kk", j)[:, n, :],
                                                                  gate["beta"][:, n, bass.ds(i * G + j, 1)],
                                                                  b["decM"][j][:, n, :], ALU.mult, ALU.mult)
                        return last

                    do("gap", gaps, pes=["row"])
                    do("decM", lambda j: tt(b["decM"][j][:], b["gap"][j][:], lower4, ALU.mult), acts=["dec"])
                    do("qg", lambda j: tt(b["qg"][j][:].rearrange("p n t -> p (n t)").unsqueeze(1),
                                          qkvT[:, bass.ds(i * G + j, 1), :],
                                          b["expRow"][j][:].rearrange("p n t -> p (n t)").unsqueeze(1), ALU.mult), acts=["expRow"])
                    do("kbg", lambda j: tt(b["kbg"][j][:], ps("knat", j)[:], col("beta_exp", j), ALU.mult), pes=["knat"])
                    do("kdec", lambda j: tt(b["kdec"][j][:], ps("knat", j)[:], col("rest", j), ALU.mult))
                    do("vb", lambda j: tt(b["vb"][j][:], ps("vnat", j)[:], col("beta", j), ALU.mult), pes=["vnat"])
                    do("L0", lows, pes=["kk"], dves=["decM"])
                    do("L", lambda j: tt(b["L"][j][:], b["L"][j][:], strict4, ALU.mult), dves=["L0"])
                    do("attnT", lambda j: tt(b["attnT"][j][:], ps("qk", j)[:], b["decMT"][j][:], ALU.mult), pes=["qk"], acts=["decMT"])
                    do("LD", lambda j: tt(b["LD"][j][:], b["L"][j][:], block4, ALU.mult), dves=["L"])
                    do("UD", lambda j: tt(b["UD"][j][:], b["U"][j][:], block4, ALU.mult), acts=["U"])
                    do("UO", lambda j: tt(b["UO"][j][:], b["U"][j][:], b["UD"][j][:], ALU.subtract), dves=["UD"])
                    do("Y0", lambda j: tt(b["Y0"][j][:], ident4, b["UD"][j][:], ALU.subtract))
                    do("U2", lambda j: nc.vector.tensor_copy(b["U2"][j][:], ps("U2", j)[:]), pes=["U2"])
                    do("Y1", lambda j: tt(b["Y1"][j][:], b["Y0"][j][:], ps("Y1", j)[:], ALU.add), pes=["Y1"])
                    do("U4", lambda j: nc.vector.tensor_copy(b["U4"][j][:], ps("U4", j)[:]), pes=["U4"])
                    do("Y2", lambda j: tt(b["Y2"][j][:], b["Y1"][j][:], ps("Y2", j)[:], ALU.add), pes=["Y2"], dves=["Y1"])
                    do("Y3", lambda j: tt(b["Y3"][j][:], b["Y2"][j][:], ps("Y3", j)[:], ALU.add), pes=["Y3"], dves=["Y2"])
                    do("NT", lambda j: nc.vector.tensor_copy(b["NT"][j][:], ps("NT", j)[:]), pes=["NT"])
                    do("W0", lambda j: tt(b["W0"][j][:], b["Y3"][j][:], ps("W0", j)[:], ALU.subtract), pes=["W0"])
                    do("N2T", lambda j: nc.vector.tensor_copy(b["N2T"][j][:], ps("N2T", j)[:]), pes=["N2T"])
                    do("W1", lambda j: tt(b["W1"][j][:], b["W0"][j][:], ps("W1", j)[:], ALU.add), pes=["W1"], dves=["W0"])
                    do("W2", lambda j: tt(b["W2"][j][:], b["W1"][j][:], ps("W2", j)[:], ALU.add), pes=["W2"], dves=["W1"])
                    do("s0", lambda j: nc.vector.tensor_copy(state[j][:], ps("s0", j)[:, 0, :]), pes=["s0"])
                    for n in range(1, C):
                        do(f"s{n}", lambda j: nc.vector.scalar_tensor_tensor(
                            state[j][:], state[j][:], gate["last"][:, n, bass.ds(i * G + j, 1)], ps(f"s{n}", j)[:, 0, :],
                            ALU.mult, ALU.add), pes=[f"s{n}", f"o{n}"], dves=[f"s{n - 1}"])
                dve.wait_ge(dve_done, DVE_STEPS.rounds(H // G))


def gdn_gate_out(nc, c, name, o, z, norm_g):
    H, L = GDN_HEADS, TT * GDN_HEADS
    with Stage(nc, name) as s:
        sq = s.sb("sq", [P, L, P])
        ss = s.sb("ss", [P, L])
        grow = s.sb("grow", [P, P])
        eps = s.sb("eps", [P, 1])
        load, ready, squared, summed, rooted = (s.sem(n) for n in ("load", "ready", "squared", "summed", "rooted"))
        inverted, scaled, gained, gated = (s.sem(n) for n in ("inverted", "scaled", "gained", "gated"))
        o3 = o[:].rearrange("p t (h d) -> p (t h) d", d=P)
        z3 = z[:].rearrange("p t (h d) -> p (t h) d", d=P)
        tile = lambda t: slice(t * H, (t + 1) * H)
        with s.block() as block:
            @block.sync
            def _(sp):
                sp.dma_start(grow[:], norm_g.broadcast_to([P, P])).then_inc(load, 16)

            @block.scalar
            def _(act):
                for t in range(TT):
                    nc.scalar.activation(sq[:, tile(t), :], o3[:, tile(t), :], ACT.Square).then_inc(squared, 1)
                act.wait_ge(ready, 1)
                act.wait_ge(summed, TT)
                nc.scalar.activation(ss[:], ss[:], ACT.Sqrt, bias=eps[:], scale=1.0 / P).then_inc(rooted, 1)

            @block.gpsimd
            def _(pool):
                pool.wait_ge(load, 16)
                for t in range(TT):
                    nc.gpsimd.tensor_tensor(z3[:, tile(t), :], z3[:, tile(t), :], grow[:].unsqueeze(1).broadcast_to([P, H, P]),
                                            ALU.mult).then_inc(gained, 1)

            @block.vector
            def _(dve):
                nc.vector.memset(eps[:], RMS_EPS).then_inc(ready, 1)
                for t in range(TT):
                    dve.wait_ge(squared, t + 1)
                    nc.vector.tensor_reduce(ss[:, tile(t)], sq[:, tile(t), :], axis=AX.X, op=ALU.add).then_inc(summed, 1)
                dve.wait_ge(rooted, 1)
                nc.vector.reciprocal(ss[:], ss[:]).then_inc(inverted, 1)
                dve.wait_ge(inverted, 1)
                for t in range(TT):
                    nc.vector.tensor_tensor(o3[:, tile(t), :], o3[:, tile(t), :],
                                            ss[:, tile(t)].unsqueeze(2).broadcast_to([P, H, P]), ALU.mult).then_inc(scaled, 1)
                for t in range(TT):
                    dve.wait_ge(scaled, t + 1)
                    dve.wait_ge(gained, t + 1)
                    nc.vector.tensor_tensor(o3[:, tile(t), :], o3[:, tile(t), :], z3[:, tile(t), :], ALU.mult).then_inc(gated, 1)
                dve.wait_ge(gated, TT)


class TileNorm:

    ON_POOL = TT // 2

    def __init__(self, nc, s, h, ln_g, ln_b):
        self.nc, self.h, self.ln_g, self.ln_b = nc, h, ln_g, ln_b
        self.gain, self.bias = s.sb("gain", [P, D]), s.sb("bias", [P, D])
        self.stats, self.mv = s.sb("stats", [P, TT, 2, 6]), s.sb("mv", [P, TT, 2])
        self.inv, self.shift, self.eps = s.sb("inv", [P, TT]), s.sb("shift", [P, TT]), s.sb("eps", [P, 1])
        self.loaded, self.own, self.measured, self.rooted, self.inverted, self.centred, self.gained, self.done, self.biased = (
            s.sem(n) for n in ("norm_loaded", "own", "measured", "rooted", "inverted", "centred", "gained", "done", "biased"))

    def load(self, sp):
        sp.dma_start(self.gain[:], self.ln_g.broadcast_to([P, D])).then_inc(self.loaded, 16)
        sp.dma_start(self.bias[:], self.ln_b.broadcast_to([P, D])).then_inc(self.loaded, 16)

    def begin(self, dve):
        self.chain = Chain(dve, self.own)
        self.chain.link(self.nc.vector.memset(self.eps[:], LN_EPS))

    def stat_step(self, dve, t):
        v, h = self.nc.vector, self.h
        for half in range(2):
            last = v.bn_stats(self.stats[:, t, half, :], h[:, t, half * BANK:(half + 1) * BANK])
        self.chain.link(last)
        v.bn_aggr(self.mv[:, t, :], self.stats[:, t, :, :]).then_inc(self.measured, 1)

    def invert_step(self, dve, t):
        v, inv, at = self.nc.vector, self.inv, slice(t, t + 1)
        dve.wait_ge(self.rooted, t + 1)
        self.chain.link(v.reciprocal(inv[:, at], inv[:, at]))
        v.scalar_tensor_tensor(self.shift[:, at], self.mv[:, t, 0:1], -1.0, inv[:, at], ALU.mult, ALU.mult).then_inc(self.inverted, 1)

    def gain_step(self, dve, t):
        dve.wait_ge(self.loaded, 32)
        dve.wait_ge(self.centred, t + 1)
        self.nc.vector.tensor_tensor(self.h[:, t, :], self.h[:, t, :], self.gain[:], ALU.mult).then_inc(self.gained, 1)

    def end(self, dve):
        for t in range(self.ON_POOL, TT):
            dve.wait_ge(self.gained, t + 1)
            self.nc.vector.tensor_tensor(self.h[:, t, :], self.h[:, t, :], self.bias[:], ALU.add).then_inc(self.biased, 1)
        dve.wait_ge(self.biased, TT - self.ON_POOL)

    def on_act(self, act):
        for t in range(TT):
            act.wait_ge(self.measured, t + 1)
            self.nc.scalar.activation(self.inv[:, t:t + 1], self.mv[:, t, 1:2], ACT.Sqrt, bias=self.eps[:]).then_inc(self.rooted, 1)
            act.wait_ge(self.inverted, t + 1)
            self.nc.scalar.activation(self.h[:, t, :], self.h[:, t, :], ACT.Identity, bias=self.shift[:, t:t + 1],
                                      scale=self.inv[:, t:t + 1]).then_inc(self.centred, 1)

    def on_pool(self, pool):
        pool.wait_ge(self.loaded, 32)
        for t in range(self.ON_POOL):
            pool.wait_ge(self.gained, t + 1)
            self.nc.gpsimd.tensor_tensor(self.h[:, t, :], self.h[:, t, :], self.bias[:], ALU.add).then_inc(self.done, 1)
        pool.wait_ge(self.done, self.ON_POOL)


def project_out(nc, c, name, o, w_out, h, ln_g, ln_b):
    SLABS = D // SLAB
    with Stage(nc, name) as s:
        oTh, oTl = s.sb("oTh", [P, KC, SEQ], F32R), s.sb("oTl", [P, KC, SEQ], F32R)
        bank = [s.ps(f"bank{i}", [P, BANK]) for i in range(HALVES * TT)]
        made, added = s.sem("made"), s.sem("added")
        slabs = Slabs(nc, s, w_out.rearrange("(k p) (s n) -> s p k n", p=P, n=SLAB), made, share=TT)
        turn = SplitTranspose(nc, s, c, o, oTh, oTl, bank[TT:])
        norm = TileNorm(nc, s, h, ln_g, ln_b)
        with s.block() as block:
            @block.sync
            def _(sp):
                for n in range(SLABS):
                    slabs.load(sp, 0, n)
                norm.load(sp)

            @block.tensor
            def _(pe):
                pe.sem_inc(made, 2 * TT)
                turn.on_pe(pe)
                turn.finished(pe)
                for n in range(SLABS):
                    slabs.wait(pe, 0, n)
                    half, at = n * SLAB // BANK, n * SLAB % BANK
                    for t in range(TT):
                        slabs.tokens(nc, bank[half * TT + t][:, at:at + SLAB], n, t, oTh, oTl).then_inc(made, 1)

            @block.vector
            def _(dve):
                turn.on_dve(dve)
                norm.begin(dve)

                def add(half, t):
                    dve.wait_ge(made, ((half + 1) * (BANK // SLAB) - 1 + 2) * TT + t + 1)
                    piece = h[:, t, half * BANK:(half + 1) * BANK]
                    nc.vector.scalar_tensor_tensor(piece, piece, ALPHA, bank[half * TT + t][:], ALU.mult, ALU.add).then_inc(added, 1)

                for t in range(TT):
                    add(0, t)
                for t in range(TT):
                    add(1, t)
                    dve.wait_ge(added, TT + t + 1)
                    norm.stat_step(dve, t)
                    norm.invert_step(dve, t)
                    if t:
                        norm.gain_step(dve, t - 1)
                norm.gain_step(dve, TT - 1)
                norm.end(dve)

            @block.scalar
            def _(act):
                turn.on_act(act)
                for n in range(SLABS):
                    slabs.split_high(act, 0, n, 0)
                norm.on_act(act)

            @block.gpsimd
            def _(pool):
                pool.sem_inc(slabs.low_ready, 2)
                for n in range(SLABS):
                    slabs.split_low(pool, 0, n)
                norm.on_pool(pool)


def normalize(nc, c, name, h, ln_g, ln_b, out=None):
    with Stage(nc, name) as s:
        stored = s.sem("stored")
        norm = TileNorm(nc, s, h, ln_g, ln_b)
        with s.block() as block:
            @block.sync
            def _(sp):
                norm.load(sp)
                if out is not None:
                    for t in range(TT):
                        if t < norm.ON_POOL:
                            sp.wait_ge(norm.done, t + 1)
                        else:
                            sp.wait_ge(norm.biased, t - norm.ON_POOL + 1)
                        sp.dma_start(out[:, t, :], h[:, t, :]).then_inc(stored, 16)
                    sp.wait_ge(stored, 16 * TT)

            @block.vector
            def _(dve):
                norm.begin(dve)
                norm.stat_step(dve, 0)
                for t in range(TT):
                    if t + 1 < TT:
                        norm.stat_step(dve, t + 1)
                    norm.invert_step(dve, t)
                    if t:
                        norm.gain_step(dve, t - 1)
                norm.gain_step(dve, TT - 1)
                norm.end(dve)

            @block.scalar
            def _(act):
                norm.on_act(act)

            @block.gpsimd
            def _(pool):
                norm.on_pool(pool)


def gdn_layer(nc, c, h, w_in, conv_w, a_log, dt_bias, norm_g, w_out, ln_g, ln_b):
    with Stage(nc, "gdn") as s:
        o, z = s.sb("o", [P, TT, D]), s.sb("z", [P, TT, D])
        gate = {n: s.sb(n, [P, TT, GDN_HEADS]) for n in ("g", "sum", "last", "rest", "exp", "beta", "beta_exp")}
        with Stage(nc, "gdn_in") as s1:
            qkvT = s1.sb("qkvT", [P, GDN_QKV, SEQ])
            logits = s1.sb("logits", [P, TT, 2 * GDN_HEADS])
            with Stage(nc, "gdn_x") as s2:
                xTh, xTl = s2.sb("xTh", [P, KC, SEQ], F32R), s2.sb("xTl", [P, KC, SEQ], F32R)
                gdn_project(nc, c, "gdnp", h, xTh, xTl, w_in, conv_w, qkvT, z, logits)
            gdn_normalize(nc, c, "gdnn", qkvT)
            gdn_gates(nc, c, "gdng", logits, a_log, dt_bias, gate)
            gdn_recur(nc, c, "gdnr", qkvT, gate, o)
        gdn_gate_out(nc, c, "gdno", o, z, norm_g)
        project_out(nc, c, "gdnq", o, w_out, h, ln_g, ln_b)


MLA_HEADS, NOPE, ROPE, VDIM = 16, 64, 32, 64
QK = NOPE + ROPE
HALF = ROPE // 2
KV_RANK, Q_RANK = 256, 384
THETA = 10000.0
TWO_PI = 2.0 * math.pi


def parts_of(x, bits, n):
    parts = []
    for _ in range(n - 1):
        unit = 2.0 ** (math.floor(math.log2(abs(x))) + 1 - bits)
        parts.append(math.floor(x / unit) * unit)
        x -= parts[-1]
    return parts + [x]


def rope_tables(nc, c, name, positions, cos, sin):
    MAGIC = 1.5 * 2.0 ** 23
    EDGE = 3.1415925
    with Stage(nc, name) as s:
        posi, pos = s.sb("posi", [P, TT], I32), s.sb("pos", [P, TT])
        freq = s.sb("freq", [P, HALF])
        ang, turns, low = s.sb("ang", [P, TT, HALF]), s.sb("turns", [P, TT, HALF]), s.sb("low", [P, TT, HALF])
        load, chain, acted = s.sem("load"), s.sem("chain"), s.sem("acted")
        with s.block() as block:
            @block.sync
            def _(sp):
                with nc.allow_non_contiguous_dma(reason="one position per partition"):
                    sp.dma_start(posi[:], positions.rearrange("a (t p) -> p (a t)", p=P)).then_inc(load, 16)

            @block.vector
            def _(dve):
                ch = Chain(dve, chain)
                for i in range(HALF):
                    last = nc.vector.memset(freq[:, i:i + 1], THETA ** (-i / HALF))
                dve.wait_ge(load, 16)
                ch.link(nc.vector.tensor_copy(pos[:], posi[:]))
                ch.link(nc.vector.tensor_tensor(ang[:], pos[:].unsqueeze(2).broadcast_to([P, TT, HALF]),
                                                freq[:].unsqueeze(1).broadcast_to([P, TT, HALF]), ALU.mult))
                for out, quarter in ((sin, 0.0), (cos, 0.25)):
                    ch.link(nc.vector.tensor_scalar(turns[:], ang[:], 1.0 / TWO_PI, quarter, ALU.mult, ALU.add))
                    ch.link(nc.vector.tensor_scalar(turns[:], turns[:], MAGIC, None, ALU.add))
                    ch.link(nc.vector.tensor_scalar(turns[:], turns[:], MAGIC, None, ALU.subtract))
                    src = ang
                    for part in parts_of(TWO_PI, 9, 3):
                        ch.link(nc.vector.scalar_tensor_tensor(low[:], turns[:], -part, src[:], ALU.mult, ALU.add))
                        src = low
                    ch.link(nc.vector.tensor_scalar(low[:], low[:], quarter * TWO_PI, EDGE, ALU.add, ALU.min))
                    ch.link(nc.vector.tensor_scalar(out[:], low[:], -EDGE, None, ALU.max))

            @block.scalar
            def _(act):
                act.wait_ge(chain, 2 + 8)
                nc.scalar.activation(sin[:], sin[:], ACT.Sin).then_inc(acted, 1)
                act.wait_ge(chain, 2 + 16)
                nc.scalar.activation(cos[:], cos[:], ACT.Sin).then_inc(acted, 1)
                act.wait_ge(acted, 2)


def mla_project(nc, c, name, h, w_kv_a, kv_norm_g, w_uk, w_uv, w_qa, q_norm_g, w_qb, cos, sin, q, k, v):
    KV = KV_RANK + ROPE
    with Stage(nc, name) as s:
        hT = s.sb("hT", [P, KC, SEQ])
        wkv, wqa = s.sb("wkv", [P, KC, KV]), s.sb("wqa", [P, KC, Q_RANK])
        wuk, wuv = s.sb("wuk", [P, KV_RANK // P, D]), s.sb("wuv", [P, KV_RANK // P, D])
        wqb = s.sb("wqb", [P, Q_RANK // P, MLA_HEADS * QK])
        gkv, gq = s.sb("gkv", [P, KV_RANK]), s.sb("gq", [P, Q_RANK])
        kv, qa = s.sb("kv", [P, TT, KV]), s.sb("qa", [P, TT, Q_RANK])
        sq = s.sb("sq", [P, TT, Q_RANK])
        ss, sr, eps = s.sb("ss", [P, TT]), s.sb("sr", [P, TT]), s.sb("eps", [P, 1])
        kvT, qaT = s.sb("kvT", [P, KV_RANK // P, SEQ]), s.sb("qaT", [P, Q_RANK // P, SEQ])
        kr = s.sb("kr", [P, TT, ROPE])
        tmp = [sq[:, :, 0:MLA_HEADS * HALF].rearrange("p t (h d) -> p t h d", d=HALF), s.sb("tmp", [P, TT, MLA_HEADS, HALF])[:]]
        bank = [s.ps(f"bank{i}", [P, BANK]) for i in range(4)]
        load = [s.sem(f"load{i}") for i in range(4)]
        made, taken, chain, rooted = s.sem("made"), s.sem("taken"), s.sem("chain"), s.sem("rooted")
        kvready, qaready = s.sem("kvready"), s.sem("qaready")
        rows = lambda w: w.rearrange("(k p) n -> p k n", p=P)
        with s.block() as block:
            @block.sync
            def _(sp):
                sp.dma_start(wkv[:], rows(w_kv_a)).then_inc(load[0], 16)
                sp.dma_start(wqa[:], rows(w_qa)).then_inc(load[1], 16)
                sp.dma_start(gkv[:], kv_norm_g.unsqueeze(0).broadcast_to([P, KV_RANK])).then_inc(load[2], 16)
                sp.dma_start(gq[:], q_norm_g.broadcast_to([P, Q_RANK])).then_inc(load[2], 16)
                sp.dma_start(wuk[:], rows(w_uk)).then_inc(load[3], 16)
                sp.dma_start(wuv[:], rows(w_uv)).then_inc(load[3], 16)
                sp.dma_start(wqb[:], rows(w_qb)).then_inc(load[3], 16)

            NT = (KV_RANK + Q_RANK) // P
            up = [("k", b) for b in range(2)] + [("v", b) for b in range(2)] + [("q", b) for b in range(3)]

            @block.tensor
            def _(pe):
                n = 0

                def slot():
                    if n >= 4:
                        pe.wait_ge(taken, n - 3)
                    return bank[n % 4]

                for kc in range(KC):
                    out = slot()
                    for t in range(TT):
                        last = nc.tensor.transpose(out[:, t * P:(t + 1) * P], h[:, t, kc * P:(kc + 1) * P], c["ident"][:])
                    last.then_inc(made, 1)
                    n += 1
                pe.wait_ge(taken, KC)
                for w, width, sem in ((wkv, KV, load[0]), (wqa, Q_RANK, load[1])):
                    pe.wait_ge(sem, 16)
                    for t in range(TT):
                        out = slot()
                        for kc in range(KC):
                            last = nc.tensor.matmul(out[:, 0:width], hT[:, kc, t * P:(t + 1) * P], w[:, kc, :],
                                                    start=(kc == 0), stop=(kc == KC - 1))
                        last.then_inc(made, 1)
                        n += 1
                for src, chunks, ready in ((kv, KV_RANK // P, kvready), (qa, Q_RANK // P, qaready)):
                    pe.wait_ge(ready, 1)
                    for kc in range(chunks):
                        out = slot()
                        for t in range(TT):
                            last = nc.tensor.transpose(out[:, t * P:(t + 1) * P], src[:, t, kc * P:(kc + 1) * P], c["ident"][:])
                        last.then_inc(made, 1)
                        n += 1
                pe.wait_ge(load[3], 48)
                pe.wait_ge(taken, n)
                for t in range(TT):
                    for what, b in up:
                        srcT, w = {"k": (kvT, wuk), "v": (kvT, wuv), "q": (qaT, wqb)}[what]
                        chunks = srcT.shape[1]
                        out = slot()
                        for kc in range(chunks):
                            last = nc.tensor.matmul(out[:], srcT[:, kc, t * P:(t + 1) * P], w[:, kc, b * BANK:(b + 1) * BANK],
                                                    start=(kc == 0), stop=(kc == chunks - 1))
                        last.then_inc(made, 1)
                        n += 1

            @block.scalar
            def _(act):
                n = 0
                for kc in range(KC):
                    act.wait_ge(made, n + 1)
                    nc.scalar.copy(hT[:, kc, :], bank[n % 4][:]).then_inc(taken, 1)
                    n += 1
                for dst, width in ((kv, KV), (qa, Q_RANK)):
                    for t in range(TT):
                        act.wait_ge(made, n + 1)
                        nc.scalar.copy(dst[:, t, :], bank[n % 4][:, 0:width]).then_inc(taken, 1)
                        n += 1
                for done in (3, 8):
                    act.wait_ge(chain, done)
                    width = KV_RANK if done == 3 else Q_RANK
                    nc.scalar.activation(sr[:], ss[:], ACT.Sqrt, bias=eps[:], scale=1.0 / width).then_inc(rooted, 1)
                for dstT in (kvT, qaT):
                    for kc in range(dstT.shape[1]):
                        act.wait_ge(made, n + 1)
                        nc.scalar.copy(dstT[:, kc, :], bank[n % 4][:]).then_inc(taken, 1)
                        n += 1
                for t in range(TT):
                    for what, b in up:
                        act.wait_ge(made, n + 1)
                        if what == "k":
                            dst = k[:, t, 8 * b:8 * b + 8, 0:NOPE]
                            src = bank[n % 4][:].rearrange("p (h d) -> p h d", d=NOPE)
                        else:
                            flat = v[:, t, :] if what == "v" else q[:, t].rearrange("p h d -> p (h d)")
                            dst, src = flat[:, b * BANK:(b + 1) * BANK], bank[n % 4][:]
                        nc.scalar.copy(dst, src).then_inc(taken, 1)
                        n += 1

            @block.vector
            def _(dve):
                ch = Chain(dve, chain)
                ch.link(nc.vector.memset(eps[:], RMS_EPS))
                for at, (m, width, g, ready) in enumerate(((kv, KV_RANK, gkv, kvready), (qa, Q_RANK, gq, qaready))):
                    x = m[:, :, 0:width]
                    dve.wait_ge(taken, KC + TT * (at + 1))
                    ch.link(nc.vector.tensor_tensor(sq[:, :, 0:width], x, x, ALU.mult))
                    ch.link(nc.vector.tensor_reduce(ss[:], sq[:, :, 0:width], axis=AX.X, op=ALU.add))
                    dve.wait_ge(rooted, at + 1)
                    ch.link(nc.vector.reciprocal(sr[:], sr[:]))
                    ch.link(nc.vector.tensor_tensor(x, x, sr[:].unsqueeze(2).broadcast_to([P, TT, width]), ALU.mult))
                    dve.wait_ge(load[2], 32)
                    last = nc.vector.tensor_tensor(x, x, g[:].unsqueeze(1).broadcast_to([P, TT, width]), ALU.mult)
                    last.then_inc(ready, 1)
                    if at == 0:
                        ch.link(nc.vector.memset(ss[:, 0:1], 0.0))

                def rotate(out, x, heads):
                    cs = cos[:].unsqueeze(2).broadcast_to([P, TT, heads, HALF])
                    sn = sin[:].unsqueeze(2).broadcast_to([P, TT, heads, HALF])
                    x1, x2 = x[:, :, :, 0:HALF], x[:, :, :, HALF:ROPE]
                    a, b = tmp[0][:, :, 0:heads, :], tmp[1][:, :, 0:heads, :]
                    nc.vector.tensor_tensor(a, x2, sn, ALU.mult)
                    ch.link(nc.vector.tensor_tensor(b, x1, sn, ALU.mult))
                    nc.vector.tensor_tensor(out[:, :, :, 0:HALF], x1, cs, ALU.mult)
                    ch.link(nc.vector.tensor_tensor(out[:, :, :, HALF:ROPE], x2, cs, ALU.mult))
                    nc.vector.tensor_tensor(out[:, :, :, 0:HALF], out[:, :, :, 0:HALF], a, ALU.subtract)
                    ch.link(nc.vector.tensor_tensor(out[:, :, :, HALF:ROPE], out[:, :, :, HALF:ROPE], b, ALU.add))

                rotate(kr[:].unsqueeze(2), kv[:, :, KV_RANK:].unsqueeze(2), 1)
                ch.link(nc.vector.tensor_copy(k[:, :, :, NOPE:], kr[:].unsqueeze(2).broadcast_to([P, TT, MLA_HEADS, ROPE])))
                dve.wait_ge(taken, KC + 2 * TT + NT + TT * len(up))
                rotate(q[:, :, :, NOPE:], q[:, :, :, NOPE:], MLA_HEADS)


def mla_attend(nc, c, name, q, k, v, o):
    G = 2
    SCALE = QK ** -0.5
    PE_STEPS = Steps("qT kT s3 s0 s2 s1 p3 p02 p1 o", G)
    ACT_STEPS = Steps("qs ks qT e3 e0 e2 e1 p3", G)
    DVE_STEPS = Steps("kT x3 x0 x2 x1 nb p02 p1 rr o", G)
    with Stage(nc, name) as s:
        far = s.sb("far", [P, P])
        qs, ks = ([s.sb(f"{n}{j}", [P, TT, QK]) for j in range(G)] for n in ("qs", "ks"))
        qT, kT = ([s.sb(f"{n}{j}", [P, SEQ]) for j in range(G)] for n in ("qT", "kT"))
        prob = [[s.sb(f"prob{j}_{i}", [P, (i + 1) * P]) for i in range(TT)] for j in range(G)]
        probT = [[s.sb(f"probT{j}_{i}", [P, i + 1, P]) for i in range(TT)] for j in range(G)]
        mx, nb, rs = ([s.sb(f"{n}{j}", [P, TT]) for j in range(G)] for n in ("mx", "nb", "rs"))
        A, B, Cb, E = ([s.ps(f"{n}{j}", [P, BANK]) for j in range(G)] for n in ("A", "B", "C", "E"))
        pe_done, act_done, dve_done, masked = s.sem("pe_done"), s.sem("act_done"), s.sem("dve_done"), s.sem("masked")
        spot = {3: (A, 0), 0: (B, 0), 2: (B, P), 1: (Cb, 0)}

        def score(i, j):
            m, at = spot[i]
            return m[j][:, at:at + (i + 1) * P]

        with s.block() as block:
            @block.tensor
            def _(pe):
                pe.wait_ge(masked, 1)
                starts_at_one(pe, pe_done)
                with pe.Fori(0, MLA_HEADS // G) as r:
                    def act_at(step, j):
                        pe.wait_ge(act_done, ACT_STEPS.after(r, step, j))

                    def dve_at(step, j):
                        pe.wait_ge(dve_done, DVE_STEPS.after(r, step, j))

                    for src, dst, step in ((qs, E, "qs"), (ks, A, "ks")):
                        for j in range(G):
                            act_at(step, j)
                            for t in range(TT):
                                last = nc.tensor.transpose(dst[j][0:QK, t * P:(t + 1) * P], src[j][:, t, :], c["ident"][:])
                            last.then_inc(pe_done, 1)
                    for i in (3, 0, 2, 1):
                        for j in range(G):
                            if i == 3:
                                act_at("qT", j)
                                dve_at("kT", j)
                            sc = score(i, j)
                            nc.tensor.matmul(sc, qT[j][0:QK, i * P:(i + 1) * P], kT[j][0:QK, 0:(i + 1) * P], start=True, stop=False)
                            nc.tensor.matmul(sc[:, i * P:], c["ident"][:], far[:], start=False, stop=True).then_inc(pe_done, 1)
                    for step, dst, tiles, ready in (("p3", A, (3,), "e3"), ("p02", B, (0, 2), "e2"), ("p1", E, (1,), "e1")):
                        for j in range(G):
                            act_at(ready, j)
                            col = 0
                            for i in tiles:
                                for kt in range(i + 1):
                                    last = nc.tensor.transpose(dst[j][:, col:col + P], prob[j][i][:, kt * P:(kt + 1) * P], c["ident"][:])
                                    col += P
                            last.then_inc(pe_done, 1)
                    for j in range(G):
                        act_at("p3", j)
                        dve_at("p1", j)
                        for i in range(TT):
                            for kt in range(i + 1):
                                last = nc.tensor.matmul(Cb[j][:, 256 + i * VDIM:256 + (i + 1) * VDIM], probT[j][i][:, kt, :],
                                                        v[:, kt, bass.ds((r * G + j) * VDIM, VDIM)], start=(kt == 0), stop=(kt == i))
                        last.then_inc(pe_done, 1)

            @block.scalar
            def _(act):
                starts_at_one(act, act_done)
                with act.Fori(0, MLA_HEADS // G) as r:
                    def pe_at(step, j):
                        act.wait_ge(pe_done, PE_STEPS.after(r, step, j))

                    for dst, src in ((qs, q), (ks, k)):
                        for j in range(G):
                            nc.scalar.copy(dst[j][:].unsqueeze(2), src[:, :, bass.ds(r * G + j, 1), :]).then_inc(act_done, 1)
                    for j in range(G):
                        pe_at("qT", j)
                        nc.scalar.copy(qT[j][0:QK, :], E[j][0:QK, :]).then_inc(act_done, 1)
                    for i in (3, 0, 2, 1):
                        for j in range(G):
                            if i == 3:
                                act.wait_ge(dve_done, DVE_STEPS.after(r, "nb", j))
                            nc.scalar.activation(prob[j][i][:], score(i, j), ACT.Exp, bias=nb[j][:, i:i + 1], scale=SCALE,
                                                 accum_out=rs[j][:, i:i + 1]).then_inc(act_done, 1)
                    for j in range(G):
                        pe_at("p3", j)
                        nc.scalar.copy(probT[j][3][:].rearrange("p k q -> p (k q)"), A[j][:]).then_inc(act_done, 1)

            @block.vector
            def _(dve):
                nc.vector.tensor_scalar(far[:], c["lower"][:], -1.0, 1.0e30, ALU.add, ALU.mult).then_inc(masked, 1)
                starts_at_one(dve, dve_done)
                with dve.Fori(0, MLA_HEADS // G) as r:
                    def pe_at(step, j):
                        dve.wait_ge(pe_done, PE_STEPS.after(r, step, j))

                    for j in range(G):
                        pe_at("kT", j)
                        nc.vector.tensor_copy(kT[j][0:QK, :], A[j][0:QK, :]).then_inc(dve_done, 1)
                    for i in (3, 0, 2, 1):
                        for j in range(G):
                            pe_at("s2" if i == 0 else f"s{i}", j)
                            nc.vector.tensor_reduce(mx[j][:, i:i + 1], score(i, j), axis=AX.X, op=ALU.max).then_inc(dve_done, 1)
                    for j in range(G):
                        dve.wait_ge(dve_done, DVE_STEPS.after(r, "x1", j))
                        nc.vector.tensor_scalar(nb[j][:], mx[j][:], -SCALE, None, ALU.mult).then_inc(dve_done, 1)
                    for j in range(G):
                        pe_at("p02", j)
                        nc.vector.tensor_copy(probT[j][0][:, 0, :], B[j][:, 0:P])
                        nc.vector.tensor_copy(probT[j][2][:].rearrange("p k q -> p (k q)"), B[j][:, P:]).then_inc(dve_done, 1)
                    for j in range(G):
                        pe_at("p1", j)
                        nc.vector.tensor_copy(probT[j][1][:].rearrange("p k q -> p (k q)"), E[j][:, 0:2 * P]).then_inc(dve_done, 1)
                    for j in range(G):
                        dve.wait_ge(act_done, ACT_STEPS.after(r, "e1", j))
                        nc.vector.reciprocal(rs[j][:], rs[j][:]).then_inc(dve_done, 1)
                    for j in range(G):
                        pe_at("o", j)
                        dve.wait_ge(dve_done, DVE_STEPS.after(r, "rr", j))
                        nc.vector.tensor_tensor(o[:, :, bass.ds((r * G + j) * VDIM, VDIM)],
                                                Cb[j][:, 256:].rearrange("p (t d) -> p t d", d=VDIM),
                                                rs[j][:].unsqueeze(2).broadcast_to([P, TT, VDIM]), ALU.mult).then_inc(dve_done, 1)
                dve.wait_ge(dve_done, DVE_STEPS.rounds(MLA_HEADS // G))


def mla_layer(nc, c, h, positions, w_kv_a, kv_norm_g, w_uk, w_uv, w_qa, q_norm_g, w_qb, w_out, ln_g, ln_b):
    with Stage(nc, "mla") as s:
        v = s.sb("v", [P, TT, MLA_HEADS * VDIM])
        o = s.sb("o", [P, TT, MLA_HEADS * VDIM])
        with Stage(nc, "mla_in") as s1:
            q, k = (s1.sb(n, [P, TT, MLA_HEADS, QK]) for n in ("q", "k"))
            cos, sin = (s1.sb(n, [P, TT, HALF]) for n in ("cos", "sin"))
            rope_tables(nc, c, "mlar", positions, cos, sin)
            mla_project(nc, c, "mlap", h, w_kv_a, kv_norm_g, w_uk, w_uv, w_qa, q_norm_g, w_qb, cos, sin, q, k, v)
            mla_attend(nc, c, "mlaa", q, k, v, o)
        project_out(nc, c, "mlaq", o, w_out, h, ln_g, ln_b)


def peer_layer(nc, c, name, h, w_q, sub_keys, u_tab, v_tab, gates, early):
    with Stage(nc, f"{name}h") as s:
        hTh, hTl = s.sb("hTh", [P, KC, SEQ], F32R), s.sb("hTl", [P, KC, SEQ], F32R)
        with Stage(nc, f"{name}k") as s1:
            giT = s1.sb("giT", [P, 3, SEQ])
            peer_select(nc, c, f"{name}s", h, hTh, hTl, w_q, sub_keys, giT, u_tab, early)
            peer_gates(nc, c, f"{name}g", h, giT, gates, hTh, hTl, u_tab, early)
        peer_experts(nc, c, f"{name}e", hTh, hTl, h, u_tab, v_tab, gates, early)


def yoco_trunk(nc, x, positions, a_w_in, a_conv_w, a_a_log, a_dt_bias, a_norm_g, a_w_out, kv_w_a, kv_norm_g, kv_w_uk,
               kv_w_uv, b_w_qa, b_q_norm_g, b_w_qb, b_w_out, peer_w_q, peer_sub_keys, peer_u, peer_v, ln_g, ln_b, out):
    gates = nc.dram_tensor("gates", [P, GRIDS, NKEYS, GRID], F32).ap()
    early = nc.dram_tensor("early", [EARLY, P, SEQ], F32).ap()
    tokens = lambda ap: ap.rearrange("a (t p) d -> p (a t) d", p=P)
    with Stage(nc, "trunk") as s:
        c = {n: s.sb(n, [P, P]) for n in ("ident", "ones", "upper", "lower", "strict", "block16", "iota")}
        h = s.sb("h", [P, TT, D])
        make_constants(nc, c, h, tokens(x))
        gdn_layer(nc, c, h, a_w_in[0], a_conv_w[0], a_a_log, a_dt_bias, a_norm_g, a_w_out[0],
                  ln_g[0, 0:1], ln_b[0, 0:1])
        peer_layer(nc, c, "p0", h, peer_w_q[0], peer_sub_keys[0], peer_u[0], peer_v[0], gates, early)
        normalize(nc, c, "ln01", h, ln_g[0, 1:2], ln_b[0, 1:2])
        mla_layer(nc, c, h, positions, kv_w_a, kv_norm_g, kv_w_uk, kv_w_uv, b_w_qa[0], b_q_norm_g, b_w_qb[0], b_w_out[0],
                  ln_g[1, 0:1], ln_b[1, 0:1])
        peer_layer(nc, c, "p1", h, peer_w_q[1], peer_sub_keys[1], peer_u[1], peer_v[1], gates, early)
        normalize(nc, c, "ln11", h, ln_g[1, 1:2], ln_b[1, 1:2], tokens(out))


_INS = ["x", "positions", "a_w_in", "a_conv_w", "a_a_log", "a_dt_bias", "a_norm_g", "a_w_out", "kv_w_a", "kv_norm_g",
        "kv_w_uk", "kv_w_uv", "b_w_qa", "b_q_norm_g", "b_w_qb", "b_w_out", "peer_w_q", "peer_sub_keys", "peer_u",
        "peer_v", "ln_g", "ln_b"]


def kernel(**inputs):
    import numpy as _np
    import concourse.bacc as _bacc
    from concourse import mybir as _mybir
    from concourse.bass_utils import run_bass_kernel_spmd as _run

    nc = _bacc.Bacc("TRN2", target_bir_lowering=False, num_devices=1)
    arrays, args = {}, []
    for name in _INS:
        a = _np.ascontiguousarray(inputs[name])
        arrays[f"in_{name}_dram"] = a
        args.append(nc.dram_tensor(f"in_{name}_dram", a.shape, _mybir.dt.from_np(a.dtype), kind="ExternalInput").ap())
    args.append(nc.dram_tensor("out_dram", (1, SEQ, D), _mybir.dt.float32, kind="ExternalOutput").ap())
    yoco_trunk(nc, *args)
    r = _run(nc, [arrays], core_ids=[0])
    return r.results[0]["out_dram"]
```
